# Optimizing a Trainium2 kernel written in Bass

```python
import math
import jax, jax.numpy as jnp
from jax import lax
import numpy as np

D_MODEL = 1024
BATCH = 1
SEQ = 256
DEPTH = 2

GRID_W = 64
N_MIXERS = 4
GROUP_WIDTH = D_MODEL // N_MIXERS
HEAD_DIM = 64
Q_BLOCK = 128
EPS = 1e-6

NA_HEADS = GROUP_WIDTH // HEAD_DIM
NA_WIN_ROWS = 8
NA_WIN_COLS = 16

DIFF_HEADS = GROUP_WIDTH // HEAD_DIM
DIFF_QK_DIM = HEAD_DIM // 2
DIFF_V_DIM = HEAD_DIM

GQA_HEADS = GROUP_WIDTH // HEAD_DIM
GQA_KV_HEADS = GQA_HEADS // 2
ROPE_THETA = 10000.0

MLA_HEADS = GROUP_WIDTH // HEAD_DIM
MLA_Q_LORA = GROUP_WIDTH
MLA_KV_LORA = GROUP_WIDTH // 2
MLA_NOPE_DIM = HEAD_DIM
MLA_ROPE_DIM = HEAD_DIM // 2
MLA_V_DIM = HEAD_DIM

D_FF = -(-8 * D_MODEL // (3 * 256)) * 256

IN_SIZES = (
    NA_HEADS * HEAD_DIM, NA_HEADS * HEAD_DIM, NA_HEADS * HEAD_DIM,
    DIFF_HEADS * 2 * DIFF_QK_DIM, DIFF_HEADS * 2 * DIFF_QK_DIM, DIFF_HEADS * DIFF_V_DIM,
    GQA_HEADS * HEAD_DIM, GQA_KV_HEADS * HEAD_DIM, GQA_KV_HEADS * HEAD_DIM,
    MLA_Q_LORA, MLA_KV_LORA, MLA_ROPE_DIM,
)
IN_WIDTH = sum(IN_SIZES)
MIX_WIDTH = NA_HEADS * HEAD_DIM + DIFF_HEADS * DIFF_V_DIM + GQA_HEADS * HEAD_DIM + MLA_HEADS * MLA_V_DIM


def rms_norm(x, w):
    xf = x.astype(jnp.float32)
    y = xf * lax.rsqrt(jnp.mean(xf * xf, axis=-1, keepdims=True) + EPS)
    return (y * w.astype(jnp.float32)).astype(x.dtype)

def rope(x, pos):
    d = x.shape[-1]
    inv = ROPE_THETA ** (-jnp.arange(0, d, 2, dtype=jnp.float32) / d)
    ang = pos.astype(jnp.float32)[:, None] * inv[None, :]
    ang = jnp.concatenate([ang, ang], axis=-1)
    xf = x.astype(jnp.float32)
    x1, x2 = jnp.split(xf, 2, axis=-1)
    rot = jnp.concatenate([-x2, x1], axis=-1)
    return (xf * jnp.cos(ang) + rot * jnp.sin(ang)).astype(x.dtype)

def axial_rope(x, row, col):
    half = x.shape[-1] // 2
    return jnp.concatenate([rope(x[..., :half], row), rope(x[..., half:], col)], axis=-1)

def split_heads(t, n):
    b, s, _ = t.shape
    return t.reshape(b, s, n, -1).transpose(0, 2, 1, 3)

def merge_heads(t):
    b, h, s, d = t.shape
    return t.transpose(0, 2, 1, 3).reshape(b, s, h * d)

def to_blocks(t):
    b, h, s, d = t.shape
    return t.reshape(b, h, s // Q_BLOCK, Q_BLOCK, d).transpose(2, 0, 1, 3, 4)

def from_blocks(t):
    nb, b, h, qb, d = t.shape
    return t.transpose(1, 2, 0, 3, 4).reshape(b, h, nb * qb, d)

def neighbourhood_attention(q, k, v, rel_bias):
    b, h, s, d = q.shape
    rows = s // GRID_W
    wr = min(NA_WIN_ROWS, rows)
    wc = NA_WIN_COLS
    q5 = q.reshape(b, h, rows, GRID_W, d)
    k5 = k.reshape(b, h, rows, GRID_W, d)
    v5 = v.reshape(b, h, rows, GRID_W, d)
    r = jnp.arange(rows)
    row_start = jnp.clip(r - wr // 2, 0, rows - wr)
    c = jnp.arange(GRID_W)
    col_idx = jnp.clip(c - wc // 2, 0, GRID_W - wc)[:, None] + jnp.arange(wc)[None, :]
    dc_idx = col_idx - c[:, None] + (NA_WIN_COLS - 1)
    scale = d ** -0.5

    def row_block(args):
        q_r, rs, r_i = args
        k_band = lax.dynamic_slice_in_dim(k5, rs, wr, axis=2)
        v_band = lax.dynamic_slice_in_dim(v5, rs, wr, axis=2)
        k_win = k_band[:, :, :, col_idx, :]
        v_win = v_band[:, :, :, col_idx, :]
        dr_idx = rs + jnp.arange(wr) - r_i + (NA_WIN_ROWS - 1)
        bias = rel_bias[:, dr_idx[None, :, None], dc_idx[:, None, :]]
        sc = jnp.einsum('bhcd,bhrcwd->bhcrw', q_r, k_win).astype(jnp.float32) * scale + bias.astype(jnp.float32)
        p = jax.nn.softmax(sc.reshape(b, h, GRID_W, wr * wc), axis=-1).reshape(b, h, GRID_W, wr, wc)
        return jnp.einsum('bhcrw,bhrcwd->bhcd', p.astype(v.dtype), v_win)

    out = lax.map(row_block, (q5.transpose(2, 0, 1, 3, 4), row_start, r))
    return out.transpose(1, 2, 0, 3, 4).reshape(b, h, s, d)

def diff_attention(q1, q2, k1, k2, v, lam, slopes):
    s = k1.shape[2]
    pos = jnp.arange(s)
    scale = DIFF_QK_DIM ** -0.5

    def block(args):
        qb1, qb2, qp = args
        dist = jnp.abs(qp[:, None] - pos[None, :]).astype(jnp.float32)
        alibi = -slopes[:, None, None] * dist
        s1 = jnp.einsum('bhqd,bhkd->bhqk', qb1, k1).astype(jnp.float32) * scale + alibi
        s2 = jnp.einsum('bhqd,bhkd->bhqk', qb2, k2).astype(jnp.float32) * scale + alibi
        a = jax.nn.softmax(s1, axis=-1) - lam * jax.nn.softmax(s2, axis=-1)
        return jnp.einsum('bhqk,bhkd->bhqd', a.astype(v.dtype), v)

    out = lax.map(block, (to_blocks(q1), to_blocks(q2), pos.reshape(-1, Q_BLOCK)))
    return from_blocks(out)

def gqa_attention(q, k, v):
    b, h, s, d = q.shape
    kvh = k.shape[1]
    g = h // kvh
    scale = d ** -0.5

    def block(qb):
        qg = qb.reshape(b, kvh, g, Q_BLOCK, d)
        sc = jnp.einsum('bkgqd,bksd->bkgqs', qg, k).astype(jnp.float32) * scale
        o = jnp.einsum('bkgqs,bksd->bkgqd', jax.nn.softmax(sc, axis=-1).astype(v.dtype), v)
        return o.reshape(b, h, Q_BLOCK, d)

    return from_blocks(lax.map(block, to_blocks(q)))

def mla_attention(q_nope, q_rope, k_nope, k_rope, v):
    scale = (MLA_NOPE_DIM + MLA_ROPE_DIM) ** -0.5

    def block(args):
        qn, qr = args
        sc = (jnp.einsum('bhqd,bhkd->bhqk', qn, k_nope)
              + jnp.einsum('bhqd,bkd->bhqk', qr, k_rope)).astype(jnp.float32) * scale
        return jnp.einsum('bhqk,bhkd->bhqd', jax.nn.softmax(sc, axis=-1).astype(v.dtype), v)

    return from_blocks(lax.map(block, (to_blocks(q_nope), to_blocks(q_rope))))

def first_inputs(seed: int = 0) -> dict:
    key = jax.random.key(seed)
    ks = jax.random.split(key, 21)

    def normal(k, shape, scale):
        return scale * jax.random.normal(k, shape, jnp.float32)

    def gain(k, shape):
        return 1.0 + normal(k, shape, 0.05)

    return {
        "x": normal(ks[0], (BATCH, SEQ, D_MODEL), 1.0),
        "pre_mix_norm": gain(ks[1], (DEPTH, D_MODEL)),
        "w_in": normal(ks[2], (DEPTH, D_MODEL, IN_WIDTH), D_MODEL ** -0.5),
        "na_rel_bias": normal(ks[3], (DEPTH, NA_HEADS, 2 * NA_WIN_ROWS - 1, 2 * NA_WIN_COLS - 1), 0.1),
        "diff_lambda_q1": normal(ks[4], (DEPTH, DIFF_QK_DIM), 0.1),
        "diff_lambda_k1": normal(ks[5], (DEPTH, DIFF_QK_DIM), 0.1),
        "diff_lambda_q2": normal(ks[6], (DEPTH, DIFF_QK_DIM), 0.1),
        "diff_lambda_k2": normal(ks[7], (DEPTH, DIFF_QK_DIM), 0.1),
        "diff_subln": gain(ks[8], (DEPTH, DIFF_V_DIM)),
        "gqa_q_norm": gain(ks[9], (DEPTH, HEAD_DIM)),
        "gqa_k_norm": gain(ks[10], (DEPTH, HEAD_DIM)),
        "mla_q_norm": gain(ks[11], (DEPTH, MLA_Q_LORA)),
        "mla_kv_norm": gain(ks[12], (DEPTH, MLA_KV_LORA)),
        "mla_w_uq": normal(ks[13], (DEPTH, MLA_Q_LORA, MLA_HEADS * (MLA_NOPE_DIM + MLA_ROPE_DIM)), MLA_Q_LORA ** -0.5),
        "mla_w_ukv": normal(ks[14], (DEPTH, MLA_KV_LORA, MLA_HEADS * (MLA_NOPE_DIM + MLA_V_DIM)), MLA_KV_LORA ** -0.5),
        "w_o": normal(ks[15], (DEPTH, MIX_WIDTH, D_MODEL), MIX_WIDTH ** -0.5),
        "post_mix_norm": gain(ks[16], (DEPTH, D_MODEL)),
        "pre_ffn_norm": gain(ks[17], (DEPTH, D_MODEL)),
        "ffn_w_gate_up": normal(ks[18], (DEPTH, D_MODEL, 2 * D_FF), D_MODEL ** -0.5),
        "ffn_w_down": normal(ks[19], (DEPTH, D_FF, D_MODEL), D_FF ** -0.5),
        "post_ffn_norm": gain(ks[20], (DEPTH, D_MODEL)),
    }

def first_block(x, pre_mix_norm, w_in, na_rel_bias, diff_lambda_q1, diff_lambda_k1, diff_lambda_q2,
              diff_lambda_k2, diff_subln, gqa_q_norm, gqa_k_norm, mla_q_norm, mla_kv_norm, mla_w_uq,
              mla_w_ukv, w_o, post_mix_norm, pre_ffn_norm, ffn_w_gate_up, ffn_w_down, post_ffn_norm):
    b, s, _ = x.shape
    pos = jnp.arange(s)
    grid_row = pos // GRID_W
    grid_col = pos % GRID_W
    offsets = [int(o) for o in np.cumsum(IN_SIZES)[:-1]]
    alibi_slopes = jnp.asarray([2.0 ** (-8.0 * (i + 1) / DIFF_HEADS) for i in range(DIFF_HEADS)], dtype=jnp.float32)

    for l in range(DEPTH):
        h = rms_norm(x, pre_mix_norm[l])
        proj = jnp.einsum('bsd,de->bse', h, w_in[l])
        (na_q, na_k, na_v, df_q, df_k, df_v, gq_q, gq_k, gq_v,
         ml_cq, ml_ckv, ml_kr) = jnp.split(proj, offsets, axis=-1)

        a_out = neighbourhood_attention(split_heads(na_q, NA_HEADS), split_heads(na_k, NA_HEADS),
                                        split_heads(na_v, NA_HEADS), na_rel_bias[l])

        lambda_init = 0.8 - 0.6 * math.exp(-0.3 * l)
        dq = df_q.reshape(b, s, DIFF_HEADS, 2, DIFF_QK_DIM).transpose(3, 0, 2, 1, 4)
        dk = df_k.reshape(b, s, DIFF_HEADS, 2, DIFF_QK_DIM).transpose(3, 0, 2, 1, 4)
        lam = (jnp.exp(jnp.sum(diff_lambda_q1[l].astype(jnp.float32) * diff_lambda_k1[l].astype(jnp.float32)))
               - jnp.exp(jnp.sum(diff_lambda_q2[l].astype(jnp.float32) * diff_lambda_k2[l].astype(jnp.float32)))
               + lambda_init)
        b_out = diff_attention(dq[0], dq[1], dk[0], dk[1], split_heads(df_v, DIFF_HEADS), lam, alibi_slopes)
        b_out = rms_norm(b_out, diff_subln[l]) * (1.0 - lambda_init)

        cq = axial_rope(rms_norm(split_heads(gq_q, GQA_HEADS), gqa_q_norm[l]), grid_row, grid_col)
        ck = axial_rope(rms_norm(split_heads(gq_k, GQA_KV_HEADS), gqa_k_norm[l]), grid_row, grid_col)
        c_out = gqa_attention(cq, ck, split_heads(gq_v, GQA_KV_HEADS))

        c_q = rms_norm(ml_cq, mla_q_norm[l])
        q_full = split_heads(jnp.einsum('bsr,re->bse', c_q, mla_w_uq[l]), MLA_HEADS)
        q_nope, q_rope = q_full[..., :MLA_NOPE_DIM], rope(q_full[..., MLA_NOPE_DIM:], pos)
        c_kv = rms_norm(ml_ckv, mla_kv_norm[l])
        kv = split_heads(jnp.einsum('bsr,re->bse', c_kv, mla_w_ukv[l]), MLA_HEADS)
        k_nope, mla_v = kv[..., :MLA_NOPE_DIM], kv[..., MLA_NOPE_DIM:]
        k_rope = rope(ml_kr, pos)
        d_out = mla_attention(q_nope, q_rope, k_nope, k_rope, mla_v)

        mix = jnp.concatenate([merge_heads(a_out), merge_heads(b_out),
                               merge_heads(c_out), merge_heads(d_out)], axis=-1)
        mix = jnp.einsum('bse,ed->bsd', mix, w_o[l])
        x = x + rms_norm(mix, post_mix_norm[l])

        h = rms_norm(x, pre_ffn_norm[l])
        gate, up = jnp.split(jnp.einsum('bsd,df->bsf', h, ffn_w_gate_up[l]), 2, axis=-1)
        f = jnp.einsum('bsf,fd->bsd', jax.nn.silu(gate) * up, ffn_w_down[l])
        x = x + rms_norm(f, post_ffn_norm[l])
    return x


DEPTH_2 = 4

N_HEADS = 8
HEAD_DIM_2 = D_MODEL // N_HEADS
D_FF_2 = 4 * D_MODEL
NORM_EPS = 1e-6
NEG_INF = -1e30

NSA_KV_GROUPS = 2
NSA_HEADS_PER_GROUP = N_HEADS // NSA_KV_GROUPS
NSA_CMP_BLOCK = 32
NSA_CMP_STRIDE = 16
NSA_SEL_BLOCK = 64
NSA_SEL_TOPK = 16
NSA_WINDOW = 512
NSA_QBLOCK = 64
NSA_FORCE_BONUS = 1000.0
NSA_IN_DIM = N_HEADS * HEAD_DIM_2 + 6 * NSA_KV_GROUPS * HEAD_DIM_2 + 3 * N_HEADS

SB_QBLOCK = 128

CONV_WIDTH = 31

MOBA_BLOCK = 256
MOBA_TOPK = 3
MOBA_QBLOCK = 32

N_NSA = (DEPTH_2 + 3) // 4
N_SB = (DEPTH_2 + 2) // 4
N_CONV = (DEPTH_2 + 1) // 4
N_MOBA = DEPTH_2 // 4


def _rms_norm(x, g):
    xf = x.astype(jnp.float32)
    y = xf * lax.rsqrt(jnp.mean(xf * xf, axis=-1, keepdims=True) + NORM_EPS)
    return (y * g.astype(jnp.float32)).astype(x.dtype)

def _rope_tables(seq):
    half = HEAD_DIM_2 // 2
    inv_freq = ROPE_THETA ** (-jnp.arange(half, dtype=jnp.float32) / half)
    ang = jnp.arange(seq, dtype=jnp.float32)[:, None] * inv_freq[None, :]
    return jnp.cos(ang), jnp.sin(ang)

def _apply_rope(x, cos, sin):
    xf = x.astype(jnp.float32)
    x1, x2 = jnp.split(xf, 2, axis=-1)
    c = cos[None, :, None, :]
    s = sin[None, :, None, :]
    return jnp.concatenate([x1 * c - x2 * s, x1 * s + x2 * c], axis=-1).astype(x.dtype)

def _masked_softmax(logits, mask):
    z = jnp.where(mask, logits.astype(jnp.float32), NEG_INF)
    return jnp.where(mask, jax.nn.softmax(z, axis=-1), 0.0)

def _nsa_mixer(h, w_in, q_gain, k_gain, cmp_pos, w_cmp, w_out, cos, sin):
    B, S, _ = h.shape
    H, G, HG, DH = N_HEADS, NSA_KV_GROUPS, NSA_HEADS_PER_GROUP, HEAD_DIM_2
    L, STR, SB, W, QB = NSA_CMP_BLOCK, NSA_CMP_STRIDE, NSA_SEL_BLOCK, NSA_WINDOW, NSA_QBLOCK
    sizes = [H * DH] + [G * DH] * 6
    q, kc, vc, ks, vs, kw, vw, gates = jnp.split(h @ w_in, np.cumsum(sizes).tolist(), axis=-1)
    q = _apply_rope(_rms_norm(q.reshape(B, S, H, DH), q_gain), cos, sin)
    kc, ks, kw = [_apply_rope(_rms_norm(k.reshape(B, S, G, DH), k_gain[i]), cos, sin)
                  for i, k in enumerate((kc, ks, kw))]
    vc, vs, vw = [v.reshape(B, S, G, DH) for v in (vc, vs, vw)]
    gates = jax.nn.sigmoid(gates.astype(jnp.float32)).reshape(B, S, 3, G, HG)
    n_cmp = (S - L) // STR + 1
    cmp_start = jnp.arange(n_cmp) * STR
    cidx = cmp_start[:, None] + jnp.arange(L)[None, :]
    kc = jnp.einsum('bnlgd,lde->bnge', kc[:, cidx] + cmp_pos[0][None, None, :, None, :], w_cmp[0])
    vc = jnp.einsum('bnlgd,lde->bnge', vc[:, cidx] + cmp_pos[1][None, None, :, None, :], w_cmp[1])
    cmp_end = cmp_start + L - 1
    n_sel = S // SB
    sel_start = jnp.arange(n_sel) * SB
    overlap = ((cmp_start[:, None] < sel_start[None, :] + SB)
               & (cmp_start[:, None] + L > sel_start[None, :])).astype(jnp.float32)
    topk = min(NSA_SEL_TOPK, n_sel)
    ks_blk = ks.reshape(B, n_sel, SB, G, DH).transpose(0, 3, 1, 2, 4)
    vs_blk = vs.reshape(B, n_sel, SB, G, DH).transpose(0, 3, 1, 2, 4)
    kw_pad = jnp.pad(kw, ((0, 0), (W, 0), (0, 0), (0, 0)))
    vw_pad = jnp.pad(vw, ((0, 0), (W, 0), (0, 0), (0, 0)))
    scale = DH ** -0.5
    b_ix = jnp.arange(B)[:, None, None, None]
    g_ix = jnp.arange(G)[None, None, :, None]
    blk = jnp.arange(n_sel)
    in_blk = jnp.arange(SB)
    win_off = jnp.arange(W + QB) - W

    def chunk(c0):
        t = c0 + jnp.arange(QB)
        qc = lax.dynamic_slice_in_dim(q, c0, QB, axis=1).reshape(B, QB, G, HG, DH)
        p_c = _masked_softmax(jnp.einsum('bqghd,bngd->bqghn', qc, kc) * scale,
                              (cmp_end[None, :] <= t[:, None])[None, :, None, None, :])
        o_c = jnp.einsum('bqghn,bngd->bqghd', p_c.astype(vc.dtype), vc)
        imp = jnp.einsum('bqgn,nj->bqgj', p_c.sum(axis=3), overlap)
        cur = c0 // SB
        forced = (blk == 0) | (blk == cur) | (blk == cur - 1)
        imp = jnp.where(blk <= cur, imp + NSA_FORCE_BONUS * forced, -1.0)
        _, idx = lax.top_k(imp, topk)
        k_sel = ks_blk[b_ix, g_ix, idx].reshape(B, QB, G, topk * SB, DH)
        v_sel = vs_blk[b_ix, g_ix, idx].reshape(B, QB, G, topk * SB, DH)
        pos = (idx[..., None] * SB + in_blk).reshape(B, QB, G, 1, topk * SB)
        p_s = _masked_softmax(jnp.einsum('bqghd,bqgmd->bqghm', qc, k_sel) * scale,
                              pos <= t[None, :, None, None, None])
        o_s = jnp.einsum('bqghm,bqgmd->bqghd', p_s.astype(v_sel.dtype), v_sel)
        pos_w = c0 + win_off
        diff = t[:, None] - pos_w[None, :]
        m_w = ((pos_w[None, :] >= 0) & (diff >= 0) & (diff < W))[None, :, None, None, :]
        kwc = lax.dynamic_slice_in_dim(kw_pad, c0, W + QB, axis=1)
        vwc = lax.dynamic_slice_in_dim(vw_pad, c0, W + QB, axis=1)
        p_w = _masked_softmax(jnp.einsum('bqghd,bkgd->bqghk', qc, kwc) * scale, m_w)
        o_w = jnp.einsum('bqghk,bkgd->bqghd', p_w.astype(vwc.dtype), vwc)
        g = lax.dynamic_slice_in_dim(gates, c0, QB, axis=1)[..., None]
        o = g[:, :, 0] * o_c + g[:, :, 1] * o_s + g[:, :, 2] * o_w
        return o.reshape(B, QB, H * DH).astype(h.dtype)

    out = lax.map(chunk, jnp.arange(S // QB) * QB)
    out = jnp.transpose(out, (1, 0, 2, 3)).reshape(B, S, H * DH)
    return out @ w_out

def _stick_breaking_mixer(h, w_in, w_out):
    B, S, _ = h.shape
    H, DH, QB = N_HEADS, HEAD_DIM_2, SB_QBLOCK
    q, k, v = [a.reshape(B, S, H, DH) for a in jnp.split(h @ w_in, 3, axis=-1)]
    scale = DH ** -0.5
    s_idx = jnp.arange(S)

    def chunk(c0):
        t = c0 + jnp.arange(QB)
        qc = lax.dynamic_slice_in_dim(q, c0, QB, axis=1)
        z = jnp.einsum('bqhd,bshd->bhqs', qc, k).astype(jnp.float32) * scale
        mask = (s_idx[None, :] < t[:, None])[None, None]
        log_beta = jax.nn.log_sigmoid(z)
        log_one_minus = jnp.where(mask, jax.nn.log_sigmoid(-z), 0.0)
        between = lax.cumsum(log_one_minus, axis=3, reverse=True) - log_one_minus
        a = jnp.where(mask, jnp.exp(log_beta + between), 0.0)
        o = jnp.einsum('bhqs,bshd->bqhd', a.astype(v.dtype), v)
        return o.reshape(B, QB, H * DH)

    out = lax.map(chunk, jnp.arange(S // QB) * QB)
    out = jnp.transpose(out, (1, 0, 2, 3)).reshape(B, S, H * DH)
    return out @ w_out

def _conformer_conv_mixer(h, w_in, dw_w, dw_b, ln_g, ln_b, w_out):
    a, b = jnp.split(h @ w_in, 2, axis=-1)
    u = a * jax.nn.sigmoid(b)
    u = lax.conv_general_dilated(u, dw_w[:, None, :], window_strides=(1,),
                                 padding=[(CONV_WIDTH - 1, 0)],
                                 dimension_numbers=('NWC', 'WIO', 'NWC'),
                                 feature_group_count=D_MODEL) + dw_b
    uf = u.astype(jnp.float32)
    mu = jnp.mean(uf, axis=-1, keepdims=True)
    var = jnp.mean(jnp.square(uf - mu), axis=-1, keepdims=True)
    un = (uf - mu) * lax.rsqrt(var + NORM_EPS) * ln_g.astype(jnp.float32) + ln_b.astype(jnp.float32)
    return jax.nn.silu(un).astype(h.dtype) @ w_out

def _moba_mixer(h, w_in, q_gain, k_gain, w_out, cos, sin):
    B, S, _ = h.shape
    H, DH, BS, QB = N_HEADS, HEAD_DIM_2, MOBA_BLOCK, MOBA_QBLOCK
    q, k, v = [a.reshape(B, S, H, DH) for a in jnp.split(h @ w_in, 3, axis=-1)]
    q = _apply_rope(_rms_norm(q, q_gain), cos, sin)
    k = _apply_rope(_rms_norm(k, k_gain), cos, sin)
    n_blk = -(-S // BS)
    pad = n_blk * BS - S
    kp = jnp.pad(k, ((0, 0), (0, pad), (0, 0), (0, 0)))
    vp = jnp.pad(v, ((0, 0), (0, pad), (0, 0), (0, 0)))
    k_blocks = kp.reshape(B, n_blk, BS, H, DH)
    k_mean = jnp.mean(k_blocks.astype(jnp.float32), axis=2)
    kb_t = k_blocks.transpose(0, 3, 1, 2, 4)
    vb_t = vp.reshape(B, n_blk, BS, H, DH).transpose(0, 3, 1, 2, 4)
    topk = min(MOBA_TOPK, n_blk)
    scale = DH ** -0.5
    b_ix = jnp.arange(B)[:, None, None, None]
    h_ix = jnp.arange(H)[None, None, :, None]
    blk = jnp.arange(n_blk)

    def chunk(c0):
        t = c0 + jnp.arange(QB)
        qc = lax.dynamic_slice_in_dim(q, c0, QB, axis=1)
        cur = c0 // BS
        gate = jnp.einsum('bqhd,bnhd->bqhn', qc.astype(jnp.float32), k_mean)
        gate = jnp.where(blk < cur, gate, NEG_INF)
        _, idx = lax.top_k(gate, topk)
        valid = idx < cur
        k_sel = kb_t[b_ix, h_ix, idx].reshape(B, QB, H, topk * BS, DH)
        v_sel = vb_t[b_ix, h_ix, idx].reshape(B, QB, H, topk * BS, DH)
        s_past = jnp.einsum('bqhd,bqhmd->bqhm', qc, k_sel) * scale
        m_past = jnp.broadcast_to(valid[..., None], (B, QB, H, topk, BS)).reshape(B, QB, H, topk * BS)
        own0 = cur * BS
        k_own = lax.dynamic_slice_in_dim(kp, own0, BS, axis=1)
        v_own = lax.dynamic_slice_in_dim(vp, own0, BS, axis=1)
        s_own = jnp.einsum('bqhd,bkhd->bqhk', qc, k_own) * scale
        m_own = jnp.broadcast_to(((own0 + jnp.arange(BS))[None, :] <= t[:, None])[None, :, None, :],
                                 (B, QB, H, BS))
        p = _masked_softmax(jnp.concatenate([s_past, s_own], axis=-1),
                            jnp.concatenate([m_past, m_own], axis=-1))
        p = p.astype(v.dtype)
        o = (jnp.einsum('bqhm,bqhmd->bqhd', p[..., :topk * BS], v_sel)
             + jnp.einsum('bqhk,bkhd->bqhd', p[..., topk * BS:], v_own))
        return o.reshape(B, QB, H * DH)

    out = lax.map(chunk, jnp.arange(S // QB) * QB)
    out = jnp.transpose(out, (1, 0, 2, 3)).reshape(B, S, H * DH)
    return out @ w_out

def second_inputs(seed: int = 0) -> dict:
    key = jax.random.key(seed)
    keys = iter(jax.random.split(key, 32))

    def w(shape, fan_in):
        return jax.random.normal(next(keys), shape, jnp.float32) * (fan_in ** -0.5)

    def gain(shape):
        return 1.0 + 0.05 * jax.random.normal(next(keys), shape, jnp.float32)

    def small(shape, s):
        return s * jax.random.normal(next(keys), shape, jnp.float32)

    D, DH, L = D_MODEL, HEAD_DIM_2, NSA_CMP_BLOCK
    return {
        'x': jax.random.normal(next(keys), (BATCH, SEQ, D), jnp.float32),
        'attn_norm': gain((DEPTH_2, D)),
        'mlp_norm': gain((DEPTH_2, D)),
        'mlp_w_up': w((DEPTH_2, D, D_FF_2), D),
        'mlp_w_down': w((DEPTH_2, D_FF_2, D), D_FF_2),
        'nsa_w_in': w((N_NSA, D, NSA_IN_DIM), D),
        'nsa_q_norm': gain((N_NSA, DH)),
        'nsa_k_norm': gain((N_NSA, 3, DH)),
        'nsa_cmp_pos': small((N_NSA, 2, L, DH), 0.1),
        'nsa_w_cmp': w((N_NSA, 2, L, DH, DH), L * DH),
        'nsa_w_out': w((N_NSA, N_HEADS * DH, D), N_HEADS * DH),
        'sb_w_in': w((N_SB, D, 3 * N_HEADS * DH), D),
        'sb_w_out': w((N_SB, N_HEADS * DH, D), N_HEADS * DH),
        'conv_w_in': w((N_CONV, D, 2 * D), D),
        'conv_dw_w': w((N_CONV, CONV_WIDTH, D), CONV_WIDTH),
        'conv_dw_b': small((N_CONV, D), 0.02),
        'conv_ln_g': gain((N_CONV, D)),
        'conv_ln_b': small((N_CONV, D), 0.02),
        'conv_w_out': w((N_CONV, D, D), D),
        'moba_w_in': w((N_MOBA, D, 3 * N_HEADS * DH), D),
        'moba_q_norm': gain((N_MOBA, DH)),
        'moba_k_norm': gain((N_MOBA, DH)),
        'moba_w_out': w((N_MOBA, N_HEADS * DH, D), N_HEADS * DH),
    }

def second_block(x, attn_norm, mlp_norm, mlp_w_up, mlp_w_down,
              nsa_w_in, nsa_q_norm, nsa_k_norm, nsa_cmp_pos, nsa_w_cmp, nsa_w_out,
              sb_w_in, sb_w_out,
              conv_w_in, conv_dw_w, conv_dw_b, conv_ln_g, conv_ln_b, conv_w_out,
              moba_w_in, moba_q_norm, moba_k_norm, moba_w_out):
    cos, sin = _rope_tables(x.shape[1])
    for i in range(DEPTH_2):
        m, j = i % N_MIXERS, i // N_MIXERS
        h = _rms_norm(x, attn_norm[i])
        if m == 0:
            y = _nsa_mixer(h, nsa_w_in[j], nsa_q_norm[j], nsa_k_norm[j], nsa_cmp_pos[j],
                           nsa_w_cmp[j], nsa_w_out[j], cos, sin)
        elif m == 1:
            y = _stick_breaking_mixer(h, sb_w_in[j], sb_w_out[j])
        elif m == 2:
            y = _conformer_conv_mixer(h, conv_w_in[j], conv_dw_w[j], conv_dw_b[j],
                                      conv_ln_g[j], conv_ln_b[j], conv_w_out[j])
        else:
            y = _moba_mixer(h, moba_w_in[j], moba_q_norm[j], moba_k_norm[j], moba_w_out[j], cos, sin)
        x = x + y.astype(x.dtype)
        hm = _rms_norm(x, mlp_norm[i])
        x = x + jnp.square(jax.nn.relu(hm @ mlp_w_up[i])) @ mlp_w_down[i]
    return x


def setup_inputs(seed=0):
    out = dict(first_inputs(seed))
    for name, value in second_inputs(seed + 1).items():
        if name != "x":
            out[name + "_2"] = value
    return out


def reference(
    x, pre_mix_norm, w_in, na_rel_bias, diff_lambda_q1, diff_lambda_k1, diff_lambda_q2,
    diff_lambda_k2, diff_subln, gqa_q_norm, gqa_k_norm, mla_q_norm, mla_kv_norm, mla_w_uq,
    mla_w_ukv, w_o, post_mix_norm, pre_ffn_norm, ffn_w_gate_up, ffn_w_down, post_ffn_norm,
    attn_norm_2, mlp_norm_2, mlp_w_up_2, mlp_w_down_2, nsa_w_in_2, nsa_q_norm_2, nsa_k_norm_2,
    nsa_cmp_pos_2, nsa_w_cmp_2, nsa_w_out_2, sb_w_in_2, sb_w_out_2, conv_w_in_2, conv_dw_w_2,
    conv_dw_b_2, conv_ln_g_2, conv_ln_b_2, conv_w_out_2, moba_w_in_2, moba_q_norm_2,
    moba_k_norm_2, moba_w_out_2,
):
    x = first_block(
        x, pre_mix_norm, w_in, na_rel_bias, diff_lambda_q1, diff_lambda_k1, diff_lambda_q2,
        diff_lambda_k2, diff_subln, gqa_q_norm, gqa_k_norm, mla_q_norm, mla_kv_norm, mla_w_uq,
        mla_w_ukv, w_o, post_mix_norm, pre_ffn_norm, ffn_w_gate_up, ffn_w_down, post_ffn_norm,
    )
    return second_block(
        x, attn_norm_2, mlp_norm_2, mlp_w_up_2, mlp_w_down_2, nsa_w_in_2, nsa_q_norm_2,
        nsa_k_norm_2, nsa_cmp_pos_2, nsa_w_cmp_2, nsa_w_out_2, sb_w_in_2, sb_w_out_2,
        conv_w_in_2, conv_dw_w_2, conv_dw_b_2, conv_ln_g_2, conv_ln_b_2, conv_w_out_2,
        moba_w_in_2, moba_q_norm_2, moba_k_norm_2, moba_w_out_2,
    )


_drawn_inputs = setup_inputs


def setup_inputs(seed=0):
    import zlib

    import numpy as np

    out = dict(_drawn_inputs(seed))
    spreads = {}
    factors = {'diff_lambda_q2': 3.355,
     'gqa_q_norm': 6.953,
     'gqa_k_norm': 6.639,
     'mla_q_norm': 5.989,
     'mla_kv_norm': 3.4,
     'nsa_q_norm_2': 8.0,
     'nsa_k_norm_2': 8.0,
     'conv_dw_b_2': 6.227,
     'conv_ln_g_2': 4.341,
     'conv_ln_b_2': 8.0,
     'moba_q_norm_2': 8.0,
     'moba_k_norm_2': 8.0}
    for name, (base, spread) in spreads.items():
        noise = np.random.default_rng([zlib.crc32(name.encode()), seed]).standard_normal(out[name].shape)
        drawn = base * np.exp(spread * noise) if base else spread * noise
        out[name] = __import__('jax').numpy.asarray(drawn.astype(out[name].dtype))
    for name, factor in factors.items():
        out[name] = (out[name] * factor).astype(out[name].dtype)
    return out
```

```python
import math
from contextlib import ExitStack

import numpy as np

import concourse.bass as bass
from concourse import mybir

F32 = mybir.dt.float32
F32R = mybir.dt.float32r
I32 = mybir.dt.int32
ALU = mybir.AluOpType
ACT = mybir.ActivationFunctionType
AX_X = mybir.AxisListType.X

P = 128
S, D = 256, 1024
TT = S // P
KT = D // P
EPS = 1e-6
NEG = -1e30
NEWTON_STEPS = 3
W = 512
PK = 4
SLOTS = 4

GRID = 64
NA_H = DF_H = GQ_H = ML_H = 4
HD = 64
FF_A = 2816
CH_A = 256
A_COLS = dict(na_q=0, na_k=256, na_v=512, df_q=768, df_k=1024, df_v=1280, gq_q=1536, gq_k=1792, gq_v=1920,
              cq=2048, ckv=2304, kr=2432)
A_IN = 2464
H2, HD2 = 8, 128
FF_B = 4096
CH_B = 512
NSA_IN = 2584
CMP_L, CMP_STRIDE, N_CMP, GROUPS = 32, 16, 15, 2
TAPS = 31

LAYERS = [("A", 0), ("A", 1), ("nsa", 0), ("sb", 1), ("conv", 2), ("moba", 3)]


def rope_tables(pos, width):
    half = width // 2
    inv = np.float32(10000.0) ** (-np.arange(half, dtype=np.float32) / np.float32(half))
    ang = pos.astype(np.float32)[:, None] * inv[None, :].astype(np.float32)
    c, s = np.cos(ang), np.sin(ang)
    return np.concatenate([c, c], 1).astype(np.float32), np.concatenate([-s, s], 1).astype(np.float32)


def constant_tables():
    def tiles(a):
        return a.reshape(TT, P, -1).transpose(1, 0, 2).reshape(P, -1)

    t = np.arange(S)
    row, col = t // GRID, t % GRID
    both = {"ident": np.eye(P)}
    c1, s1 = rope_tables(row, HD // 2)
    c2, s2 = rope_tables(col, HD // 2)
    cm, sm = rope_tables(t, HD // 2)
    start = np.clip(col - 8, 0, GRID - 16)
    seen = (col[None, :] >= start[:, None]) & (col[None, :] < start[:, None] + 16)
    first = {
        "flip": np.kron(np.eye(2), np.eye(GRID)[::-1]),
        "na_mask": np.where(seen, 0.0, NEG)[:P],
        "dist": tiles(np.abs(t[:, None] - t[None, :])),
        "gq_cos": tiles(np.concatenate([c1, c2], 1)), "gq_sin": tiles(np.concatenate([s1, s2], 1)),
        "ml_cos": tiles(cm), "ml_sin": tiles(sm),
    }
    cb, sb = rope_tables(t, HD2)
    end = np.arange(N_CMP) * CMP_STRIDE + CMP_L - 1
    second = {
        "causal": tiles(np.where(t[None, :] <= t[:, None], 0.0, NEG)),
        "before01": tiles((t[:, None] < t[None, :]) * 1.0),
        "before": tiles(np.where(t[:, None] < t[None, :], 0.0, NEG)),
        "later": (np.arange(P)[:, None] >= np.arange(P)[None, :]) * 1.0,
        "ones": np.ones((P, P)),
        "cos": tiles(cb), "sin": tiles(sb),
        "cmp_mask": tiles(np.where(end[None, :] <= t[:, None], 0.0, NEG)),
        "cmp_any": tiles((t >= end[0])[:, None] * 1.0),
    }
    return both, first, second


def packed(tables):
    at, where = 0, {}
    for name, a in tables.items():
        where[name] = (at, at + a.shape[1])
        at += a.shape[1]
    return np.ascontiguousarray(np.concatenate(list(tables.values()), 1).astype(np.float32)), where


class Piece:

    def __init__(self, index, slot, parts):
        self.index, self.slot, self.parts = index, slot, parts
        self.floats = sum(kt * n for _, kt, n, _ in parts)
        self.before = -1
        self.landed = 0


class Plan:
    def __init__(self):
        self.pieces = []
        self.holder = {}
        self.slot_count = {}
        self.ring_start = 0

    def align(self):
        self.ring_start = len(self.pieces)

    def add(self, parts, ring=SLOTS):
        p = Piece(len(self.pieces), (len(self.pieces) - self.ring_start) % ring, parts)
        p.before = self.holder.get(p.slot, -1)
        self.slot_count[p.slot] = self.slot_count.get(p.slot, 0) + 16 * len(parts)
        p.landed = self.slot_count[p.slot]
        self.holder[p.slot] = p.index
        self.pieces.append(p)
        return p.index


class Phase:

    def __init__(self, kind, counts=None, chunks=None, out=None, gain=None, layer=None, post=None,
                 bias_load=None, bias=None, row=None, l=None, uq=None, ukv=None, cmp=None, variant=None,
                 first=None, n=None, per=None, ups=None, downs=None, kt=None, early=None):
        self.kind, self.counts = kind, counts or {}
        self.chunks, self.out, self.gain, self.layer, self.post, self.bias_load, self.bias = chunks, out, gain, layer, post, bias_load, bias
        self.early, self.order = early, None
        self.row, self.l, self.uq, self.ukv, self.cmp = row, l, uq, ukv, cmp
        self.variant, self.first, self.n, self.per, self.ups, self.downs, self.kt = variant, first, n, per, ups, downs, kt


def add_gemm(plan, w, k_rows, width, out):
    chunks = []
    kt_all = k_rows // P
    for n0 in range(0, width, W):
        n = min(W, width - n0)
        pieces = []
        for k0 in range(0, kt_all, PK):
            kt = min(PK, kt_all - k0)
            pieces.append((plan.add([(0, kt, n, ("rows", w, k0, n0))]), k0, kt))
        chunks.append((n0, n, pieces))
    ph = Phase("gemm", chunks=chunks, out=out)
    if out == "proj":
        ph.counts = {"evac_a": len(chunks), "evac_d": len(chunks)}
    elif out == "y":
        ph.counts = {"tile_done": len(chunks), "y_sq": TT * len(chunks), "x_written": 2 * TT}
    else:
        ph.counts = {"x_written": TT * len(chunks)}
    return ph


def make_plan(A):
    plan, phases = Plan(), []

    def norm(gain_col, layer, early, post=None, bias_load=None):
        phases.append(Phase("norm", gain=gain_col, layer=layer, early=early, post=post, bias_load=bias_load,
                            counts={"ss_ready": TT, "rstd_ready": 1, "hT_tr": KT // 2, "hT_hi": KT, "hT_lo": KT}))

    def units(n, n_t, qk_jobs):
        return {"s_ready": n, "s_max": n, "p_exp": 2 * n, "p_norm": 2 * n_t, "pt_ready": n_t + qk_jobs,
                "pt_evac": n_t + qk_jobs, "o_done": n_t}

    def mix_counts(base):
        c = dict(base)
        c.update({"hT_hi": KT, "hT_lo": KT})
        return c

    for index, (kind, l) in enumerate(LAYERS):
        if kind == "A":
            norm(8 * l, index, 3, ("post_mix_norm", l), 0 if l == 0 else None)
            g1 = add_gemm(plan, A["w_in"][l], D, A_IN, "proj")
            g1.bias = l
            g1.counts.update({"na_flip": 1, "na_ready": NA_H})
            phases.append(g1)
            uq = plan.add([(0, 2, 384, ("rows", A["mla_w_uq"][l], 0, 0))])
            ukv = plan.add([(0, 1, 512, ("rows", A["mla_w_ukv"][l], 0, 0))])
            c = mix_counts(units(20, 16, 10))
            c.update({"prep": 4, "aux_tr": 2, "aux_hi": 3, "aux_lo": 3, "evac_a": 2,
                      "evac_d": 2, "lam_ready": 1, "lam_exp": 1, "hT_tr": 1, "kcat_a": 2, "od_ready": 1})
            phases.append(Phase("mixA", l=l, uq=uq, ukv=ukv, counts=c))
            g2 = add_gemm(plan, A["w_o"][l], D, D, "y")
            g2.row = 2 * l
            g2.order = (0, 1, 4, 5, 6, 7, 2, 3)
            phases.append(g2)
            norm(16 + 8 * l, None, 3, ("post_ffn_norm", l), 1 if l == 0 else None)
            plan.align()
            first = len(plan.pieces)
            n = FF_A // CH_A
            gu, down = A["ffn_w_gate_up"][l], A["ffn_w_down"][l]

            def up(c):
                for k0 in (0, PK):
                    plan.add([(0, PK, CH_A, ("rows", gu, k0, c * CH_A)),
                              (PK * CH_A, PK, CH_A, ("rows", gu, k0, FF_A + c * CH_A))], ring=3)

            up(0)
            for c in range(1, n):
                up(c)
                plan.add([(0, 2, D, ("rows", down, 2 * (c - 1), 0))], ring=3)
            plan.add([(0, 2, D, ("rows", down, 2 * (n - 1), 0))], ring=3)
            plan.align()
            phases.append(Phase("ffn", variant="A", first=first, n=n, per=3, ups=2, downs=1, kt=2, row=2 * l + 1,
                                counts={"r_ready": 2 * n, "r2_ready": 2 * n, "act_tr": n, "act_hi": n, "act_lo": n,
                                        "tile_done": 1, "y_sq": 2 * TT, "x_written": 2 * TT}))
        else:
            width = {"nsa": NSA_IN, "sb": 3 * D, "conv": 2 * D, "moba": 3 * D}[kind]
            norm(32 + 8 * l, index, 3 if LAYERS[index - 1][0] == "A" else 2)
            phases.append(add_gemm(plan, A[kind + "_w_in_2"][0], D, width, "proj"))
            if kind == "nsa":
                cmp_pieces = [[plan.add([(0, 16, P, ("taps", A["nsa_w_cmp_2"][0, j], 16 * half))])
                               for half in range(2)] for j in range(2)]
                c = mix_counts(units(16, 16, 8 + 4 + 1))
                c.update({"prep": 1, "aux_hi": 2, "aux_lo": 2, "cmp_evac": 2,
                          "x_tap": 2, "gate_ready": 1, "c_ready": 1, "c_sub": 1, "c_exp": 1,
                          "c_prob": 1})
                phases.append(Phase("nsa", cmp=cmp_pieces, counts=c))
            elif kind == "sb":
                c = mix_counts({"s_ready": H2, "sb_log": H2, "sb_sp": H2, "pt_ready": H2 + 8, "sb_diff": H2,
                                "pt_evac": H2 + 8, "o_done": H2})
                phases.append(Phase("sb", counts=c))
            elif kind == "conv":
                c = mix_counts({"gate_ready": TT, "prep": TT, "pt_ready": 4, "pt_evac": 4, "conv_done": 1,
                                "mean_ready": 1, "centred": 1, "sq_ready": 1, "var_ready": 1,
                                "normed": 1, "silu_ready": KT})
                phases.append(Phase("conv", counts=c))
            else:
                c = mix_counts(units(8, 8, 8))
                c.update({"prep": 1})
                phases.append(Phase("moba", counts=c))
            phases.append(add_gemm(plan, A[kind + "_w_out_2"][0], D, D, "x"))
            norm(64 + 8 * l, None, 2)
            plan.align()
            first = len(plan.pieces)
            n = FF_B // CH_B
            w_up, w_down = A["mlp_w_up_2"][l], A["mlp_w_down_2"][l]

            def up_b(c):
                for k0 in (0, PK):
                    plan.add([(0, PK, W, ("rows", w_up, k0, c * CH_B))])

            def down_b(c):
                for n0 in (0, W):
                    plan.add([(0, PK, W, ("rows", w_down, PK * c, n0))])

            up_b(0)
            for c in range(1, n):
                up_b(c)
                down_b(c - 1)
            down_b(n - 1)
            phases.append(Phase("ffn", variant="B", first=first, n=n, per=4, ups=2, downs=2, kt=PK,
                                counts={"r_ready": 2 * n, "r2_ready": 2 * n, "act_tr": 2 * n, "act_hi": 2 * n,
                                        "act_lo": 2 * n, "x_written": 2 * TT}))
    return plan, phases


class Tally:

    def __init__(self):
        self.n = {}

    def __getitem__(self, name):
        return self.n.get(name, 0)

    def advance(self, phase):
        for name, k in phase.counts.items():
            self.n[name] = self.n.get(name, 0) + k


def along(i, steps, value):
    seen = [value(c) for c in steps]
    if i is None:
        return seen[0]
    rise = seen[1] - seen[0] if len(seen) > 1 else 0
    assert all(b - a == rise for a, b in zip(seen, seen[1:])), seen
    return seen[0] if rise == 0 else i * rise + seen[0]


def ffn_schedule(ph, engine):
    yield None, [0]
    yield None, [1]
    with engine.Fori(0, ph.n - 3) as i:
        yield i, list(range(2, ph.n - 1))
    yield None, [ph.n - 1]


SEMS = ["x_landed", "const_landed", "second_landed", "vec_landed", "row_landed", "na_landed", "post_landed",
        "out_stored", "hi_ready", "lo_ready", "piece_used", "x_written", "ss_ready", "rstd_ready", "tile_done", "y_sq", "hT_tr", "hT_hi",
        "hT_lo", "evac_a", "evac_d", "s_ready", "s_max", "p_exp", "p_norm", "pt_ready", "pt_evac", "o_done",
        "prep", "aux_tr", "aux_hi", "aux_lo", "na_ready", "na_flip", "lam_ready", "lam_exp", "kcat_a", "r_ready",
        "r2_ready", "act_tr", "act_hi", "act_lo", "od_ready", "cmp_evac", "x_tap", "gate_ready", "c_ready", "c_sub",
        "c_exp", "c_prob", "sb_log", "sb_sp", "sb_diff", "conv_done", "mean_ready", "centred", "sq_ready",
        "var_ready", "normed", "silu_ready", "dve_step", "act_step", "vec_tr", "vec_evac"]


def first_second_block(nc, A, out, where_both, where_first, where_second):
    plan, phases = make_plan(A)
    with ExitStack() as ctx:
        def sb(name, shape, dt=F32):
            return ctx.enter_context(nc.sbuf_tensor(name, shape, dt))

        def ps(name, shape):
            return ctx.enter_context(nc.psum_tensor(name, shape, F32))

        sem = {name: ctx.enter_context(nc.semaphore(name)) for name in SEMS}
        raw_landed = [ctx.enter_context(nc.semaphore(f"raw_landed{s}")) for s in range(SLOTS)]

        raw = sb("raw", [P, SLOTS, PK * W])
        w_hi = sb("w_hi", [P, SLOTS, PK * W], F32R)
        w_lo = sb("w_lo", [P, SLOTS, PK * W], F32R)
        x = sb("x", [P, TT, D])
        h = sb("h", [P, TT, D])
        hT_hi = sb("hT_hi", [P, KT, S], F32R)
        hT_lo = sb("hT_lo", [P, KT, S], F32R)
        proj = sb("proj", [P, TT, 3 * D])
        tiles = sb("tiles", [P, 20, S])
        prob = sb("prob", [P, 4, TT, S])
        probT = sb("probT", [P, 2, TT * S])
        aux_hi = sb("aux_hi", [P, PK * S], F32R)
        aux_lo = sb("aux_lo", [P, PK * S], F32R)
        both = sb("both", [P, where_both["ident"][1]])
        n_first = max(b for _, b in where_first.values())
        n_second = max(b for _, b in where_second.values())
        region = sb("region", [P, max(2048 + n_first, n_second + 6 * HD2)])
        na_bias = region[:, 0:2048].rearrange("p (h k) -> p h k", h=NA_H)
        na_raw = tiles[:, 0:8, :].rearrange("p a s -> p (a s)").rearrange("p (h k) -> p h k", h=NA_H)
        nsa_gain = region[:, n_second:n_second + 4 * HD2]
        moba_gain = region[:, n_second + 4 * HD2:n_second + 6 * HD2]
        vec_rows = h[:, 0, 0:512].rearrange("p (a b) -> p a b", a=4)
        vecT = sb("vecT", [P, 4, P])
        post_gain = sb("post_gain", [P, D])
        gq_gain = sb("gq_gain", [P, 2, 6 * HD])
        subln = sb("subln", [P, 2, HD])
        lam_rows = sb("lam_rows", [P, 2, 4 * 32])
        small = sb("small", [P, 224])
        norm_rstd = small[:, 184:186]
        newton = small[:, 152:184]
        ss = small[:, 2:34]
        rstd = small[:, 34:66]
        mx = small[:, 66:74]
        nmx = small[:, 74:82]
        den = small[:, 82:90]
        rec = small[:, 90:98]
        lam = small[:, 98:104]
        gates = small[:, 104:152].rearrange("p (t b) -> p t b", t=TT)
        c_max = small[:, 186:202]
        c_rec = small[:, 202:218]

        acc = ps("acc", [P, 4, W])
        tr = ps("tr", [P, 2, W])
        up = ps("up", [P, 2, W])
        def norm_bank(ph, j):
            return (tr, acc if ph.layer is None else up)[j // 2][:, j % 2, :]

        def sum_bank(ph, i, t):
            if ph.out == "proj":
                return acc[:, 2 * (i % 2) + t, :]
            return (up, acc)[i][:, t, :]

        def flip_bank(j):
            return (tr, up)[j // 2][:, j % 2, :]

        accT = acc[:, :, :].rearrange("p b (k s) -> p (b k) s", k=2)

        def cb(name):
            a, b = where_both[name]
            return both[:, a:b]

        def c1(name):
            a, b = where_first[name]
            return region[:, 2048 + a:2048 + b]

        def c2(name):
            a, b = where_second[name]
            return region[:, a:b]

        ident = cb("ident")
        gain_col = vecT[:, 0, :]
        conv_b, conv_g, conv_beta = (vecT[:, 1, 8 * j:8 * j + 8] for j in range(3))
        cmp_pos = vecT[:, 1, 24:88].rearrange("p (j l) -> p j l", j=2)

        def tap(j, k):
            r = j * KT + k
            return vecT[:, 2 + r // 124, r % 124:r % 124 + 1]

        def f32(ap):
            return ap.bitcast(F32)

        def col(name):
            return A_COLS[name]

        def bc(ap, shape):
            return ap.broadcast_to(shape)

        def piece_view(buf, slot, start, kt, n):
            return buf[:, slot, start:start + kt * n].rearrange("p (k n) -> p k n", k=kt)

        def repeated(name, start, *dims):
            return bass.AP(A[name].tensor, start, [[0, P], *dims])

        rows = []
        for l in range(2):
            heads = gq_gain[:, l, :].rearrange("p (h c) -> p h c", c=HD)
            rows += [(heads[:, 0:4, :], repeated("gqa_q_norm", l * HD, [0, 4], [1, HD])),
                     (heads[:, 4:6, :], repeated("gqa_k_norm", l * HD, [0, 2], [1, HD])),
                     (subln[:, l, :], repeated("diff_subln", l * HD, [1, HD]))]
            for m, name in enumerate(("q1", "k1", "q2", "k2")):
                rows.append((lam_rows[:, l, 32 * m:32 * m + 32], repeated("diff_lambda_" + name, l * 32, [1, 32])))
        ROWS_LANDED = 16 * (len(rows) + 1)
        second_rows = [(nsa_gain[:, 0:HD2], repeated("nsa_q_norm_2", 0, [1, HD2])),
                       (nsa_gain[:, HD2:4 * HD2], repeated("nsa_k_norm_2", 0, [1, 3 * HD2])),
                       (moba_gain[:, 0:HD2], repeated("moba_q_norm_2", 0, [1, HD2])),
                       (moba_gain[:, HD2:2 * HD2], repeated("moba_k_norm_2", 0, [1, HD2]))]
        SECOND_LANDED = 16 * (len(second_rows) + 1)
        VEC_ROWS = (102, 88, 124, 124)
        FIRST_B = next((i for i, (kind, _) in enumerate(LAYERS) if kind != "A"), None)

        block = ctx.enter_context(nc.Block())

        def unit(q, k, outs, bias=None, bias_scale=1.0, scale=1.0, gate=None, pair=None):
            return dict(q=q, k=k, outs=outs, bias=bias, bias_scale=bias_scale, scale=scale, gate=gate, pair=pair)

        def half_rows(tile, row, rows):
            return tiles[row:row + rows, tile, :]

        def v_outs(kt_heads, v_col, dv, row, k_tile):
            return [(accT[row:row + dv, k_tile, :], proj[:, kt, v_col:v_col + dv], ("probT", kt))
                    for kt in range(TT)]

        def units_A():
            us = []
            for hh in range(NA_H):
                row, t = HD * (hh % 2), hh // 2
                us.append(unit(half_rows(t, row, HD), half_rows(2 + t, row, HD),
                               v_outs(None, col("na_v") + HD * hh, HD, row, t),
                               bias=na_bias[:, hh, :], bias_scale=float(HD) ** 0.5, scale=float(HD) ** -0.5))
            for hh in range(DF_H):
                slope, scale = 2.0 ** (-8.0 * (hh + 1) / DF_H), 32.0 ** -0.5
                for m in range(2):
                    row, t = 64 * (hh % 2) + 32 * m, hh // 2
                    us.append(unit(half_rows(4 + t, row, 32), half_rows(6 + t, row, 32),
                                   [(acc[:, 1, qt * 256 + HD * hh:qt * 256 + HD * hh + HD], ("probT_q", kt, qt),
                                     proj[:, kt, col("df_v") + HD * hh:col("df_v") + HD * hh + HD])
                                    for qt in range(TT) for kt in range(TT)],
                                   bias=c1("dist"), bias_scale=-slope / scale, scale=scale, pair=m))
            for hh in range(GQ_H):
                row, t = 64 * (hh // 2), hh % 2
                us.append(unit(half_rows(8 + t, row, HD), half_rows(10, row, HD),
                               v_outs(None, col("gq_v") + HD * (hh // 2), HD, HD * (hh % 2), 4 + hh // 2),
                               scale=float(HD) ** -0.5))
            for hh in range(ML_H):
                us.append(unit(tiles[0:96, 11 + hh, :], tiles[0:96, 15 + hh, :],
                               v_outs(None, A_IN + 128 * hh + 64, HD, HD * (hh % 2), 6 + hh // 2),
                               scale=96.0 ** -0.5))
            return us

        def units_nsa():
            us = []
            c_probT = proj[0:N_CMP, :, 0:D].rearrange("p t (a s) -> p t a s", a=4)
            for hh in range(H2):
                g = hh // 4
                for b in range(2):
                    outs = v_outs(None, (1792, 2304)[b] + HD2 * g, HD2, 0, hh)
                    if b == 0:
                        outs = [(accT[:, hh, :], c_value[0:N_CMP, HD2 * g:HD2 * g + HD2],
                                 c_probT[:, hh // 4, hh % 4, :])] + outs
                    us.append(unit(tiles[:, hh, :], tiles[:, (10, 12)[b] + g, :], outs, bias=c2("causal"),
                                   scale=float(HD2) ** -0.5, gate=gates[:, :, 8 * (b + 1) + hh], pair=("open", "close")[b]))
            return us

        def units_moba():
            return [unit(tiles[:, hh, :], tiles[:, H2 + hh, :], v_outs(None, 2 * D + HD2 * hh, HD2, 0, hh),
                         bias=c2("causal"), scale=float(HD2) ** -0.5) for hh in range(H2)]

        x_tap = h[:, 0, 0:CMP_L * GROUPS * N_CMP]
        c_keyT = h[:, 0, 960:990]
        c_valueT = h[:, 0, 990:1020]
        c_score = h[:, 1, 0:240].rearrange("p (a n) -> p a n", n=N_CMP)
        c_value = h[:, 1, 256:512]
        sq_tmp = h[:, 0, :]
        flat = tiles[:, :, :].rearrange("p a s -> p (a s)")
        u_pad = flat[:, 0:KT * (S + TAPS - 1)].rearrange("p (k s) -> p k s", k=KT)
        conv = flat[:, 2304:2304 + KT * S].rearrange("p (k s) -> p k s", k=KT)
        centre_sq = proj[:, 0, 0:KT * S].rearrange("p (k s) -> p k s", k=KT)
        silu = proj[:, 1, 0:KT * S].rearrange("p (k s) -> p k s", k=KT)
        mean_b = proj[:, 0, 2048:2048 + S]
        rstd_b = proj[:, 0, 2304:2304 + S]

        def jobs_for(kind):
            def two(c, w=P, step=P):
                return [proj[:, t, c + step * i:c + step * i + w] for i in range(2) for t in range(TT)]

            if kind == "A":
                one = [proj[:, t, col("gq_k"):col("gq_k") + P] for t in range(TT)]
                kcat = h[:, 1, 0:768].rearrange("p (t h c) -> p t h c", t=TT, h=ML_H)
                ks = [[kcat[:, t, 2 * j + i, :] for i in range(2) for t in range(TT)] for j in range(2)]
                return [(two(col("na_q")), tiles[:, 0:2, :], 1.0), (two(col("na_k")), tiles[:, 2:4, :], 1.0),
                        (two(col("df_q")), tiles[:, 4:6, :], 1.0), (two(col("df_k")), tiles[:, 6:8, :], 1.0),
                        (two(col("gq_q")), tiles[:, 8:10, :], 1.0), (one, tiles[:, 10:11, :], 1.0),
                        (two(2048, 96, 96), tiles[0:96, 11:13, :], 1.0),
                        (two(2048 + 192, 96, 96), tiles[0:96, 13:15, :], 1.0),
                        (ks[0], tiles[0:96, 15:17, :], 1.0), (ks[1], tiles[0:96, 17:19, :], 1.0)]
            qs = [(two(2 * P * j), tiles[:, 2 * j:2 * j + 2, :], 1.0) for j in range(4)]
            if kind == "nsa":
                return qs + [(two(c), tiles[:, 8 + 2 * j:10 + 2 * j, :], 1.0)
                             for j, c in enumerate((1024, 1536, 2048, 1280))]
            if kind == "sb":
                qs = [(src, dst, float(HD2) ** -0.5) for src, dst, _ in qs]
            return qs + [(two(D + 2 * P * j), tiles[:, H2 + 2 * j:H2 + 2 * j + 2, :], 1.0) for j in range(4)]

        @block.sync
        def _(sp):
            def load(ps_, i=None):
                p0 = ps_[0]
                if p0.before >= 0:
                    sp.wait_ge(sem["lo_ready"], along(i, ps_, lambda p: p.before + 1))
                for j, (at, kt, n, (what, w, *where)) in enumerate(p0.parts):
                    if what == "taps":
                        src = w[where[0]:where[0] + 16].rearrange("l p n -> p l n")
                    else:
                        k0 = along(i, ps_, lambda p: p.parts[j][3][2])
                        n0 = along(i, ps_, lambda p: p.parts[j][3][3])
                        rows = w.rearrange("(k p) n -> p k n", p=P)
                        src = rows[:, bass.ds(k0, kt), bass.ds(n0, n)]
                    sp.dma_start(piece_view(raw, p0.slot, at, kt, n), src).then_inc(raw_landed[p0.slot], 16)

            sp.dma_start(x[:, :, :], A["x"][0].rearrange("(t p) d -> p t d", p=P)).then_inc(sem["x_landed"], 16)
            sp.dma_start(both[:, :], A["both"]).then_inc(sem["const_landed"], 16)
            for r0, slab, name in ((0, 0, "pre_mix_norm"), (16, 0, "pre_ffn_norm"), (32, 0, "attn_norm_2"),
                                   (64, 0, "mlp_norm_2"), (96, 0, "mla_q_norm"), (100, 0, "mla_kv_norm"),
                                   (0, 1, "conv_dw_b_2"), (8, 1, "conv_ln_g_2"), (16, 1, "conv_ln_b_2")):
                v = A[name].rearrange("l (k c) -> (l k) c", c=P)
                sp.dma_start(vec_rows[r0:r0 + v.shape[0], slab, :], v).then_inc(sem["vec_landed"], 16)
            pos = A["nsa_cmp_pos_2"][0].rearrange("j l d -> (j l) d")
            sp.dma_start(vec_rows[24:88, 1, :], pos).then_inc(sem["vec_landed"], 16)
            taps = A["conv_dw_w_2"][0].rearrange("j (k c) -> (j k) c", c=P)
            for half in range(2):
                sp.dma_start(vec_rows[0:124, 2 + half, :], taps[124 * half:124 * half + 124, :])\
                  .then_inc(sem["vec_landed"], 16)
            at = 0
            for ph in phases:
                last = phases[-1] is ph
                if ph.kind == "ffn":
                    while at < ph.first:
                        load([plan.pieces[at]])
                        at += 1
                    head = ph.ups + ph.per
                    for p in range(at, ph.first + head):
                        load([plan.pieces[p]])
                    with sp.Fori(0, ph.n - 2) as i:
                        for j in range(ph.per):
                            load([plan.pieces[ph.first + head + ph.per * s + j] for s in range(ph.n - 2)], i)
                    at = ph.first + head + ph.per * (ph.n - 2)
                    for j in range(ph.downs):
                        load([plan.pieces[at]])
                        at += 1
            total = Tally()
            for ph in phases:
                total.advance(ph)
            sp.wait_ge(sem["x_written"], total["x_written"])
            sp.dma_start(out[0].rearrange("(t p) d -> p t d", p=P), x[:, :, :]).then_inc(sem["out_stored"], 16)
            sp.wait_ge(sem["out_stored"], 16)

        @block.gpsimd
        def _(pool):
            n = Tally()
            for ph in phases:
                if ph.kind == "ffn" and ph.variant == "B":
                    for i, steps in ffn_schedule(ph, pool):
                        for t in range(TT):
                            pool.wait_ge(sem["r_ready"], along(i, steps, lambda c: n["r_ready"] + 2 * c + t + 1))
                            r = proj[:, t, 0:W]
                            nc.gpsimd.tensor_tensor(proj[:, t, W:2 * W], r, r, ALU.mult).then_inc(sem["r2_ready"], 1)
                n.advance(ph)

        @block.scalar
        def _(act):
            n = Tally()
            steps_done = [0]
            split_at = [0]

            def link(ins):
                steps_done[0] += 1
                ins.then_inc(sem["act_step"], 1)
                act.wait_ge(sem["act_step"], steps_done[0])

            def split_hi(ps_, i=None):
                p0 = ps_[0]
                act.wait_ge(raw_landed[p0.slot], along(i, ps_, lambda p: p.landed))
                if p0.before >= 0:
                    act.wait_ge(sem["piece_used"], along(i, ps_, lambda p: p.before + 1))
                nc.scalar.activation(w_hi[:, p0.slot, 0:p0.floats], raw[:, p0.slot, 0:p0.floats], ACT.Copy)\
                    .then_inc(sem["hi_ready"], 1)

            def split_next(k=2):
                for _ in range(k):
                    if split_at[0] < len(plan.pieces):
                        split_hi([plan.pieces[split_at[0]]])
                        split_at[0] += 1

            def norm(ph):
                for k in range(KT):
                    if k % 2 == 0:
                        act.wait_ge(sem["hT_tr"], n["hT_tr"] + k // 2 + 1)
                    g = gain_col[:, ph.gain + k:ph.gain + k + 1]
                    nc.scalar.activation(hT_hi[:, k, :], norm_bank(ph, k // 2)[:, S * (k % 2):S * (k % 2) + S], ACT.Copy,
                                         scale=g).then_inc(sem["hT_hi"], 1)
                if n["x_written"]:
                    act.wait_ge(sem["x_written"], n["x_written"])
                if ph.bias_load is not None:
                    for r in range(S // GRID):
                        for hh in range(NA_H):
                            start = ((ph.bias_load * NA_H + hh) * 15 + 7 - r) * 31 + 15 - (GRID - 1)
                            src = bass.AP(A["na_rel_bias"].tensor, start, [[1, GRID], [31, S // GRID], [1, GRID]])
                            dst = na_raw[GRID * (r % 2):GRID * (r % 2) + GRID, hh, S * (r // 2):S * (r // 2) + S]
                            act.dma_start(dst.rearrange("p (a c) -> p a c", c=GRID), src).then_inc(sem["na_landed"], 16)
                if ph.post is not None:
                    act.dma_start(post_gain[:, :], repeated(ph.post[0], ph.post[1] * D, [1, D])).then_inc(sem["post_landed"], 16)
                for t in range(TT):
                    nc.scalar.activation(h[:, t, :], x[:, t, :], ACT.Square, accum_out=ss[:, t:t + 1])\
                        .then_inc(sem["ss_ready"], 1)

            def y_square(bank, t, b):
                nc.scalar.activation(proj[:, t, W * b:W * b + W], bank, ACT.Square,
                                     accum_out=ss[:, 2 + 2 * t + b:3 + 2 * t + b]).then_inc(sem["y_sq"], 1)

            def gemm(ph):
                for i, (n0, w, pieces) in enumerate(ph.chunks):
                    split_next()
                    if ph.out == "x":
                        continue
                    if ph.out == "y":
                        act.wait_ge(sem["tile_done"], n["tile_done"] + i + 1)
                        y_square(sum_bank(ph, i, 0), 0, i)
                        act.wait_ge(sem["piece_used"], pieces[-1][0] + 1)
                        y_square(sum_bank(ph, i, 1), 1, i)
                        continue
                    act.wait_ge(sem["piece_used"], pieces[-1][0] + 1)
                    act.wait_ge(sem["rstd_ready"], n["rstd_ready"])
                    nc.scalar.activation(proj[:, 0, n0:n0 + w], sum_bank(ph, i, 0)[:, 0:w], ACT.Copy,
                                         scale=norm_rstd[:, 0:1]).then_inc(sem["evac_a"], 1)

            def evac_job(j, dst, scale, base):
                act.wait_ge(sem["pt_ready"], base + j + 1)
                src = tr[0:dst.shape[0], j % 2, 0:dst.shape[1] * S].rearrange("p (a s) -> p a s", s=S)
                nc.scalar.activation(dst, src, ACT.Copy, scale=scale).then_inc(sem["pt_evac"], 1)

            def unit_pipeline(us, jobs):
                with_T = [i for i, u in enumerate(us) if u["pair"] != 0]
                for i in range(len(us) + 2):
                    if i < len(us):
                        u = us[i]
                        act.wait_ge(sem["s_max"], n["s_max"] + i + 1)
                        slot = i % 4
                        for qt in range(TT):
                            c = 2 * slot + qt
                            src = prob[:, slot, qt, :] if u["bias"] is not None else up[:, i % 2, S * qt:S * qt + S]
                            nc.scalar.activation(prob[:, slot, qt, :], src, ACT.Exp, bias=nmx[:, c:c + 1],
                                                 scale=u["scale"], accum_out=den[:, c:c + 1]).then_inc(sem["p_exp"], 1)
                    if i >= 2 and (i - 2) in with_T:
                        j = with_T.index(i - 2)
                        act.wait_ge(sem["pt_ready"], n["pt_ready"] + jobs + j + 1)
                        if j >= 2:
                            act.wait_ge(sem["o_done"], n["o_done"] + j - 1)
                        nc.scalar.activation(probT[:, j % 2, :], tr[:, (jobs + j) % 2, :], ACT.Copy)\
                            .then_inc(sem["pt_evac"], 1)

            def mix_out_hi(ks, n_o):
                act.wait_ge(sem["o_done"], n["o_done"] + n_o)
                for k in ks:
                    nc.scalar.activation(hT_hi[:, k, :], accT[:, k, :], ACT.Copy).then_inc(sem["hT_hi"], 1)

            def mix_A(ph):
                l = ph.l
                jobs = jobs_for("A")
                for j in range(4):
                    evac_job(j, jobs[j][1], 1.0, n["pt_ready"])
                act.wait_ge(sem["lam_ready"], n["lam_ready"] + 1)
                nc.scalar.activation(lam[:, 0:2], lam[:, 2:4], ACT.Exp).then_inc(sem["lam_exp"], 1)
                for k in range(3):
                    act.wait_ge(sem["aux_tr"], n["aux_tr"] + (1 if k < 2 else 2))
                    g = 96 + 2 * l + k if k < 2 else 100 + l
                    nc.scalar.activation(aux_hi[:, S * k:S * k + S], tr[:, k // 2, S * (k % 2):S * (k % 2) + S],
                                         ACT.Copy, scale=gain_col[:, g:g + 1]).then_inc(sem["aux_hi"], 1)
                for j in (4, 5):
                    evac_job(j, jobs[j][1], 1.0, n["pt_ready"])
                act.wait_ge(sem["piece_used"], ph.uq + 1)
                nc.scalar.activation(proj[:, 0, 2048:2432], acc[:, 0, 0:384], ACT.Copy).then_inc(sem["evac_a"], 1)
                act.wait_ge(sem["piece_used"], ph.ukv + 1)
                nc.scalar.activation(proj[:, 0, A_IN:A_IN + W], acc[:, 2, :], ACT.Copy).then_inc(sem["evac_a"], 1)
                act.wait_ge(sem["evac_a"], n["evac_a"] + 2)
                act.wait_ge(sem["evac_d"], n["evac_d"] + 2)
                act.wait_ge(sem["prep"], n["prep"] + 2)
                kcat = h[:, 1, 0:768].rearrange("p (t h c) -> p t h c", t=TT, h=ML_H)
                for t in range(TT):
                    kv = proj[:, t, A_IN:A_IN + W].rearrange("p (h c) -> p h c", h=ML_H)
                    nc.scalar.activation(kcat[:, t, :, 0:HD], kv[:, :, 0:HD], ACT.Copy).then_inc(sem["kcat_a"], 1)
                split_next()
                for j in range(6, 10):
                    evac_job(j, jobs[j][1], 1.0, n["pt_ready"])
                unit_pipeline(units_A(), 10)
                mix_out_hi((0, 1, 4, 5, 6, 7), 16)
                act.wait_ge(sem["hT_tr"], n["hT_tr"] + 1)
                for k in range(2):
                    nc.scalar.activation(hT_hi[:, 2 + k, :], tr[:, 0, S * k:S * k + S], ACT.Copy)\
                        .then_inc(sem["hT_hi"], 1)

            def mix_nsa(ph):
                jobs = jobs_for("nsa")
                act.wait_ge(sem["evac_a"], n["evac_a"])
                act.wait_ge(sem["evac_d"], n["evac_d"])
                nc.scalar.activation(gates, proj[:, :, 2560:2584], ACT.Sigmoid).then_inc(sem["gate_ready"], 1)
                for j in (7, 4, 0, 1, 2, 3, 5, 6):
                    jj = (7, 4, 0, 1, 2, 3, 5, 6).index(j)
                    act.wait_ge(sem["pt_ready"], n["pt_ready"] + jj + 1)
                    src = tr[:, jj % 2, :].rearrange("p (a s) -> p a s", s=S)
                    nc.scalar.activation(jobs[j][1], src, ACT.Copy).then_inc(sem["pt_evac"], 1)
                for b in range(2):
                    act.wait_ge(sem["x_tap"], n["x_tap"] + b + 1)
                    nc.scalar.activation(aux_hi[:, 0:960], x_tap, ACT.Copy).then_inc(sem["aux_hi"], 1)
                    split_next()
                    act.wait_ge(sem["piece_used"], ph.cmp[b][1] + 1)
                    nc.scalar.activation((c_keyT, c_valueT)[b], up[:, b, 0:30], ACT.Copy).then_inc(sem["cmp_evac"], 1)
                act.wait_ge(sem["pt_ready"], n["pt_ready"] + 9)
                nc.scalar.activation(c_value[0:N_CMP, :], tr[0:N_CMP, 0, 0:2 * HD2], ACT.Copy)\
                    .then_inc(sem["pt_evac"], 1)
                act.wait_ge(sem["c_sub"], n["c_sub"] + 1)
                nc.scalar.activation(c_score, c_score, ACT.Exp, scale=float(HD2) ** -0.5).then_inc(sem["c_exp"], 1)
                c_probT = proj[0:N_CMP, :, 0:D].rearrange("p t (a s) -> p t a s", a=4)
                for j in range(4):
                    act.wait_ge(sem["pt_ready"], n["pt_ready"] + 10 + j)
                    src = tr[0:N_CMP, (9 + j) % 2, :].rearrange("p (a s) -> p a s", s=S)
                    nc.scalar.activation(c_probT[:, j // 2, 2 * (j % 2):2 * (j % 2) + 2, :], src, ACT.Copy)\
                        .then_inc(sem["pt_evac"], 1)
                unit_pipeline(units_nsa(), 13)
                mix_out_hi(range(KT), 16)

            def mix_moba(ph):
                jobs = jobs_for("moba")
                for j, (_, dst, scale) in enumerate(jobs):
                    evac_job(j, dst, scale, n["pt_ready"])
                unit_pipeline(units_moba(), 8)
                mix_out_hi(range(KT), 8)

            def mix_sb(ph):
                jobs = jobs_for("sb")
                for j, (_, dst, scale) in enumerate(jobs):
                    evac_job(j, dst, scale, n["pt_ready"])
                for i in range(H2 + 1):
                    if i < H2:
                        act.wait_ge(sem["s_ready"], n["s_ready"] + i + 1)
                        if i >= 2:
                            act.wait_ge(sem["pt_ready"], n["pt_ready"] + 8 + i - 1)
                        w1 = prob[:, i % 2, :, :].rearrange("p t s -> p (t s)")
                        link(nc.scalar.activation(w1, up[:, i % 2, :], ACT.Abs))
                        link(nc.scalar.activation(w1, w1, ACT.Exp, scale=-1.0))
                        nc.scalar.activation(w1, w1, ACT.Ln, bias=1.0).then_inc(sem["sb_log"], 1)
                    if i >= 1:
                        j = i - 1
                        act.wait_ge(sem["sb_diff"], n["sb_diff"] + j + 1)
                        if j >= 2:
                            act.wait_ge(sem["o_done"], n["o_done"] + j - 1)
                        w2 = prob[:, 2 + j % 2, :, :].rearrange("p t s -> p (t s)")
                        nc.scalar.activation(probT[:, j % 2, :], w2, ACT.Exp).then_inc(sem["pt_evac"], 1)
                mix_out_hi(range(KT), H2)

            def mix_conv(ph):
                act.wait_ge(sem["evac_a"], n["evac_a"])
                act.wait_ge(sem["evac_d"], n["evac_d"])
                for t in range(TT):
                    b = proj[:, t, D:2 * D]
                    nc.scalar.activation(b, b, ACT.Sigmoid).then_inc(sem["gate_ready"], 1)
                for j in range(4):
                    act.wait_ge(sem["pt_ready"], n["pt_ready"] + j + 1)
                    src = tr[:, j % 2, :].rearrange("p (a s) -> p a s", s=S)
                    nc.scalar.activation(u_pad[:, 2 * j:2 * j + 2, TAPS - 1:TAPS - 1 + S], src, ACT.Copy)\
                        .then_inc(sem["pt_evac"], 1)
                act.wait_ge(sem["centred"], n["centred"] + 1)
                nc.scalar.activation(centre_sq, conv, ACT.Square).then_inc(sem["sq_ready"], 1)
                act.wait_ge(sem["normed"], n["normed"] + 1)
                for k in range(KT):
                    nc.scalar.activation(silu[:, k, :], conv[:, k, :], ACT.Silu, scale=conv_g[:, k:k + 1],
                                         bias=conv_beta[:, k:k + 1]).then_inc(sem["silu_ready"], 1)
                for k in range(KT):
                    act.wait_ge(sem["silu_ready"], n["silu_ready"] + k + 1)
                    nc.scalar.activation(hT_hi[:, k, :], silu[:, k, :], ACT.Copy).then_inc(sem["hT_hi"], 1)

            def ffn(ph):
                def used(c):
                    return ph.first + (ph.ups if c == 0 else ph.ups + ph.per * (c - 1) + ph.ups)

                for i, steps in ffn_schedule(ph, act):
                    def pieces_at(offset):
                        at = [ph.first + ph.ups + ph.per * (c - 1) + offset for c in steps]
                        return [plan.pieces[p] for p in at if p < len(plan.pieces)]

                    if steps[0] > 0:
                        for j in range(ph.downs):
                            split_hi(pieces_at(ph.ups + j), i)
                    if steps[0] == 0:
                        act.wait_ge(sem["rstd_ready"], n["rstd_ready"])
                    act.wait_ge(sem["piece_used"], along(i, steps, used))
                    for t in range(TT):
                        if ph.variant == "B":
                            nc.scalar.activation(proj[:, t, 0:W], up[:, t, :], ACT.Relu, scale=norm_rstd[:, t:t + 1])\
                                .then_inc(sem["r_ready"], 1)
                        else:
                            nc.scalar.activation(proj[:, t, 0:CH_A], up[:, t, 0:CH_A], ACT.Silu,
                                                 scale=norm_rstd[:, t:t + 1])\
                                .then_inc(sem["r_ready"], 1)
                    for j in range(2):
                        if pieces_at(ph.per + j):
                            split_hi(pieces_at(ph.per + j), i)
                    jobs = ph.kt // 2
                    for j in range(jobs):
                        act.wait_ge(sem["act_tr"], along(i, steps, lambda c: n["act_tr"] + jobs * c + j + 1))
                        nc.scalar.activation(aux_hi[:, W * j:W * j + W], tr[:, j, :], ACT.Copy)\
                            .then_inc(sem["act_hi"], 1)
                end = ph.first + ph.ups + ph.per * (ph.n - 1) + ph.downs
                split_at[0] = ph.first + ph.ups + ph.per * (ph.n - 1) + 2
                split_next(end + 2 - split_at[0])
                if ph.variant == "A":
                    for t in range(TT):
                        if t == 0:
                            act.wait_ge(sem["tile_done"], n["tile_done"] + 1)
                        else:
                            act.wait_ge(sem["piece_used"], end)
                        for b in range(2):
                            y_square(acc[:, 2 * t + b, :], t, b)

            for dst, src in rows:
                act.dma_start(dst, src).then_inc(sem["row_landed"], 16)
            act.dma_start(region[:, 2048:2048 + n_first], A["first"]).then_inc(sem["row_landed"], 16)
            for s, w in enumerate(VEC_ROWS):
                act.wait_ge(sem["vec_tr"], 1)
                nc.scalar.activation(vecT[:, s, 0:w], tr[:, 0, P * s:P * s + w], ACT.Copy).then_inc(sem["vec_evac"], 1)
            act.wait_ge(sem["vec_evac"], 4)
            split_next()
            todo = {"norm": norm, "gemm": gemm, "mixA": mix_A, "nsa": mix_nsa, "sb": mix_sb,
                    "conv": mix_conv, "moba": mix_moba, "ffn": ffn}
            for index, ph in enumerate(phases):
                if ph.kind == "norm" and ph.layer == FIRST_B:
                    act.wait_ge(sem["x_written"], n["x_written"])
                    act.dma_start(region[:, 0:n_second], A["second"]).then_inc(sem["second_landed"], 16)
                    for dst, src in second_rows:
                        act.dma_start(dst, src).then_inc(sem["second_landed"], 16)
                todo[ph.kind](ph)
                n.advance(ph)

        @block.vector
        def _(dve):
            n = Tally()
            done = [0]
            split_at = [0]

            def link(ins):
                done[0] += 1
                ins.then_inc(sem["dve_step"], 1)
                dve.wait_ge(sem["dve_step"], done[0])

            def split_lo(ps_, i=None):
                p0 = ps_[0]
                dve.wait_ge(sem["hi_ready"], along(i, ps_, lambda p: p.index + 1))
                m = p0.floats
                nc.vector.tensor_tensor(w_lo[:, p0.slot, 0:m], raw[:, p0.slot, 0:m], f32(w_hi[:, p0.slot, 0:m]),
                                        ALU.subtract).then_inc(sem["lo_ready"], 1)

            def split_next(k=2):
                for _ in range(k):
                    if split_at[0] < len(plan.pieces):
                        split_lo([plan.pieces[split_at[0]]])
                        split_at[0] += 1

            def root(dst, sums, width, a=None):
                a, t = newton[:, 0:dst.shape[1]] if a is None else a, sums
                link(nc.vector.tensor_scalar(a, sums, 1.0 / width, EPS, ALU.mult, ALU.add))
                link(nc.vector.tensor_scalar(t.bitcast(I32), a.bitcast(I32), 1, None, ALU.logical_shift_right))
                link(nc.vector.tensor_scalar(dst.bitcast(I32), t.bitcast(I32), -1.0, float(0x5f3759df), ALU.mult,
                                             ALU.add))
                link(nc.vector.tensor_scalar(a, a, -0.5, None, ALU.mult))
                for step in range(NEWTON_STEPS):
                    link(nc.vector.tensor_tensor(t, dst, dst, ALU.mult))
                    link(nc.vector.tensor_tensor(t, t, a, ALU.mult))
                    ins = nc.vector.scalar_tensor_tensor(out=dst, in0=t, scalar=1.5, in1=dst, op0=ALU.add, op1=ALU.mult)
                    if step < NEWTON_STEPS - 1:
                        link(ins)
                return ins

            def norm(ph):
                for k in range(KT):
                    dve.wait_ge(sem["hT_hi"], n["hT_hi"] + 2 * (k // 2) + 2)
                    g = gain_col[:, ph.gain + k:ph.gain + k + 1]
                    nc.vector.scalar_tensor_tensor(
                        out=hT_lo[:, k, :], in0=norm_bank(ph, k // 2)[:, S * (k % 2):S * (k % 2) + S], scalar=g,
                        in1=f32(hT_hi[:, k, :]), op0=ALU.mult, op1=ALU.subtract).then_inc(sem["hT_lo"], 1)
                dve.wait_ge(sem["ss_ready"], n["ss_ready"] + TT)
                root(norm_rstd, ss[:, 0:TT], D).then_inc(sem["rstd_ready"], 1)

            def gemm(ph):
                dve.wait_ge(sem["rstd_ready"], n["rstd_ready"])
                for i, (n0, w, pieces) in enumerate(ph.chunks):
                    split_next()
                    if ph.out == "y":
                        for t in range(TT):
                            dve.wait_ge(sem["y_sq"], n["y_sq"] + 2 * i + t + 1)
                            y_gain(ph, sum_bank(ph, i, t), t, i)
                            if i == len(ph.chunks) - 1:
                                add_y(t)
                        continue
                    dve.wait_ge(sem["piece_used"], pieces[-1][0] + 1)
                    if ph.out == "x":
                        for t in range(TT):
                            xt = x[:, t, n0:n0 + w]
                            nc.vector.tensor_tensor(xt, xt, sum_bank(ph, i, t), ALU.add).then_inc(sem["x_written"], 1)
                    else:
                        nc.vector.tensor_scalar(proj[:, 1, n0:n0 + w], sum_bank(ph, i, 1)[:, 0:w], norm_rstd[:, 1:2], None,
                                                ALU.mult).then_inc(sem["evac_d"], 1)
                    if i == 0 and ph.bias is not None:
                        dve.wait_ge(sem["na_flip"], n["na_flip"] + 1)
                        dve.wait_ge(sem["row_landed"], ROWS_LANDED)
                        mask = bc(c1("na_mask").unsqueeze(1), [P, TT, S])
                        for hh in range(NA_H):
                            nc.vector.tensor_tensor(na_bias[:, hh, :].rearrange("p (t k) -> p t k", t=TT),
                                                    flip_bank(hh).rearrange("p (t k) -> p t k", t=TT), mask, ALU.add)\
                                .then_inc(sem["na_ready"], 1)

            def y_gain(ph, bank, t, b):
                dve.wait_ge(sem["post_landed"], 16 * (ph.row + 1))
                c = slice(W * b, W * b + W)
                link(nc.vector.tensor_tensor(h[:, t, c], bank, post_gain[:, c], ALU.mult))

            def add_y(t):
                sums, r = ss[:, 6 + t:7 + t], rstd[:, t:t + 1]
                link(nc.vector.tensor_tensor(sums, ss[:, 2 + 2 * t:3 + 2 * t], ss[:, 3 + 2 * t:4 + 2 * t], ALU.add))
                link(root(r, sums, D))
                for b in range(2):
                    c = slice(W * b, W * b + W)
                    nc.vector.scalar_tensor_tensor(out=x[:, t, c], in0=h[:, t, c], scalar=r, in1=x[:, t, c],
                                                   op0=ALU.mult, op1=ALU.add).then_inc(sem["x_written"], 1)

            def unit_pipeline(us):
                for i in range(len(us) + 1):
                    if i < len(us):
                        u, slot = us[i], i % 4
                        dve.wait_ge(sem["s_ready"], n["s_ready"] + i + 1)
                        sc = up[:, i % 2, :]
                        if u["bias"] is not None:
                            sp_ = prob[:, slot, :, :].rearrange("p t s -> p (t s)")
                            link(nc.vector.scalar_tensor_tensor(out=sp_, in0=u["bias"], scalar=u["bias_scale"], in1=sc,
                                                                op0=ALU.mult, op1=ALU.add))
                            sc = sp_
                        c = slice(2 * slot, 2 * slot + 2)
                        link(nc.vector.tensor_reduce(mx[:, c], sc.rearrange("p (t s) -> p t s", t=TT), AX_X, ALU.max))
                        nc.vector.tensor_scalar(nmx[:, c], mx[:, c], -u["scale"], None, ALU.mult)\
                            .then_inc(sem["s_max"], 1)
                    if i >= 1:
                        u, slot = us[i - 1], (i - 1) % 4
                        c = slice(2 * slot, 2 * slot + 2)
                        dve.wait_ge(sem["p_exp"], n["p_exp"] + 2 * i)
                        link(nc.vector.reciprocal(rec[:, c], den[:, c]))
                        if u["gate"] is not None:
                            link(nc.vector.tensor_tensor(rec[:, c], rec[:, c], u["gate"], ALU.mult))
                        if u["pair"] == 1:
                            link(nc.vector.tensor_scalar(rec[:, c], rec[:, c], lam[:, 4:5], None, ALU.mult))
                        for qt in range(TT):
                            r = rec[:, 2 * slot + qt:2 * slot + qt + 1]
                            pq = prob[:, slot, qt, :]
                            if u["pair"] == 0:
                                link(nc.vector.tensor_scalar(pq, pq, r, None, ALU.mult))
                            elif u["pair"] == 1:
                                nc.vector.scalar_tensor_tensor(out=pq, in0=pq, scalar=r, in1=prob[:, (i - 2) % 4, qt, :],
                                                               op0=ALU.mult, op1=ALU.add).then_inc(sem["p_norm"], 1)
                            else:
                                nc.vector.tensor_scalar(pq, pq, r, None, ALU.mult).then_inc(sem["p_norm"], 1)

            def mix_out_lo(ks, src):
                for j, k in enumerate(ks):
                    dve.wait_ge(sem["hT_hi"], n["hT_hi"] + 2 * (j // 2) + 2)
                    nc.vector.tensor_tensor(hT_lo[:, k, :], src(k), f32(hT_hi[:, k, :]), ALU.subtract)\
                        .then_inc(sem["hT_lo"], 1)

            def sums_of_squares(src, heads, width, dst, tmp):
                link(nc.vector.tensor_tensor(tmp, src, src, ALU.mult))
                return nc.vector.tensor_reduce(dst, tmp, AX_X, ALU.add)

            def mix_A(ph):
                l = ph.l
                dve.wait_ge(sem["evac_a"], n["evac_a"])
                dve.wait_ge(sem["evac_d"], n["evac_d"])
                dve.wait_ge(sem["row_landed"], ROWS_LANDED)
                gq = [proj[:, t, col("gq_q"):col("gq_q") + 6 * HD].rearrange("p (h c) -> p h c", c=HD) for t in range(TT)]
                t1 = [h[:, 0, 384 * t:384 * t + 384].rearrange("p (h c) -> p h c", c=HD) for t in range(TT)]
                t2 = [h[:, 1, 384 * t:384 * t + 384].rearrange("p (h c) -> p h c", c=HD) for t in range(TT)]
                for t in range(TT):
                    link(sums_of_squares(gq[t], 6, HD, ss[:, 6 * t:6 * t + 6], t1[t]))
                for t in range(TT):
                    cq = proj[:, t, 2048:2304].unsqueeze(1)
                    link(sums_of_squares(cq, 1, 256, ss[:, 12 + t:13 + t], h[:, 0, 0:256].unsqueeze(1)))
                for t in range(TT):
                    ckv = proj[:, t, 2304:2432].unsqueeze(1)
                    ins = sums_of_squares(ckv, 1, P, ss[:, 14 + t:15 + t], h[:, 0, 0:P].unsqueeze(1))
                    link(ins)
                for a, b, width in ((0, 12, HD), (12, 14, 256), (14, 16, P)):
                    link(root(rstd[:, a:b], ss[:, a:b], width))
                lr = lam_rows[:, l, :].rearrange("p (m a c) -> p m a c", m=2, a=2)
                pr = h[:, 0, 0:64].rearrange("p (m c) -> p m c", m=2)
                link(nc.vector.tensor_tensor(pr, lr[:, :, 0, :], lr[:, :, 1, :], ALU.mult))
                nc.vector.tensor_reduce(lam[:, 2:4], pr, AX_X, ALU.add).then_inc(sem["lam_ready"], 1)
                for t in range(TT):
                    for a, b, r in ((2048, 2304, 12 + t), (2304, 2432, 14 + t)):
                        ins = nc.vector.tensor_scalar(proj[:, t, a:b], proj[:, t, a:b], rstd[:, r:r + 1], None, ALU.mult)
                        if (t, a) != (TT - 1, 2304):
                            link(ins)
                ins.then_inc(sem["prep"], 1)
                for t in range(TT):
                    r = bc(rstd[:, 6 * t:6 * t + 6].unsqueeze(2), [P, 6, HD])
                    link(nc.vector.tensor_tensor(t1[t], gq[t], r, ALU.mult))
                    g = gq_gain[:, l, :].rearrange("p (h c) -> p h c", c=HD)
                    link(nc.vector.tensor_tensor(t1[t], t1[t], g, ALU.mult))
                    cos = c1("gq_cos")[:, HD * t:HD * t + HD]
                    sin = c1("gq_sin")[:, HD * t:HD * t + HD].rearrange("p (b a c) -> p b a c", b=2, a=2)
                    a4 = t1[t].rearrange("p h (b a c) -> p h b a c", b=2, a=2)
                    b4 = t2[t].rearrange("p h (b a c) -> p h b a c", b=2, a=2)
                    for b in range(2):
                        for a in range(2):
                            s = bc(sin[:, b, a, :].unsqueeze(1), [P, 6, 16])
                            link(nc.vector.tensor_tensor(b4[:, :, b, a, :], a4[:, :, b, 1 - a, :], s, ALU.mult))
                    link(nc.vector.tensor_tensor(t1[t], t1[t], bc(cos.unsqueeze(1), [P, 6, HD]), ALU.mult))
                    def perm(v):
                        return v[:, 0:4, :].rearrange("p (b a) c -> p a b c", a=2)
                    dst = gq[t][:, 0:4, :].rearrange("p (a b) c -> p a b c", a=2)
                    link(nc.vector.tensor_tensor(dst, perm(t1[t]), perm(t2[t]), ALU.add))
                    ins = nc.vector.tensor_tensor(gq[t][:, 4:6, :], t1[t][:, 4:6, :], t2[t][:, 4:6, :], ALU.add)
                    if t < TT - 1:
                        link(ins)
                ins.then_inc(sem["prep"], 1)
                dve.wait_ge(sem["lam_exp"], n["lam_exp"] + 1)
                link(nc.vector.tensor_tensor(lam[:, 5:6], lam[:, 1:2], lam[:, 0:1], ALU.subtract))
                link(nc.vector.tensor_scalar(lam[:, 4:5], lam[:, 5:6], -(0.8 - 0.6 * math.exp(-0.3 * l)), None, ALU.add))
                for k in range(3):
                    dve.wait_ge(sem["aux_hi"], n["aux_hi"] + (2 if k < 2 else 3))
                    g = 96 + 2 * l + k if k < 2 else 100 + l
                    nc.vector.scalar_tensor_tensor(
                        out=aux_lo[:, S * k:S * k + S], in0=tr[:, k // 2, S * (k % 2):S * (k % 2) + S],
                        scalar=gain_col[:, g:g + 1], in1=f32(aux_hi[:, S * k:S * k + S]), op0=ALU.mult,
                        op1=ALU.subtract).then_inc(sem["aux_lo"], 1)
                dve.wait_ge(sem["piece_used"], ph.uq + 1)
                nc.vector.tensor_copy(proj[:, 1, 2048:2432], acc[:, 1, 0:384]).then_inc(sem["evac_d"], 1)
                dve.wait_ge(sem["piece_used"], ph.ukv + 1)
                nc.vector.tensor_copy(proj[:, 1, A_IN:A_IN + W], acc[:, 3, :]).then_inc(sem["evac_d"], 1)
                dve.wait_ge(sem["evac_a"], n["evac_a"] + 2)
                dve.wait_ge(sem["evac_d"], n["evac_d"] + 2)
                kcat = h[:, 1, 0:768].rearrange("p (t h c) -> p t h c", t=TT, h=ML_H)
                for t in range(TT):
                    cos = c1("ml_cos")[:, 32 * t:32 * t + 32]
                    sin = c1("ml_sin")[:, 32 * t:32 * t + 32]
                    q = proj[:, t, 2048:2432].rearrange("p (h c) -> p h c", h=ML_H)[:, :, HD:HD + 32]
                    k = proj[:, t, 2432:2464].unsqueeze(1)
                    for v, hh in ((q, ML_H), (k, 1)):
                        tmp = h[:, 0, 0:32 * hh].rearrange("p (h c) -> p h c", h=hh)
                        for a in range(2):
                            s = bc(sin[:, 16 * a:16 * a + 16].unsqueeze(1), [P, hh, 16])
                            link(nc.vector.tensor_tensor(tmp[:, :, 16 * a:16 * a + 16],
                                                         v[:, :, 16 - 16 * a:32 - 16 * a], s, ALU.mult))
                        link(nc.vector.tensor_tensor(v, v, bc(cos.unsqueeze(1), [P, hh, 32]), ALU.mult))
                        ins = nc.vector.tensor_tensor(v, v, tmp, ALU.add)
                        if (t, hh) != (TT - 1, 1):
                            link(ins)
                ins.then_inc(sem["prep"], 1)
                dve.wait_ge(sem["prep"], n["prep"] + 3)
                for t in range(TT):
                    k = bc(proj[:, t, 2432:2464].unsqueeze(1), [P, ML_H, 32])
                    ins = nc.vector.tensor_copy(kcat[:, t, :, HD:HD + 32], k)
                    if t < TT - 1:
                        link(ins)
                ins.then_inc(sem["prep"], 1)
                split_next()
                dve.wait_ge(sem["na_ready"], n["na_ready"])
                unit_pipeline(units_A())
                mix_out_lo((0, 1, 4, 5, 6, 7), lambda k: accT[:, k, :])
                od = h[:, 0, 0:512].rearrange("p (a c) -> p a c", c=HD)
                tmp = h[:, 0, 512:1024].rearrange("p (a c) -> p a c", c=HD)
                link(nc.vector.tensor_copy(h[:, 0, 0:512], acc[:, 1, :]))
                link(sums_of_squares(od, 8, HD, ss[:, 16:24], tmp))
                link(root(rstd[:, 16:24], ss[:, 16:24], HD))
                link(nc.vector.tensor_tensor(od, od, bc(rstd[:, 16:24].unsqueeze(2), [P, 8, HD]), ALU.mult))
                keep = 1.0 - (0.8 - 0.6 * math.exp(-0.3 * l))
                nc.vector.scalar_tensor_tensor(out=od, in0=od, scalar=keep,
                                               in1=bc(subln[:, l, :].unsqueeze(1), [P, 8, HD]), op0=ALU.mult,
                                               op1=ALU.mult).then_inc(sem["od_ready"], 1)
                for k in range(2):
                    dve.wait_ge(sem["hT_hi"], n["hT_hi"] + 8)
                    nc.vector.tensor_tensor(hT_lo[:, 2 + k, :], tr[:, 0, S * k:S * k + S], f32(hT_hi[:, 2 + k, :]),
                                            ALU.subtract).then_inc(sem["hT_lo"], 1)

            def head_norm_rope(view, dims, gain, cos, sin, r):
                shape = [P, *dims, HD2]
                tmp = sq_tmp[:, 0:int(np.prod(dims)) * HD2]
                tmp = tmp.rearrange("p (a c) -> p a c", c=HD2) if len(dims) == 1 else \
                    tmp.rearrange("p (a b c) -> p a b c", b=dims[1], c=HD2)
                half = [P, *dims, HD2 // 2]

                def wide(ap, shp):
                    for _ in range(len(dims)):
                        ap = ap.unsqueeze(1)
                    return bc(ap, shp)

                def cut(ap, a):
                    lo, hi = 64 * a, 64 * a + 64
                    return ap[:, :, lo:hi] if len(dims) == 1 else ap[:, :, :, lo:hi]

                link(nc.vector.tensor_tensor(view, view, bc(r.unsqueeze(len(dims) + 1), shape), ALU.mult))
                g = wide(gain, shape) if len(dims) == 1 else bc(gain.unsqueeze(2), shape)
                link(nc.vector.tensor_tensor(view, view, g, ALU.mult))
                for a in range(2):
                    link(nc.vector.tensor_tensor(cut(tmp, a), cut(view, 1 - a),
                                                 wide(sin[:, 64 * a:64 * a + 64], half), ALU.mult))
                link(nc.vector.tensor_tensor(view, view, wide(cos, shape), ALU.mult))
                return nc.vector.tensor_tensor(view, view, tmp, ALU.add)

            def tables(t):
                return c2("cos")[:, HD2 * t:HD2 * t + HD2], c2("sin")[:, HD2 * t:HD2 * t + HD2]

            def mix_nsa(ph):
                dve.wait_ge(sem["evac_a"], n["evac_a"])
                dve.wait_ge(sem["evac_d"], n["evac_d"])
                dve.wait_ge(sem["second_landed"], SECOND_LANDED)
                q = [proj[:, t, 0:D].rearrange("p (h c) -> p h c", c=HD2) for t in range(TT)]
                k = [proj[:, t, D:D + 3 * 512].rearrange("p (a m) -> p a m", a=3)[:, :, 0:256]
                     .rearrange("p a (g c) -> p a g c", c=HD2) for t in range(TT)]
                for t in range(TT):
                    link(sums_of_squares(q[t], H2, HD2, ss[:, 14 * t:14 * t + 8],
                                         sq_tmp.rearrange("p (h c) -> p h c", c=HD2)))
                    tmp = sq_tmp[:, 0:768]
                    link(nc.vector.tensor_tensor(tmp.rearrange("p (a g c) -> p a g c", a=3, g=2), k[t], k[t], ALU.mult))
                    ins = nc.vector.tensor_reduce(ss[:, 14 * t + 8:14 * t + 14], tmp.rearrange("p (a c) -> p a c", c=HD2),
                                                  AX_X, ALU.add)
                    link(ins)
                link(root(rstd[:, 0:28], ss[:, 0:28], HD2))
                for t in range(TT):
                    cos, sin = tables(t)
                    kr = rstd[:, 14 * t + 8:14 * t + 14].rearrange("p (a g) -> p a g", a=3)
                    link(head_norm_rope(k[t], (3, 2), nsa_gain[:, HD2:4 * HD2].rearrange("p (a c) -> p a c", a=3),
                                        cos, sin, kr))
                    ins = head_norm_rope(q[t], (H2,), nsa_gain[:, 0:HD2], cos, sin, rstd[:, 14 * t:14 * t + 8])
                    if t < TT - 1:
                        link(ins)
                    else:
                        ins.then_inc(sem["prep"], 1)
                dve.wait_ge(sem["prep"], n["prep"] + 1)
                for b in range(2):
                    t0 = (8, 14)[b]
                    dve.wait_ge(sem["pt_evac"], n["pt_evac"] + 2 - b)
                    if b == 1:
                        dve.wait_ge(sem["piece_used"], ph.cmp[0][1] + 1)
                    src = bass.AP(tiles[:, t0, :].tensor, tiles[:, t0, :].offset,
                                  [list(tiles[:, t0, :].ap[0]), [1, CMP_L], [S, GROUPS], [CMP_STRIDE, N_CMP]])
                    dst = x_tap.rearrange("p (l g m) -> p l g m", l=CMP_L, g=GROUPS)
                    pos = bc(cmp_pos[:, b, :].unsqueeze(2).unsqueeze(3), [P, CMP_L, GROUPS, N_CMP])
                    nc.vector.tensor_tensor(dst, src, pos, ALU.add).then_inc(sem["x_tap"], 1)
                    dve.wait_ge(sem["aux_hi"], n["aux_hi"] + b + 1)
                    nc.vector.tensor_tensor(aux_lo[:, 0:960], x_tap, f32(aux_hi[:, 0:960]), ALU.subtract)\
                        .then_inc(sem["aux_lo"], 1)
                    split_next()
                dve.wait_ge(sem["c_ready"], n["c_ready"] + 1)
                src = up[:, 0, 0:256].rearrange("p (t h m) -> p t h m", t=TT, h=H2)[:, :, :, 0:N_CMP]
                c4 = h[:, 1, 0:240].rearrange("p (t h m) -> p t h m", t=TT, h=H2)
                mask = bc(c2("cmp_mask").rearrange("p (t m) -> p t m", t=TT).unsqueeze(2), [P, TT, H2, N_CMP])
                link(nc.vector.tensor_tensor(c4, src, mask, ALU.add))
                link(nc.vector.tensor_reduce(c_max, c_score, AX_X, ALU.max))
                nc.vector.tensor_tensor(c_score, c_score, bc(c_max.unsqueeze(2), [P, 16, N_CMP]), ALU.subtract)\
                    .then_inc(sem["c_sub"], 1)
                dve.wait_ge(sem["c_exp"], n["c_exp"] + 1)
                link(nc.vector.tensor_reduce(c_max, c_score, AX_X, ALU.add))
                link(nc.vector.reciprocal(c_rec, c_max))
                r3 = c_rec.rearrange("p (t h) -> p t h", t=TT)
                dve.wait_ge(sem["gate_ready"], n["gate_ready"] + 1)
                link(nc.vector.tensor_tensor(r3, r3, gates[:, :, 0:8], ALU.mult))
                link(nc.vector.tensor_tensor(r3, r3, bc(c2("cmp_any").unsqueeze(2), [P, TT, H2]), ALU.mult))
                nc.vector.tensor_tensor(c_score, c_score, bc(c_rec.unsqueeze(2), [P, 16, N_CMP]), ALU.mult)\
                    .then_inc(sem["c_prob"], 1)
                unit_pipeline(units_nsa())
                mix_out_lo(range(KT), lambda k: accT[:, k, :])

            def mix_moba(ph):
                dve.wait_ge(sem["evac_a"], n["evac_a"])
                dve.wait_ge(sem["evac_d"], n["evac_d"])
                dve.wait_ge(sem["second_landed"], SECOND_LANDED)
                v = {(t, j): proj[:, t, D * j:D * j + D].rearrange("p (h c) -> p h c", c=HD2)
                     for t in range(TT) for j in range(2)}
                for (t, j), a in v.items():
                    at = 16 * t + 8 * j
                    ins = sums_of_squares(a, H2, HD2, ss[:, at:at + 8], sq_tmp.rearrange("p (h c) -> p h c", c=HD2))
                    link(ins)
                link(root(rstd[:, 0:32], ss[:, 0:32], HD2))
                for (t, j), a in v.items():
                    at = 16 * t + 8 * j
                    cos, sin = tables(t)
                    ins = head_norm_rope(a, (H2,), moba_gain[:, HD2 * j:HD2 * j + HD2], cos, sin, rstd[:, at:at + 8])
                    if (t, j) != (TT - 1, 1):
                        link(ins)
                ins.then_inc(sem["prep"], 1)
                unit_pipeline(units_moba())
                mix_out_lo(range(KT), lambda k: accT[:, k, :])

            def mix_sb(ph):
                dve.wait_ge(sem["second_landed"], SECOND_LANDED)
                for i in range(H2 + 1):
                    if i < H2:
                        w1 = prob[:, i % 2, :, :].rearrange("p t s -> p (t s)")
                        w2 = prob[:, 2 + i % 2, :, :].rearrange("p t s -> p (t s)")
                        dve.wait_ge(sem["sb_log"], n["sb_log"] + i + 1)
                        link(nc.vector.scalar_tensor_tensor(out=w1, in0=up[:, i % 2, :], scalar=0.0, in1=w1,
                                                            op0=ALU.max, op1=ALU.add))
                        link(nc.vector.tensor_tensor(w1, w1, c2("before01"), ALU.mult))
                        if i >= 2:
                            dve.wait_ge(sem["pt_evac"], n["pt_evac"] + 8 + i - 1)
                        nc.vector.tensor_tensor(w2, up[:, i % 2, :], c2("before"), ALU.add).then_inc(sem["sb_sp"], 1)
                    if i >= 1:
                        j = i - 1
                        w2 = prob[:, 2 + j % 2, :, :].rearrange("p t s -> p (t s)")
                        dve.wait_ge(sem["sb_sp"], n["sb_sp"] + j + 1)
                        dve.wait_ge(sem["pt_ready"], n["pt_ready"] + 8 + j + 1)
                        nc.vector.tensor_tensor(w2, w2, tr[:, j % 2, :], ALU.subtract).then_inc(sem["sb_diff"], 1)
                mix_out_lo(range(KT), lambda k: accT[:, k, :])

            def mix_conv(ph):
                link(nc.vector.memset(u_pad[:, :, 0:TAPS - 1], 0.0))
                for t in range(TT):
                    dve.wait_ge(sem["gate_ready"], n["gate_ready"] + t + 1)
                    nc.vector.tensor_tensor(proj[:, t, 0:D], proj[:, t, 0:D], proj[:, t, D:2 * D], ALU.mult)\
                        .then_inc(sem["prep"], 1)
                dve.wait_ge(sem["pt_evac"], n["pt_evac"] + 4)
                first = done[0]
                for j in range(TAPS):
                    for k in range(KT):
                        src = u_pad[:, k, j:j + S]
                        if j == 0:
                            ins = nc.vector.tensor_scalar(conv[:, k, :], src, tap(0, k), conv_b[:, k:k + 1], ALU.mult,
                                                          ALU.add)
                        else:
                            dve.wait_ge(sem["dve_step"], first + KT * (j - 1) + k + 1)
                            ins = nc.vector.scalar_tensor_tensor(out=conv[:, k, :], in0=src, scalar=tap(j, k),
                                                                 in1=conv[:, k, :], op0=ALU.mult, op1=ALU.add)
                        if (j, k) == (TAPS - 1, KT - 1):
                            ins.then_inc(sem["conv_done"], 1)
                        else:
                            ins.then_inc(sem["dve_step"], 1)
                            done[0] += 1
                dve.wait_ge(sem["mean_ready"], n["mean_ready"] + 1)
                link(nc.vector.tensor_scalar(mean_b, up[:, 0, 0:S], 1.0 / D, None, ALU.mult))
                nc.vector.tensor_tensor(conv, conv, bc(mean_b.unsqueeze(1), [P, KT, S]), ALU.subtract)\
                    .then_inc(sem["centred"], 1)
                dve.wait_ge(sem["var_ready"], n["var_ready"] + 1)
                step_b, sums_b = (proj[:, 0, 2560 + S * j:2560 + S * j + S] for j in range(2))
                link(nc.vector.tensor_copy(sums_b, up[:, 1, 0:S]))
                link(root(rstd_b, sums_b, D, step_b))
                nc.vector.tensor_tensor(conv, conv, bc(rstd_b.unsqueeze(1), [P, KT, S]), ALU.mult)\
                    .then_inc(sem["normed"], 1)
                mix_out_lo(range(KT), lambda k: silu[:, k, :])

            def ffn(ph):
                dve.wait_ge(sem["rstd_ready"], n["rstd_ready"])
                for i, steps in ffn_schedule(ph, dve):
                    def pieces_at(offset):
                        at = [ph.first + ph.ups + ph.per * (c - 1) + offset for c in steps]
                        return [plan.pieces[p] for p in at if p < len(plan.pieces)]

                    if steps[0] > 0:
                        for j in range(ph.downs):
                            split_lo(pieces_at(ph.ups + j), i)
                    if ph.variant == "A":
                        for t in range(TT):
                            dve.wait_ge(sem["r_ready"], along(i, steps, lambda c: n["r_ready"] + 2 * c + t + 1))
                            nc.vector.scalar_tensor_tensor(
                                out=proj[:, t, W:W + CH_A], in0=up[:, t, CH_A:2 * CH_A], scalar=norm_rstd[:, t:t + 1],
                                in1=proj[:, t, 0:CH_A], op0=ALU.mult, op1=ALU.mult).then_inc(sem["r2_ready"], 1)
                    for j in range(2):
                        if pieces_at(ph.per + j):
                            split_lo(pieces_at(ph.per + j), i)
                    jobs = ph.kt // 2
                    for j in range(jobs):
                        dve.wait_ge(sem["act_hi"], along(i, steps, lambda c: n["act_hi"] + jobs * c + j + 1))
                        nc.vector.tensor_tensor(aux_lo[:, W * j:W * j + W], tr[:, j, :], f32(aux_hi[:, W * j:W * j + W]),
                                                ALU.subtract).then_inc(sem["act_lo"], 1)
                split_at[0] = ph.first + ph.ups + ph.per * (ph.n - 1) + 2
                end = ph.first + ph.ups + ph.per * (ph.n - 1) + ph.downs
                split_next(end + 2 - split_at[0])
                if ph.variant == "A":
                    for t in range(TT):
                        for b in range(2):
                            dve.wait_ge(sem["y_sq"], n["y_sq"] + 2 * t + b + 1)
                            y_gain(ph, acc[:, 2 * t + b, :], t, b)
                        add_y(t)
                else:
                    for b in range(2):
                        dve.wait_ge(sem["piece_used"], end - 1 + b)
                        for t in range(TT):
                            xt = x[:, t, W * b:W * b + W]
                            nc.vector.tensor_tensor(xt, xt, acc[:, 2 * t + b, :], ALU.add).then_inc(sem["x_written"], 1)

            split_next()
            todo = {"norm": norm, "gemm": gemm, "mixA": mix_A, "nsa": mix_nsa, "sb": mix_sb,
                    "conv": mix_conv, "moba": mix_moba, "ffn": ffn}
            for ph in phases:
                todo[ph.kind](ph)
                n.advance(ph)

        @block.tensor
        def _(pe):
            n = Tally()

            def three(dst, hi, lo, whi, wlo, first, last):
                nc.tensor.matmul(dst, hi, whi, start=first, stop=False)
                nc.tensor.matmul(dst, hi, wlo, start=False, stop=False)
                return nc.tensor.matmul(dst, lo, whi, start=False, stop=last)

            def norm(ph):
                for j in range(KT // 2):
                    if n["x_written"]:
                        pe.wait_ge(sem["x_written"], n["x_written"] - 4 + (ph.early if j < 2 else 4))
                    else:
                        pe.wait_ge(sem["x_landed"], 16)
                        pe.wait_ge(sem["vec_evac"], 4)
                    for k in range(2):
                        for t in range(TT):
                            c = P * (2 * j + k)
                            last = nc.tensor.transpose(norm_bank(ph, j)[:, S * k + P * t:S * k + P * t + P], x[:, t, c:c + P],
                                                       ident)
                    last.then_inc(sem["hT_tr"], 1)

            def gemm(ph):
                place = {k: j for j, k in enumerate(ph.order or range(KT))}
                for i, (n0, w, pieces) in enumerate(ph.chunks):
                    if i >= 2:
                        if ph.out == "proj":
                            pe.wait_ge(sem["evac_a"], n["evac_a"] + i - 1)
                            pe.wait_ge(sem["evac_d"], n["evac_d"] + i - 1)
                    for p, k0, kt in pieces:
                        slot = plan.pieces[p].slot
                        pe.wait_ge(sem["lo_ready"], p + 1)
                        whi, wlo = piece_view(w_hi, slot, 0, kt, w), piece_view(w_lo, slot, 0, kt, w)
                        for t in range(TT):
                            for k in range(kt):
                                kk = k0 + k
                                if i == 0 and t == 0:
                                    pe.wait_ge(sem["hT_lo"], n["hT_lo"] - KT + place[kk] + 1)
                                last = three(sum_bank(ph, i, t)[:, 0:w], hT_hi[:, kk, P * t:P * t + P],
                                             hT_lo[:, kk, P * t:P * t + P], whi[:, k, :], wlo[:, k, :],
                                             kk == 0, kk == KT - 1)
                            if ph.out == "y" and t == 0 and p == pieces[-1][0]:
                                last.then_inc(sem["tile_done"], 1)
                        last.then_inc(sem["piece_used"], 1)
                    if i == 0 and ph.bias is not None:
                        pe.wait_ge(sem["na_landed"], 256 * (ph.bias + 1))
                        pe.wait_ge(sem["row_landed"], ROWS_LANDED)
                        for hh in range(NA_H):
                            last = nc.tensor.matmul(flip_bank(hh), c1("flip"), na_raw[:, hh, :], start=True, stop=True)
                        last.then_inc(sem["na_flip"], 1)

            def job(j, src, base):
                if j >= 2:
                    pe.wait_ge(sem["pt_evac"], base + j - 1)
                for b, ap in enumerate(src):
                    last = nc.tensor.transpose(tr[0:ap.shape[1], j % 2, P * b:P * b + P], ap, ident)
                last.then_inc(sem["pt_ready"], 1)

            def unit_pipeline(us, jobs):
                with_T = [i for i, u in enumerate(us) if u["pair"] != 0]
                for i in range(len(us) + 3):
                    if i < len(us):
                        u = us[i]
                        if i >= 2 and us[i - 2]["bias"] is not None:
                            pe.wait_ge(sem["s_max"], n["s_max"] + i - 1)
                        elif i >= 2:
                            pe.wait_ge(sem["p_exp"], n["p_exp"] + 2 * (i - 1))
                        for qt in range(TT):
                            last = nc.tensor.matmul(up[:, i % 2, S * qt:S * qt + S], u["q"][:, P * qt:P * qt + P], u["k"],
                                                    start=True, stop=True)
                        last.then_inc(sem["s_ready"], 1)
                    if i >= 2 and (i - 2) in with_T:
                        j = with_T.index(i - 2)
                        pe.wait_ge(sem["p_norm"], n["p_norm"] + 2 * (j + 1))
                        if jobs + j >= 2:
                            pe.wait_ge(sem["pt_evac"], n["pt_evac"] + jobs + j - 1)
                        for kt in range(TT):
                            for qt in range(TT):
                                last = nc.tensor.transpose(
                                    tr[:, (jobs + j) % 2, S * kt + P * qt:S * kt + P * qt + P],
                                    prob[:, (i - 2) % 4, qt, P * kt:P * kt + P], ident)
                        last.then_inc(sem["pt_ready"], 1)
                    if i >= 3 and (i - 3) in with_T:
                        j = with_T.index(i - 3)
                        u = us[i - 3]
                        pe.wait_ge(sem["pt_evac"], n["pt_evac"] + jobs + j + 1)
                        pT = probT[:, j % 2, :].rearrange("p (k s) -> p k s", k=TT)

                        def operand(o):
                            if isinstance(o, tuple):
                                return pT[:, o[1], :] if o[0] == "probT" else pT[:, o[1], P * o[2]:P * o[2] + P]
                            return o
                        for m, (dst, lhs, rhs) in enumerate(u["outs"]):
                            if u["pair"] == 1:
                                start, stop = m % TT == 0, m % TT == TT - 1
                            else:
                                start = m == 0 and u["pair"] != "close"
                                stop = m == len(u["outs"]) - 1 and u["pair"] != "open"
                            last = nc.tensor.matmul(dst, operand(lhs), operand(rhs), start=start, stop=stop)
                        last.then_inc(sem["o_done"], 1)

            def mix_A(ph):
                jobs = jobs_for("A")
                pe.wait_ge(sem["evac_a"], n["evac_a"])
                pe.wait_ge(sem["evac_d"], n["evac_d"])
                pe.wait_ge(sem["na_ready"], n["na_ready"])
                for j in range(4):
                    job(j, jobs[j][0], n["pt_evac"])
                pe.wait_ge(sem["prep"], n["prep"] + 1)
                pe.wait_ge(sem["pt_evac"], n["pt_evac"] + 4)
                for k in range(3):
                    for t in range(TT):
                        c = 2048 + P * k
                        last = nc.tensor.transpose(tr[:, k // 2, S * (k % 2) + P * t:S * (k % 2) + P * t + P],
                                                   proj[:, t, c:c + P], ident)
                    if k:
                        last.then_inc(sem["aux_tr"], 1)
                pe.wait_ge(sem["aux_lo"], n["aux_lo"] + 3)
                for p, ks, w, b in ((ph.uq, (0, 1), 384, 0), (ph.ukv, (2,), W, 2)):
                    slot = plan.pieces[p].slot
                    pe.wait_ge(sem["lo_ready"], p + 1)
                    whi, wlo = piece_view(w_hi, slot, 0, len(ks), w), piece_view(w_lo, slot, 0, len(ks), w)
                    for t in range(TT):
                        for i, k in enumerate(ks):
                            c = S * k + P * t
                            last = three(acc[:, b + t, 0:w], aux_hi[:, c:c + P], aux_lo[:, c:c + P], whi[:, i, :],
                                         wlo[:, i, :], i == 0, i == len(ks) - 1)
                    last.then_inc(sem["piece_used"], 1)
                pe.wait_ge(sem["prep"], n["prep"] + 2)
                for j in (4, 5):
                    job(j, jobs[j][0], n["pt_evac"])
                pe.wait_ge(sem["prep"], n["prep"] + 4)
                pe.wait_ge(sem["kcat_a"], n["kcat_a"] + 2)
                for j in range(6, 10):
                    job(j, jobs[j][0], n["pt_evac"])
                pe.wait_ge(sem["pt_evac"], n["pt_evac"] + 10)
                unit_pipeline(units_A(), 10)
                pe.wait_ge(sem["od_ready"], n["od_ready"] + 1)
                for k in range(2):
                    for t in range(TT):
                        last = nc.tensor.transpose(tr[:, 0, S * k + P * t:S * k + P * t + P],
                                                   h[:, 0, 256 * t + P * k:256 * t + P * k + P], ident)
                last.then_inc(sem["hT_tr"], 1)

            def mix_nsa(ph):
                jobs = jobs_for("nsa")
                pe.wait_ge(sem["evac_a"], n["evac_a"])
                pe.wait_ge(sem["evac_d"], n["evac_d"])
                for jj, j in enumerate((7, 4, 0, 1, 2, 3, 5, 6)):
                    if jj == 1:
                        pe.wait_ge(sem["prep"], n["prep"] + 1)
                    job(jj, jobs[j][0], n["pt_evac"])
                for b in range(2):
                    pe.wait_ge(sem["aux_lo"], n["aux_lo"] + b + 1)
                    for half in range(2):
                        p = ph.cmp[b][half]
                        slot = plan.pieces[p].slot
                        pe.wait_ge(sem["lo_ready"], p + 1)
                        whi, wlo = piece_view(w_hi, slot, 0, 16, P), piece_view(w_lo, slot, 0, 16, P)
                        for l in range(16):
                            c = 30 * (16 * half + l)
                            dst = up[:, b, 0:30]
                            first, end = (half, l) == (0, 0), (half, l) == (1, 15)
                            nc.tensor.matmul(dst, whi[:, l, :], aux_hi[:, c:c + 30], start=first, stop=False)
                            nc.tensor.matmul(dst, whi[:, l, :], aux_lo[:, c:c + 30], start=False, stop=False)
                            last = nc.tensor.matmul(dst, wlo[:, l, :], aux_hi[:, c:c + 30], start=False, stop=end)
                        last.then_inc(sem["piece_used"], 1)
                pe.wait_ge(sem["cmp_evac"], n["cmp_evac"] + 2)
                pe.wait_ge(sem["pt_evac"], n["pt_evac"] + 8)
                for g in range(GROUPS):
                    last = nc.tensor.transpose(tr[0:N_CMP, 0, HD2 * g:HD2 * g + HD2],
                                               c_valueT[:, N_CMP * g:N_CMP * g + N_CMP], ident)
                last.then_inc(sem["pt_ready"], 1)
                for t in range(TT):
                    for hh in range(H2):
                        c = 128 * t + 16 * hh
                        g = hh // 4
                        last = nc.tensor.matmul(up[:, 0, c:c + N_CMP], tiles[:, hh, P * t:P * t + P],
                                                c_keyT[:, N_CMP * g:N_CMP * g + N_CMP], start=True, stop=True)
                last.then_inc(sem["c_ready"], 1)
                pe.wait_ge(sem["c_prob"], n["c_prob"] + 1)
                for j in range(4):
                    src = [c_score[:, 8 * t + 2 * j + i, :] for i in range(2) for t in range(TT)]
                    job(9 + j, src, n["pt_evac"])
                pe.wait_ge(sem["pt_evac"], n["pt_evac"] + 13)
                unit_pipeline(units_nsa(), 13)

            def mix_moba(ph):
                pe.wait_ge(sem["prep"], n["prep"] + 1)
                for j, (src, _, _) in enumerate(jobs_for("moba")):
                    job(j, src, n["pt_evac"])
                pe.wait_ge(sem["pt_evac"], n["pt_evac"] + 8)
                unit_pipeline(units_moba(), 8)

            def mix_sb(ph):
                pe.wait_ge(sem["evac_a"], n["evac_a"])
                pe.wait_ge(sem["evac_d"], n["evac_d"])
                pe.wait_ge(sem["second_landed"], SECOND_LANDED)
                for j, (src, _, _) in enumerate(jobs_for("sb")):
                    job(j, src, n["pt_evac"])
                pe.wait_ge(sem["pt_evac"], n["pt_evac"] + 8)
                for i in range(H2 + 2):
                    if i < H2:
                        if i >= 2:
                            pe.wait_ge(sem["sb_sp"], n["sb_sp"] + i - 1)
                        for st in range(TT):
                            last = nc.tensor.matmul(up[:, i % 2, S * st:S * st + S], tiles[:, H2 + i, P * st:P * st + P],
                                                    tiles[:, i, :], start=True, stop=True)
                        last.then_inc(sem["s_ready"], 1)
                    if 1 <= i <= H2:
                        j = i - 1
                        pe.wait_ge(sem["sb_sp"], n["sb_sp"] + j + 1)
                        if j >= 2:
                            pe.wait_ge(sem["sb_diff"], n["sb_diff"] + j - 1)
                        w1 = prob[:, j % 2, :, :]
                        nc.tensor.matmul(tr[:, j % 2, 0:S], c2("later"), w1[:, 0, :], start=True, stop=False)
                        nc.tensor.matmul(tr[:, j % 2, 0:S], c2("ones"), w1[:, 1, :], start=False, stop=True)
                        nc.tensor.matmul(tr[:, j % 2, S:2 * S], c2("later"), w1[:, 1, :], start=True, stop=True)\
                            .then_inc(sem["pt_ready"], 1)
                    if i >= 2:
                        j = i - 2
                        pe.wait_ge(sem["pt_evac"], n["pt_evac"] + 8 + j + 1)
                        for st in range(TT):
                            c = 2 * D + HD2 * j
                            last = nc.tensor.matmul(accT[:, j, :], proj[:, st, c:c + HD2],
                                                    probT[:, j % 2, S * st:S * st + S], start=st == 0, stop=st == TT - 1)
                        last.then_inc(sem["o_done"], 1)

            def mix_conv(ph):
                for j in range(4):
                    if j == 0:
                        pe.wait_ge(sem["prep"], n["prep"] + TT)
                    job(j, [proj[:, t, P * (2 * j + i):P * (2 * j + i) + P] for i in range(2) for t in range(TT)],
                        n["pt_evac"])
                pe.wait_ge(sem["conv_done"], n["conv_done"] + 1)
                pe.wait_ge(sem["second_landed"], SECOND_LANDED)
                for k in range(KT):
                    last = nc.tensor.matmul(up[:, 0, 0:S], c2("ones"), conv[:, k, :], start=k == 0, stop=k == KT - 1)
                last.then_inc(sem["mean_ready"], 1)
                pe.wait_ge(sem["sq_ready"], n["sq_ready"] + 1)
                for k in range(KT):
                    last = nc.tensor.matmul(up[:, 1, 0:S], c2("ones"), centre_sq[:, k, :], start=k == 0, stop=k == KT - 1)
                last.then_inc(sem["var_ready"], 1)

            def ffn(ph):
                wide = 2 * CH_A if ph.variant == "A" else W
                jobs = ph.kt // 2

                def hidden(i, steps):
                    for j in range(ph.ups):
                        ps_ = [plan.pieces[ph.first + j if c == 0 else ph.first + ph.ups + ph.per * (c - 1) + j]
                               for c in steps]
                        slot = ps_[0].slot
                        pe.wait_ge(sem["lo_ready"], along(i, ps_, lambda p: p.index + 1))
                        if j == 0 and steps[0] > 0:
                            name = "r_ready" if ph.variant == "B" else "r2_ready"
                            pe.wait_ge(sem[name], along(i, steps, lambda c: n[name] + 2 * c))
                        for t in range(TT):
                            for k in range(PK):
                                kk = PK * j + k
                                if steps[0] == 0 and t == 0:
                                    pe.wait_ge(sem["hT_lo"], n["hT_lo"] - KT + kk + 1)
                                xs = hT_hi[:, kk, P * t:P * t + P], hT_lo[:, kk, P * t:P * t + P]
                                if ph.variant == "B":
                                    a = W * k
                                    last = three(up[:, t, :], *xs, w_hi[:, slot, a:a + W], w_lo[:, slot, a:a + W],
                                                 kk == 0, kk == KT - 1)
                                else:
                                    def gate_up(w):
                                        v = w[:, slot, :].rearrange("p (g k n) -> p g k n", g=2, k=PK)
                                        return v[:, :, k, :]
                                    dst = up[:, t, :].rearrange("p (g n) -> p g n", g=2)
                                    last = three(dst, *xs, gate_up(w_hi), gate_up(w_lo), kk == 0, kk == KT - 1)
                        last.then_inc(sem["piece_used"], 1)

                def down(i, steps, first, final):
                    pe.wait_ge(sem["act_lo"], along(i, steps, lambda c: n["act_lo"] + jobs * c))
                    for j in range(ph.downs):
                        ps_ = [plan.pieces[ph.first + ph.ups + ph.per * (c - 1) + (ph.ups if c < ph.n else 0) + j]
                               for c in steps]
                        slot = ps_[0].slot
                        pe.wait_ge(sem["lo_ready"], along(i, ps_, lambda p: p.index + 1))
                        for t in range(TT):
                            for k in range(ph.kt):
                                c = S * k + P * t
                                for b in ((0, 1) if ph.downs == 1 else (j,)):
                                    a = D * k + W * b if ph.downs == 1 else W * k
                                    last = three(acc[:, 2 * t + b, :], aux_hi[:, c:c + P], aux_lo[:, c:c + P],
                                                 w_hi[:, slot, a:a + W], w_lo[:, slot, a:a + W], first and k == 0,
                                                 final and k == ph.kt - 1)
                            if ph.variant == "A" and final and t == 0:
                                last.then_inc(sem["tile_done"], 1)
                        last.then_inc(sem["piece_used"], 1)

                def turn(i, steps):
                    for t in range(TT):
                        pe.wait_ge(sem["r2_ready"], along(i, steps, lambda c: n["r2_ready"] + 2 * c + t + 1))
                    for j in range(jobs):
                        for k in range(2):
                            for t in range(TT):
                                c = W + P * (2 * j + k)
                                last = nc.tensor.transpose(tr[:, j, S * k + P * t:S * k + P * t + P],
                                                           proj[:, t, c:c + P], ident)
                        last.then_inc(sem["act_tr"], 1)

                for i, steps in ffn_schedule(ph, pe):
                    hidden(i, steps)
                    if steps[0] > 0:
                        down(i, steps, steps[0] == 1, False)
                    turn(i, steps)
                down(None, [ph.n], False, True)

            pe.wait_ge(sem["const_landed"], 16)
            pe.wait_ge(sem["vec_landed"], 16 * 12)
            for s, w in enumerate(VEC_ROWS):
                last = nc.tensor.transpose(tr[:, 0, P * s:P * s + w], vec_rows[0:w, s, :], ident[0:w, 0:w])
            last.then_inc(sem["vec_tr"], 1)
            todo = {"norm": norm, "gemm": gemm, "mixA": mix_A, "nsa": mix_nsa, "sb": mix_sb, "conv": mix_conv,
                    "moba": mix_moba, "ffn": ffn}
            for ph in phases:
                if ph.kind in todo:
                    todo[ph.kind](ph)
                n.advance(ph)


def kernel(**inputs):
    import concourse.bacc as bacc
    from concourse.bass_utils import run_bass_kernel_spmd

    tables = [packed(t) for t in constant_tables()]
    nc = bacc.Bacc("TRN2", target_bir_lowering=False, num_devices=1, dynamic_dma_scratch_size=1024)
    arrays, A = {}, {}
    given = {name: np.ascontiguousarray(a) for name, a in inputs.items()}
    given.update(zip(("both", "first", "second"), (t[0] for t in tables)))
    for name, a in given.items():
        arrays["in_" + name] = a
        A[name] = nc.dram_tensor("in_" + name, list(a.shape), mybir.dt.from_np(a.dtype), kind="ExternalInput").ap()
    out = nc.dram_tensor("out", [1, S, D], F32, kind="ExternalOutput").ap()
    first_second_block(nc, A, out, *(t[1] for t in tables))
    r = run_bass_kernel_spmd(nc, [arrays], core_ids=[0])
    return r.results[0]["out"]
```

```python
import math
from contextlib import ExitStack

import numpy as np

import concourse.bass as bass
from concourse import mybir

F32 = mybir.dt.float32
F32R = mybir.dt.float32r
I32 = mybir.dt.int32
ALU = mybir.AluOpType
ACT = mybir.ActivationFunctionType
AX_X = mybir.AxisListType.X

P = 128
S, D = 256, 1024
TT = S // P
KT = D // P
EPS = 1e-6
NEG = -1e30
LOWEST = -3e38
W = 512
PK = 4
SLOTS = 4

GRID = 64
NA_H = DF_H = GQ_H = ML_H = 4
HD = 64
FF_A = 2816
CH_A = 256
A_COLS = dict(na_q=0, na_k=256, na_v=512, df_q=768, df_k=1024, df_v=1280, gq_q=1536, gq_k=1792, gq_v=1920,
              cq=2048, ckv=2304, kr=2432)
A_IN = 2464
H2, HD2 = 8, 128
FF_B = 4096
CH_B = 512
NSA_IN = 2584
CMP_L, CMP_STRIDE, N_CMP, GROUPS = 32, 16, 15, 2
TAPS = 31
CONV_PE = 4
PE_TAPS = CONV_PE * TAPS

LAYERS = [("A", 0), ("A", 1), ("nsa", 0), ("sb", 1), ("conv", 2), ("moba", 3)]


def rope_tables(pos, width):
    half = width // 2
    inv = np.float32(10000.0) ** (-np.arange(half, dtype=np.float32) / np.float32(half))
    ang = pos.astype(np.float32)[:, None] * inv[None, :].astype(np.float32)
    c, s = np.cos(ang), np.sin(ang)
    return np.concatenate([c, c], 1).astype(np.float32), np.concatenate([-s, s], 1).astype(np.float32)


def df_slope(head):
    return 2.0 ** (-8.0 * (head + 1) / DF_H)


def constant_tables():
    def tiles(a):
        return a.reshape(TT, P, -1).transpose(1, 0, 2).reshape(P, -1)

    t = np.arange(S)
    row, col = t // GRID, t % GRID
    both = {"ident": np.eye(P), "ones": np.ones((P, P))}
    c1, s1 = rope_tables(row, HD // 2)
    c2, s2 = rope_tables(col, HD // 2)
    cm, sm = rope_tables(t, HD // 2)
    start = np.clip(col - 8, 0, GRID - 16)
    seen = (col[None, :] >= start[:, None]) & (col[None, :] < start[:, None] + 16)
    first = {
        "flip": np.kron(np.eye(2), np.eye(GRID)[::-1]),
        "na_mask": np.where(seen, 0.0, NEG)[:P],
        "dist": tiles(-np.abs(t[:, None] - t[None, :])),
        "df_scale": np.array([[32.0 ** -0.5 / df_slope(2 * a + p // HD) for a in range(2)] for p in range(P)]),
        "gq_cos": tiles(np.concatenate([c1, c2], 1)), "gq_sin": tiles(np.concatenate([s1, s2], 1)),
        "ml_cos": tiles(cm), "ml_sin": tiles(sm),
    }
    cb, sb = rope_tables(t, HD2)
    end = np.arange(N_CMP) * CMP_STRIDE + CMP_L - 1
    second = {
        "causal": tiles(np.where(t[None, :] <= t[:, None], 0.0, NEG))[:, np.r_[0:P, S:2 * S]],
        "before": tiles(np.where(t[:, None] < t[None, :], 0.0, NEG))[:, np.r_[0:S, S + P:2 * S]],
        "later": (np.arange(P)[:, None] >= np.arange(P)[None, :]) * 1.0,
        "cos": tiles(cb), "sin": tiles(sb),
        "cmp_mask": tiles(np.where(end[None, :] <= t[:, None], 0.0, NEG)),
        "cmp_any": tiles((t >= end[0])[:, None] * 1.0),
    }
    return both, first, second


def packed(tables):
    at, where = 0, {}
    for name, a in tables.items():
        where[name] = (at, at + a.shape[1])
        at += a.shape[1]
    return np.ascontiguousarray(np.concatenate(list(tables.values()), 1).astype(np.float32)), where


class Piece:

    def __init__(self, index, slot, parts):
        self.index, self.slot, self.parts = index, slot, parts
        self.floats = sum(kt * n for _, kt, n, _ in parts)
        self.before = -1
        self.landed = 0


class Plan:
    def __init__(self):
        self.pieces = []
        self.holder = {}
        self.slot_count = {}
        self.ring_start = 0

    def align(self):
        self.ring_start = len(self.pieces)

    def add(self, parts, ring=SLOTS):
        p = Piece(len(self.pieces), (len(self.pieces) - self.ring_start) % ring, parts)
        p.before = self.holder.get(p.slot, -1)
        self.slot_count[p.slot] = self.slot_count.get(p.slot, 0) + 16 * len(parts)
        p.landed = self.slot_count[p.slot]
        self.holder[p.slot] = p.index
        self.pieces.append(p)
        return p.index


class Phase:

    def __init__(self, kind, counts=None, chunks=None, out=None, gain=None, layer=None, post=None,
                 row=None, l=None, uq=None, ukv=None, cmp=None, variant=None,
                 first=None, n=None, per=None, ups=None, downs=None, kt=None):
        self.kind, self.counts = kind, counts or {}
        self.chunks, self.out, self.gain, self.layer, self.post = chunks, out, gain, layer, post
        self.order = None
        self.mix = None
        self.row, self.l, self.uq, self.ukv, self.cmp = row, l, uq, ukv, cmp
        self.variant, self.first, self.n, self.per, self.ups, self.downs, self.kt = variant, first, n, per, ups, downs, kt


def add_gemm(plan, w, k_rows, width, out, order=None, between=None):
    chunks = []
    kt_all = k_rows // P
    for n0 in (range(0, width, W) if order is None else [W * c for c in order]):
        n = min(W, width - n0)
        pieces = []
        for k0 in range(0, kt_all, PK):
            kt = min(PK, kt_all - k0)
            pieces.append((plan.add([(0, kt, n, ("rows", w, k0, n0))]), k0, kt))
        chunks.append((n0, n, pieces))
        if between and len(chunks) - 1 in between:
            between[len(chunks) - 1]()
    ph = Phase("gemm", chunks=chunks, out=out)
    if out == "proj":
        ph.counts = {"evac_a": len(chunks), "evac_d": len(chunks)}
    elif out == "gated":
        ph.counts = {"pad_ready": 1, "evac_a": len(chunks) // 2, "evac_d": len(chunks) // 2}
    elif out == "y":
        ph.counts = {"tile_done": len(chunks), "y_sq": TT * len(chunks), "x_written": 2 * TT}
    else:
        ph.counts = {"x_written": TT * len(chunks)}
    return ph


def make_plan(A):
    plan, phases = Plan(), []

    def norm(gain_col, layer, post=None):
        phases.append(Phase("norm", gain=gain_col, layer=layer, post=post,
                            counts={"ss_ready": TT, "rstd_ready": 1, "hT_tr": KT // 2, "hT_hi": KT, "hT_lo": KT}))

    def units(n, n_t, qk_jobs):
        return {"s_ready": n, "s_max": n, "p_exp": 2 * n, "p_norm": 2 * n_t, "pt_ready": n_t + qk_jobs,
                "pt_evac": n_t + qk_jobs, "o_done": n_t}

    def mix_counts(base):
        c = dict(base)
        c.update({"hT_hi": KT, "hT_lo": KT})
        return c

    for index, (kind, l) in enumerate(LAYERS):
        if kind == "A":
            norm(8 * l, index, ("post_mix_norm", l))
            latent = []

            def up_projections():
                latent.append(plan.add([(0, 2, 384, ("rows", A["mla_w_uq"][l], 0, 0))]))
                latent.append(plan.add([(0, 1, 512, ("rows", A["mla_w_ukv"][l], 0, 0))]))

            g1 = add_gemm(plan, A["w_in"][l], D, A_IN, "proj", (4, 3, 0, 1, 2), {2: up_projections})
            phases.append(g1)
            uq, ukv = latent
            c = mix_counts(units(20, 16, 10))
            c.update({"prep": 1, "lat_sq": 4, "gq_root": 1, "gq_prep": 1, "ml_prep": 1, "lat_a": 2, "lat_d": 2,
                      "na_flip": 1, "na_ready": NA_H, "aux_tr": 2, "aux_hi": 3, "aux_lo": 3,
                      "lam_ready": 1, "lam_exp": 1, "hT_tr": 1, "kcat_a": 2, "od_ready": 1})
            phases.append(Phase("mixA", l=l, uq=uq, ukv=ukv, counts=c))
            g1.mix = phases[-1]
            g2 = add_gemm(plan, A["w_o"][l], D, D, "y")
            g2.row = 2 * l
            phases.append(g2)
            norm(16 + 8 * l, None, ("post_ffn_norm", l))
            plan.align()
            first = len(plan.pieces)
            n = FF_A // CH_A
            gu, down = A["ffn_w_gate_up"][l], A["ffn_w_down"][l]

            def up(c):
                for k0 in (0, PK):
                    plan.add([(0, PK, CH_A, ("rows", gu, k0, c * CH_A)),
                              (PK * CH_A, PK, CH_A, ("rows", gu, k0, FF_A + c * CH_A))], ring=3)

            up(0)
            for c in range(1, n):
                up(c)
                plan.add([(0, 2, D, ("rows", down, 2 * (c - 1), 0))], ring=3)
            plan.add([(0, 2, D, ("rows", down, 2 * (n - 1), 0))], ring=3)
            plan.align()
            phases.append(Phase("ffn", variant="A", first=first, n=n, per=3, ups=2, downs=1, kt=2, row=2 * l + 1,
                                counts={"diag_ready": 1, "rows_done": 1, "g_ready": n, "u_ready": n, "r_ready": n, "r2_ready": n,
                                        "act_hi": n, "act_lo": n, "tile_done": 1, "y_sq": 2 * TT, "x_written": 2 * TT}))
        else:
            width = {"nsa": NSA_IN, "sb": 3 * D, "conv": 2 * D, "moba": 3 * D}[kind]
            norm(32 + 8 * l, index)
            if kind == "conv":
                phases.append(add_gemm(plan, A["conv_w_in_2"][0], D, width, "gated", (2, 3, 0, 1)))
            elif kind == "nsa":
                cmp_pieces = {}

                def add_cmp(j):
                    cmp_pieces[j] = [plan.add([(0, 16, P, ("taps", A["nsa_w_cmp_2"][0, j], 16 * half))])
                                     for half in range(2)]

                g1 = add_gemm(plan, A["nsa_w_in_2"][0], D, width, "proj", (2, 0, 1, 3, 4, 5),
                              {2: lambda: add_cmp(1), 4: lambda: add_cmp(0)})
                g1.counts["tab_ready"] = 1
            else:
                g1 = add_gemm(plan, A[kind + "_w_in_2"][0], D, width, "proj")
                g1.counts["tab_ready"] = 1 if kind == "moba" else 0
            if kind != "conv":
                phases.append(g1)
            if kind == "nsa":
                c = mix_counts(units(16, 16, 8 + 1))
                c.update({"c_turned": 4, "c_turn_evac": 4, "prep": 6, "heads_sq": 6, "heads_root": 3, "heads_scaled": 6, "aux_hi": 2, "aux_lo": 2,
                          "cmp_raw": 2, "cmp_tr": 2, "cmp_evac": 2, "x_tap": 2, "gate_ready": 1, "c_ready": 1, "c_sub": 1, "c_exp": 1,
                          "c_prob": 1})
                phases.append(Phase("nsa", cmp=cmp_pieces, counts=c))
                g1.mix = phases[-1]
            elif kind == "sb":
                c = mix_counts({name: H2 for name in ("s_ready", "sb_z", "sb_n", "sb_exp", "sb_log", "sb_sp", "sb_sum",
                                                      "sb_diff", "sb_prob", "pt_ready", "pt_evac", "o_done")})
                phases.append(Phase("sb", counts=c))
                g1.mix = phases[-1]
            elif kind == "conv":
                c = mix_counts({"pt_ready": 4, "pt_evac": 4, "diag_ready": PE_TAPS, "diag_used": PE_TAPS,
                                "conv_evac": CONV_PE, "conv_done": 1, "mean_ready": 1,
                                "centred": KT, "sq_ready": KT, "var_ready": 1, "normed": KT, "silu_ready": KT})
                phases.append(Phase("conv", counts=c))
            else:
                c = mix_counts(units(8, 8, 8))
                c.update({"prep": 4, "heads_sq": 4, "heads_root": 2, "heads_scaled": 4})
                phases.append(Phase("moba", counts=c))
                g1.mix = phases[-1]
            phases.append(add_gemm(plan, A[kind + "_w_out_2"][0], D, D, "x"))
            norm(64 + 8 * l, None)
            plan.align()
            first = len(plan.pieces)
            n = FF_B // CH_B
            w_up, w_down = A["mlp_w_up_2"][l], A["mlp_w_down_2"][l]

            def up_b(c):
                for k0 in (0, PK):
                    plan.add([(0, PK, W, ("rows", w_up, k0, c * CH_B))])

            def down_b(c):
                for n0 in (0, W):
                    plan.add([(0, PK, W, ("rows", w_down, PK * c, n0))])

            up_b(0)
            for c in range(1, n):
                up_b(c)
                down_b(c - 1)
            down_b(n - 1)
            phases.append(Phase("ffn", variant="B", first=first, n=n, per=4, ups=2, downs=2, kt=PK,
                                counts={"r_ready": 2 * n, "r2_ready": 2 * n, "act_hi": 2 * n, "act_lo": 2 * n, "x_written": 2 * TT}))
    return plan, phases


class Tally:

    def __init__(self):
        self.n = {}

    def __getitem__(self, name):
        return self.n.get(name, 0)

    def advance(self, phase):
        for name, k in phase.counts.items():
            self.n[name] = self.n.get(name, 0) + k


def along(i, steps, value):
    seen = [value(c) for c in steps]
    if i is None:
        return seen[0]
    rise = seen[1] - seen[0] if len(seen) > 1 else 0
    assert all(b - a == rise for a, b in zip(seen, seen[1:])), seen
    return seen[0] if rise == 0 else i * rise + seen[0]


def ffn_schedule(ph, engine):
    yield None, [0]
    yield None, [1]
    with engine.Fori(0, ph.n - 3) as i:
        yield i, list(range(2, ph.n - 1))
    yield None, [ph.n - 1]


SEMS = ["x_landed", "const_landed", "second_landed", "vec_landed", "vec_later_landed", "row_landed", "na_landed", "post_landed",
        "out_stored", "hi_ready", "lo_ready", "piece_used", "x_written", "ss_ready", "rstd_ready", "tile_done", "y_sq", "hT_tr", "hT_hi",
        "hT_lo", "evac_a", "evac_d", "s_ready", "s_max", "p_exp", "p_norm", "pt_ready", "pt_evac", "o_done",
        "prep", "lat_sq", "gq_root", "gq_prep", "ml_prep", "lat_a", "lat_d", "tab_ready", "heads_sq", "heads_root", "heads_scaled", "aux_tr", "aux_hi", "aux_lo", "na_ready", "na_flip", "lam_ready", "lam_exp", "kcat_a", "r_ready",
        "r2_ready", "g_ready", "u_ready", "rows_done", "act_hi", "act_lo", "od_ready", "cmp_raw", "cmp_tr", "cmp_evac", "x_tap", "gate_ready", "c_ready", "c_sub",
        "c_exp", "c_prob", "c_turned", "c_turn_evac", "sb_z", "sb_n", "sb_exp", "sb_log", "sb_sp", "sb_sum", "sb_diff", "sb_prob", "pad_ready", "diag_ready", "diag_used", "conv_evac", "conv_done", "mean_ready", "centred", "sq_ready",
        "var_ready", "normed", "silu_ready", "dve_step", "act_step", "pool_step", "vec_tr", "vec_evac"]


def first_second_block(nc, A, out, where_both, where_first, where_second):
    plan, phases = make_plan(A)
    with ExitStack() as ctx:
        def sb(name, shape, dt=F32):
            return ctx.enter_context(nc.sbuf_tensor(name, shape, dt))

        def ps(name, shape):
            return ctx.enter_context(nc.psum_tensor(name, shape, F32))

        sem = {name: ctx.enter_context(nc.semaphore(name)) for name in SEMS}
        raw_landed = [ctx.enter_context(nc.semaphore(f"raw_landed{s}")) for s in range(SLOTS)]

        raw = sb("raw", [P, SLOTS, PK * W])
        w_hi = sb("w_hi", [P, SLOTS, PK * W], F32R)
        w_lo = sb("w_lo", [P, SLOTS, PK * W], F32R)
        x = sb("x", [P, TT, D])
        h = sb("h", [P, TT, D])
        hT_hi = sb("hT_hi", [P, KT, S], F32R)
        hT_lo = sb("hT_lo", [P, KT, S], F32R)
        proj = sb("proj", [P, TT, 3 * D])
        tiles = sb("tiles", [P, 20, S])
        prob = sb("prob", [P, 4, TT, S])
        probT = sb("probT", [P, 2, TT * S])
        aux_hi = sb("aux_hi", [P, PK * S], F32R)
        aux_lo = sb("aux_lo", [P, PK * S], F32R)
        both = sb("both", [P, where_both["ones"][1]])
        n_first = max(b for _, b in where_first.values())
        n_second = max(b for _, b in where_second.values())
        region = sb("region", [P, max(2048 + n_first, n_second + 6 * HD2)])
        na_bias = region[:, 0:2048].rearrange("p (h k) -> p h k", h=NA_H)
        na_raw = tiles[:, 0:8, :].rearrange("p a s -> p (a s)").rearrange("p (h k) -> p h k", h=NA_H)
        nsa_gain = region[:, n_second:n_second + 4 * HD2]
        moba_gain = region[:, n_second + 4 * HD2:n_second + 6 * HD2]
        vec_rows = [h[:, 0, 0:P]] + [tiles[:, 8:10, :].rearrange("p a s -> p (a s)")[:, P * j:P * j + P] for j in range(3)]
        vecT = sb("vecT", [P, 4, P])
        post_gain = sb("post_gain", [P, D])
        gq_gain = sb("gq_gain", [P, 2, 6 * HD])
        subln = sb("subln", [P, 2, HD])
        lam_rows = sb("lam_rows", [P, 2, 4 * 32])
        small = sb("small", [P, 224])
        norm_rstd = small[:, 184:186]
        newton = small[:, 152:184]
        ss = small[:, 2:34]
        rstd = small[:, 34:66]
        mx = small[:, 66:74]
        nmx = small[:, 74:82]
        den = small[:, 82:90]
        rec = small[:, 90:98]
        lam = small[:, 98:104]
        gates = small[:, 104:152].rearrange("p (t b) -> p t b", t=TT)
        c_max = small[:, 186:202]
        c_rec = small[:, 202:218]

        acc = ps("acc", [P, 4, W])
        tr = ps("tr", [P, 2, W])
        up = ps("up", [P, 2, W])
        def norm_bank(ph, j):
            return (tr, acc if ph.layer is None else up)[j // 2][:, j % 2, :]

        def sum_bank(ph, i, t):
            if ph.out in ("proj", "gated"):
                return acc[:, 2 * (i % 2) + t, :]
            return (up, acc)[i][:, t, :]

        def flip_bank(j):
            return (tr, up)[j // 2][:, j % 2, :]

        accT = acc[:, :, :].rearrange("p b (k s) -> p (b k) s", k=2)

        def cb(name):
            a, b = where_both[name]
            return both[:, a:b]

        def c1(name):
            a, b = where_first[name]
            return region[:, 2048 + a:2048 + b]

        def c2(name):
            a, b = where_second[name]
            return region[:, a:b]

        ident = cb("ident")
        gain_col = vecT[:, 0, :]
        conv_b, conv_g, conv_beta = (vecT[:, 1, 8 * j:8 * j + 8] for j in range(3))
        cmp_pos = vecT[:, 1, 24:88].rearrange("p (j l) -> p j l", j=2)

        hidden_sums = [(up, tr)[a // 2][:, a % 2, 0:S] for a in range(4)]
        wide_sums = [bank[:, :, 0:S] for bank in (up, tr)]
        ffn_r = proj[:, 0, 0:4 * S]
        ffn_r2 = proj[:, 0, 4 * S:8 * S]
        gate_scaled, gate_silu, up_scaled, ffn_product = (proj[:, 0, 2 * S * j:2 * S * j + 2 * S] for j in range(4))
        rstd_diag = prob[:, 0, :, :].rearrange("p t s -> p (t s)")[:, 0:S]
        rstd_rows = prob[:, 1, 0, :]
        rstd_sq = small[:, 218:220]

        def pairs(ap):
            return ap.rearrange("p (a s) -> p a s", s=S)

        def tap(j, k):
            r = j * KT + k
            return vecT[:, 2 + r // 124, r % 124:r % 124 + 1]

        def f32(ap):
            return ap.bitcast(F32)

        def col(name):
            return A_COLS[name]

        def bc(ap, shape):
            return ap.broadcast_to(shape)

        def piece_view(buf, slot, start, kt, n):
            return buf[:, slot, start:start + kt * n].rearrange("p (k n) -> p k n", k=kt)

        def repeated(name, start, *dims):
            return bass.AP(A[name].tensor, start, [[0, P], *dims])

        rows = []
        for l in range(2):
            heads = gq_gain[:, l, :].rearrange("p (h c) -> p h c", c=HD)
            rows += [(heads[:, 0:4, :], repeated("gqa_q_norm", l * HD, [0, 4], [1, HD])),
                     (heads[:, 4:6, :], repeated("gqa_k_norm", l * HD, [0, 2], [1, HD])),
                     (subln[:, l, :], repeated("diff_subln", l * HD, [1, HD]))]
            for m, name in enumerate(("q1", "k1", "q2", "k2")):
                rows.append((lam_rows[:, l, 32 * m:32 * m + 32], repeated("diff_lambda_" + name, l * 32, [1, 32])))
        ROWS_LANDED = 16 * (len(rows) + 1)
        second_rows = [(nsa_gain[:, 0:HD2], repeated("nsa_q_norm_2", 0, [1, HD2])),
                       (nsa_gain[:, HD2:4 * HD2], repeated("nsa_k_norm_2", 0, [1, 3 * HD2])),
                       (moba_gain[:, 0:HD2], repeated("moba_q_norm_2", 0, [1, HD2])),
                       (moba_gain[:, HD2:2 * HD2], repeated("moba_k_norm_2", 0, [1, HD2]))]
        SECOND_LANDED = 16 * (len(second_rows) + 1)
        VEC_ROWS = (102, 88, 124, 124)
        FIRST_B = next((i for i, (kind, _) in enumerate(LAYERS) if kind != "A"), None)

        block = ctx.enter_context(nc.Block())

        def unit(q, k, outs, bias=None, scale=1.0, gate=None, pair=None, causal=False):
            return dict(q=q, k=k, outs=outs, bias=bias, scale=scale, gate=gate, pair=pair,
                        causal=causal)

        def score_columns(u, qt):
            return slice(P if u["causal"] and qt == 0 else S * qt, S * qt + S)

        def scores_of(slot):
            return prob[:, slot, :, :].rearrange("p t s -> p (t s)")

        def causal_outs(dst, v_col):
            v = [proj[:, kt, v_col:v_col + HD2] for kt in range(TT)]
            return [(dst, v[0], ("columns", 0, S)), (dst[:, P:S], v[1], ("columns", S, S + P))]

        def half_rows(tile, row, rows):
            return tiles[row:row + rows, tile, :]

        def v_outs(kt_heads, v_col, dv, row, k_tile):
            return [(accT[row:row + dv, k_tile, :], proj[:, kt, v_col:v_col + dv], ("probT", kt))
                    for kt in range(TT)]

        def units_A():
            us = []
            for hh in range(NA_H):
                row, t = HD * (hh % 2), hh // 2
                us.append(unit(half_rows(t, row, HD), half_rows(2 + t, row, HD),
                               v_outs(None, col("na_v") + HD * hh, HD, row, t),
                               bias=na_bias[:, hh, :], scale=float(HD) ** -0.5))
            for hh in range(DF_H):
                slope = df_slope(hh)
                for m in range(2):
                    row, t = 64 * (hh % 2) + 32 * m, hh // 2
                    us.append(unit(half_rows(4 + t, row, 32), half_rows(6 + t, row, 32),
                                   [(acc[:, 1, qt * 256 + HD * hh:qt * 256 + HD * hh + HD], ("probT_q", kt, qt),
                                     proj[:, kt, col("df_v") + HD * hh:col("df_v") + HD * hh + HD])
                                    for qt in range(TT) for kt in range(TT)],
                                   bias=c1("dist"), scale=slope, pair=m))
            for hh in range(GQ_H):
                row, t = 64 * (hh // 2), hh % 2
                us.append(unit(half_rows(8 + t, row, HD), half_rows(10, row, HD),
                               v_outs(None, col("gq_v") + HD * (hh // 2), HD, HD * (hh % 2), 4 + hh // 2),
                               scale=float(HD) ** -0.5))
            for hh in range(ML_H):
                us.append(unit(tiles[0:96, 11 + hh, :], tiles[0:96, 15 + hh, :],
                               v_outs(None, A_IN + 128 * hh + 64, HD, HD * (hh % 2), 6 + hh // 2),
                               scale=96.0 ** -0.5))
            return us

        NSA_ORDER = (0, 2, 4, 6, 1, 3, 5, 7)

        def c_share(hh):
            g = hh // 4
            return c_value[0:N_CMP, HD2 * g:HD2 * g + HD2], c_probT[:, hh // 4, hh % 4, :]

        def units_nsa():
            us = []
            for hh in NSA_ORDER:
                g = hh // 4
                for b in range(2):
                    outs = causal_outs(accT[:, hh, :], (1792, 2304)[b] + HD2 * g)
                    if hh % 2 and b == 1:
                        outs.append((accT[:, hh, :], *c_share(hh)))
                    us.append(unit(tiles[:, hh, :], tiles[:, (10, 12)[b] + g, :], outs, bias=c2("causal"), causal=True,
                                   scale=float(HD2) ** -0.5, gate=gates[:, :, 8 * (b + 1) + hh], pair=(("open", "inner") if hh % 2 == 0 else ("open", "close"))[b]))
            return us

        def units_moba():
            def outs(hh):
                first, later = (2 * D + HD2 * hh, accT[:, hh, 0:P]), accT[:, hh, P:S]
                v = [proj[:, kt, first[0]:first[0] + HD2] for kt in range(TT)]
                return [(first[1], v[0], ("columns", 0, P)), (later, v[0], ("columns", P, S)),
                        (later, v[1], ("columns", S, S + P))]

            return [unit(tiles[:, hh, :], tiles[:, H2 + hh, :], outs(hh), bias=c2("causal"), causal=True,
                         scale=float(HD2) ** -0.5, pair="halves") for hh in range(H2)]

        x_tap = h[:, 0, 0:CMP_L * GROUPS * N_CMP]
        c_keyT = h[:, 0, 960:990]
        c_valueT = h[:, 0, 990:1020]
        c_score = h[:, 1, 0:240].rearrange("p (a n) -> p a n", n=N_CMP)
        c_raw = [tiles[0:2 * N_CMP, 16 + b, 0:HD2] for b in range(2)]
        c_value = post_gain[:, 0:256]
        c_probT = proj[0:N_CMP, :, 0:D].rearrange("p t (a s) -> p t a s", a=4)
        lat_tmp = prob[:, 2:4, :, :].rearrange("p a t s -> p (a t s)")
        kcat = prob[:, 0:2, :, :].rearrange("p a t s -> p (a t s)")[:, 0:768]\
            .rearrange("p (t h c) -> p t h c", t=TT, h=ML_H)
        gq = [proj[:, t, col("gq_q"):col("gq_q") + 6 * HD].rearrange("p (h c) -> p h c", c=HD) for t in range(TT)]
        gq_t1 = [h[:, 0, 384 * t:384 * t + 384].rearrange("p (h c) -> p h c", c=HD) for t in range(TT)]
        gq_t2 = [h[:, 1, 384 * t:384 * t + 384].rearrange("p (h c) -> p h c", c=HD) for t in range(TT)]

        head_tab = [post_gain[:, 512 * j:512 * j + 512] for j in range(2)] + \
                   [probT[:, j, :] for j in range(2)]
        head_sq = [prob[:, 2 * t:2 * t + 2, :, :].rearrange("p a t s -> p (a t s)") for t in range(TT)]
        rope_tmp = h[:, 1, :]

        def head_set(kind, s):
            if kind == "moba":
                return ([proj[:, t, D * s:D * s + D].rearrange("p (h c) -> p h c", c=HD2) for t in range(TT)], H2,
                        [16 * s + 8 * t for t in range(TT)], s)
            if s == 0:
                return ([proj[:, t, D:D + 256].rearrange("p (h c) -> p h c", c=HD2) for t in range(TT)], 2, [0, 2], 0)
            if s == 1:
                return ([proj[:, t, 0:D].rearrange("p (h c) -> p h c", c=HD2) for t in range(TT)], H2, [4, 12], 1)
            return ([proj[:, t, 1536:2560].rearrange("p (a m) -> p a m", a=2)[:, :, 0:256]
                     .rearrange("p a (g c) -> p a g c", c=HD2) for t in range(TT)], 4, [20, 24], 2)

        def head_gains(kind):
            if kind == "moba":
                return [moba_gain[:, 0:HD2], moba_gain[:, HD2:2 * HD2]]
            return [nsa_gain[:, HD2:2 * HD2], nsa_gain[:, 0:HD2], nsa_gain[:, 2 * HD2:3 * HD2],
                    nsa_gain[:, 3 * HD2:4 * HD2]]

        def shaped_like(flat_, view):
            dims = view.shape[1:]
            flat_ = flat_[:, 0:int(np.prod(dims))]
            return flat_.rearrange("p (h c) -> p h c", c=HD2) if len(dims) == 2 else \
                flat_.rearrange("p (a g c) -> p a g c", g=dims[1], c=HD2)

        SEEN = S + P
        rooms = [prob[:, :, :, :].rearrange("p a t s -> p (a t s)"), h[:, :, :].rearrange("p t d -> p (t d)"),
                 probT[:, :, :].rearrange("p a s -> p (a s)"), post_gain[:, :],
                 tiles[:, 16:20, :].rearrange("p a s -> p (a s)")]
        places = [a[:, SEEN * j:SEEN * j + SEEN] for a in rooms for j in range(a.shape[1] // SEEN)]
        sb_log, sb_logit = places[0:H2], places[H2:2 * H2]
        flat = tiles[:, :, :].rearrange("p a s -> p (a s)")
        u_pad = flat[:, 0:KT * (S + TAPS - 1)].rearrange("p (k s) -> p k s", k=KT)
        conv = flat[:, 2304:2304 + KT * S].rearrange("p (k s) -> p k s", k=KT)
        centre_sq = proj[:, 0, 0:KT * S].rearrange("p (k s) -> p k s", k=KT)
        silu = proj[:, 1, 0:KT * S].rearrange("p (k s) -> p k s", k=KT)
        diags = [a[:, P * j:P * j + P] for a in
                 [h[:, 0, :], h[:, 1, :], proj[:, 0, 2 * D:3 * D], proj[:, 1, 2 * D:3 * D], post_gain[:, :],
                  prob[:, :, :, :].rearrange("p a t s -> p (a t s)"), probT[:, :, :].rearrange("p a s -> p (a s)"),
                  flat[:, 2304 + KT * S:20 * S]] for j in range(a.shape[1] // P)]
        mean_b = proj[:, 0, 2048:2048 + S]
        rstd_b = proj[:, 0, 2304:2304 + S]

        def jobs_for(kind):
            def two(c, w=P, step=P):
                return [proj[:, t, c + step * i:c + step * i + w] for i in range(2) for t in range(TT)]

            if kind == "A":
                one = [proj[:, t, col("gq_k"):col("gq_k") + P] for t in range(TT)]
                ks = [[kcat[:, t, 2 * j + i, :] for i in range(2) for t in range(TT)] for j in range(2)]
                return [(two(col("na_q")), tiles[:, 0:2, :], 1.0), (two(col("na_k")), tiles[:, 2:4, :], 1.0),
                        (two(col("df_q")), tiles[:, 4:6, :], 1.0), (two(col("df_k")), tiles[:, 6:8, :], 1.0),
                        (two(col("gq_q")), tiles[:, 8:10, :], 1.0), (one, tiles[:, 10:11, :], 1.0),
                        (two(2048, 96, 96), tiles[0:96, 11:13, :], 1.0),
                        (two(2048 + 192, 96, 96), tiles[0:96, 13:15, :], 1.0),
                        (ks[0], tiles[0:96, 15:17, :], 1.0), (ks[1], tiles[0:96, 17:19, :], 1.0)]
            qs = [(two(2 * P * j), tiles[:, 2 * j:2 * j + 2, :], 1.0) for j in range(4)]
            if kind == "nsa":
                return qs + [(two(c), tiles[:, 8 + 2 * j:10 + 2 * j, :], 1.0)
                             for j, c in enumerate((1024, 1536, 2048, 1280))]
            if kind == "sb":
                qs = [(src, dst, float(HD2) ** -0.5) for src, dst, _ in qs]
            return qs + [(two(D + 2 * P * j), tiles[:, H2 + 2 * j:H2 + 2 * j + 2, :], 1.0) for j in range(4)]

        def load_bias(engine, l):
            for r in range(S // GRID):
                for hh in range(NA_H):
                    start = ((l * NA_H + hh) * 15 + 7 - r) * 31 + 15 - (GRID - 1)
                    src = bass.AP(A["na_rel_bias"].tensor, start, [[1, GRID], [31, S // GRID], [1, GRID]])
                    dst = na_raw[GRID * (r % 2):GRID * (r % 2) + GRID, hh, S * (r // 2):S * (r // 2) + S]
                    engine.dma_start(dst.rearrange("p (a c) -> p a c", c=GRID), src).then_inc(sem["na_landed"], 16)

        @block.sync
        def _(sp):
            def load(ps_, i=None):
                p0 = ps_[0]
                if p0.before >= 0:
                    sp.wait_ge(sem["lo_ready"], along(i, ps_, lambda p: p.before + 1))
                for j, (at, kt, n, (what, w, *where)) in enumerate(p0.parts):
                    if what == "taps":
                        src = w[where[0]:where[0] + 16].rearrange("l p n -> p l n")
                    else:
                        k0 = along(i, ps_, lambda p: p.parts[j][3][2])
                        n0 = along(i, ps_, lambda p: p.parts[j][3][3])
                        rows = w.rearrange("(k p) n -> p k n", p=P)
                        src = rows[:, bass.ds(k0, kt), bass.ds(n0, n)]
                    sp.dma_start(piece_view(raw, p0.slot, at, kt, n), src).then_inc(raw_landed[p0.slot], 16)

            sp.dma_start(both[:, :], A["both"]).then_inc(sem["const_landed"], 16)
            sp.dma_start(x[:, :, :], A["x"][0].rearrange("(t p) d -> p t d", p=P)).then_inc(sem["x_landed"], 16)

            def load_rows(vectors, landed):
                for r0, dst, name in vectors:
                    v = A[name].rearrange("l (k c) -> (l k) c", c=P)
                    sp.dma_start(dst[r0:r0 + v.shape[0], :], v).then_inc(sem[landed], 16)

            load_rows([(r0, vec_rows[0], name) for r0, name in (
                (0, "pre_mix_norm"), (16, "pre_ffn_norm"), (32, "attn_norm_2"), (64, "mlp_norm_2"), (96, "mla_q_norm"),
                (100, "mla_kv_norm"))], "vec_landed")
            for at in range(SLOTS):
                load([plan.pieces[at]])
            sp.dma_start(region[:, 2048:2048 + n_first], A["first"]).then_inc(sem["row_landed"], 16)
            for dst, src in rows:
                sp.dma_start(dst, src).then_inc(sem["row_landed"], 16)
            load_rows([(0, vec_rows[1], "conv_dw_b_2"), (8, vec_rows[1], "conv_ln_g_2"),
                       (16, vec_rows[1], "conv_ln_b_2")], "vec_later_landed")
            pos = A["nsa_cmp_pos_2"][0].rearrange("j l d -> (j l) d")
            sp.dma_start(vec_rows[1][24:88, :], pos).then_inc(sem["vec_later_landed"], 16)
            taps = A["conv_dw_w_2"][0].rearrange("j (k c) -> (j k) c", c=P)
            for half in range(2):
                sp.dma_start(vec_rows[2 + half][0:124, :], taps[124 * half:124 * half + 124, :])\
                  .then_inc(sem["vec_later_landed"], 16)
            load([plan.pieces[SLOTS]])
            load_bias(sp, 0)
            at = SLOTS + 1
            for ph in phases:
                if ph.kind == "ffn":
                    while at < ph.first:
                        load([plan.pieces[at]])
                        at += 1
                    head = ph.ups + ph.per
                    for p in range(at, ph.first + head):
                        load([plan.pieces[p]])
                    with sp.Fori(0, ph.n - 2) as i:
                        for j in range(ph.per):
                            load([plan.pieces[ph.first + head + ph.per * s + j] for s in range(ph.n - 2)], i)
                    at = ph.first + head + ph.per * (ph.n - 2)
                    for j in range(ph.downs):
                        load([plan.pieces[at]])
                        at += 1
                    if ph.variant == "A" and ph.row == 1 and LAYERS[1:2] == [("A", 1)]:
                        sp.wait_ge(sem["x_written"], 4)
                        load_bias(sp, 1)
            total = Tally()
            for ph in phases:
                total.advance(ph)
            sp.wait_ge(sem["x_written"], total["x_written"])
            sp.dma_start(out[0].rearrange("(t p) d -> p t d", p=P), x[:, :, :]).then_inc(sem["out_stored"], 16)
            sp.wait_ge(sem["out_stored"], 16)

        @block.gpsimd
        def _(pool):
            n = Tally()
            done = [0]

            def link(ins):
                done[0] += 1
                ins.then_inc(sem["pool_step"], 1)
                pool.wait_ge(sem["pool_step"], done[0])

            def gq_rotate(ph):
                pool.wait_ge(sem["gq_root"], n["gq_root"] + 1)
                for t in range(TT):
                    t1, t2 = gq_t1[t], gq_t2[t]
                    r = bc(rstd[:, 6 * t:6 * t + 6].unsqueeze(2), [P, 6, HD])
                    link(nc.gpsimd.tensor_tensor(t1, gq[t], r, ALU.mult))
                    g = gq_gain[:, ph.l, :].rearrange("p (h c) -> p h c", c=HD)
                    link(nc.gpsimd.tensor_tensor(t1, t1, g, ALU.mult))
                    cos = c1("gq_cos")[:, HD * t:HD * t + HD]
                    sin = c1("gq_sin")[:, HD * t:HD * t + HD].rearrange("p (b a c) -> p b a c", b=2, a=2)
                    a4 = t1.rearrange("p h (b a c) -> p h b a c", b=2, a=2)
                    b4 = t2.rearrange("p h (b a c) -> p h b a c", b=2, a=2)
                    for b in range(2):
                        for a in range(2):
                            s = bc(sin[:, b, a, :].unsqueeze(1), [P, 6, 16])
                            link(nc.gpsimd.tensor_tensor(b4[:, :, b, a, :], a4[:, :, b, 1 - a, :], s, ALU.mult))
                    link(nc.gpsimd.tensor_tensor(t1, t1, bc(cos.unsqueeze(1), [P, 6, HD]), ALU.mult))

                    def perm(v):
                        return v[:, 0:4, :].rearrange("p (b a) c -> p a b c", a=2)
                    dst = gq[t][:, 0:4, :].rearrange("p (a b) c -> p a b c", a=2)
                    link(nc.gpsimd.tensor_tensor(dst, perm(t1), perm(t2), ALU.add))
                    ins = nc.gpsimd.tensor_tensor(gq[t][:, 4:6, :], t1[:, 4:6, :], t2[:, 4:6, :], ALU.add)
                    if t < TT - 1:
                        link(ins)
                ins.then_inc(sem["gq_prep"], 1)

            def ml_rotate(ph):
                pool.wait_ge(sem["lat_a"], n["lat_a"] + 2)
                pool.wait_ge(sem["lat_d"], n["lat_d"] + 2)
                for t in range(TT):
                    cos = c1("ml_cos")[:, 32 * t:32 * t + 32]
                    sin = c1("ml_sin")[:, 32 * t:32 * t + 32]
                    q = proj[:, t, 2048:2432].rearrange("p (h c) -> p h c", h=ML_H)[:, :, HD:HD + 32]
                    k = proj[:, t, 2432:2464].unsqueeze(1)
                    for v, hh in ((q, ML_H), (k, 1)):
                        tmp = h[:, 1, 768:768 + 32 * hh].rearrange("p (h c) -> p h c", h=hh)
                        for a in range(2):
                            s = bc(sin[:, 16 * a:16 * a + 16].unsqueeze(1), [P, hh, 16])
                            link(nc.gpsimd.tensor_tensor(tmp[:, :, 16 * a:16 * a + 16],
                                                         v[:, :, 16 - 16 * a:32 - 16 * a], s, ALU.mult))
                        link(nc.gpsimd.tensor_tensor(v, v, bc(cos.unsqueeze(1), [P, hh, 32]), ALU.mult))
                        link(nc.gpsimd.tensor_tensor(v, v, tmp, ALU.add))
                for t in range(TT):
                    k = bc(proj[:, t, 2432:2464].unsqueeze(1), [P, ML_H, 32])
                    ins = nc.gpsimd.tensor_copy(kcat[:, t, :, HD:HD + 32], k)
                    if t < TT - 1:
                        link(ins)
                ins.then_inc(sem["ml_prep"], 1)

            for ph in phases:
                if ph.kind == "gemm" and ph.mix is not None and ph.mix.kind == "mixA":
                    gq_rotate(ph.mix)
                    ml_rotate(ph.mix)
                if ph.kind == "gemm" and ph.mix is not None and ph.counts.get("tab_ready"):
                    pool.wait_ge(sem["ss_ready"], n["ss_ready"])
                    pool.wait_ge(sem["second_landed"], SECOND_LANDED)
                    for gain, tab in zip(head_gains(ph.mix.kind), head_tab):
                        for t in range(TT):
                            cos, sin = (c2(name)[:, HD2 * t:HD2 * t + HD2] for name in ("cos", "sin"))
                            at = 256 * t
                            nc.gpsimd.tensor_tensor(tab[:, at:at + 128], cos, gain, ALU.mult)
                            for a in (0, 64):
                                last = nc.gpsimd.tensor_tensor(tab[:, at + 128 + a:at + 192 + a], sin[:, a:a + 64],
                                                               gain[:, 64 - a:128 - a], ALU.mult)
                    last.then_inc(sem["tab_ready"], 1)
                if ph.kind == "gemm" and ph.out == "gated":
                    pool.wait_ge(sem["ss_ready"], n["ss_ready"])
                    nc.gpsimd.memset(u_pad[:, :, 0:TAPS - 1], 0.0).then_inc(sem["pad_ready"], 1)
                    for i in range(PE_TAPS):
                        k, j = i // TAPS, i % TAPS
                        if i >= len(diags):
                            pool.wait_ge(sem["diag_used"], n["diag_used"] + i - len(diags) + 1)
                        nc.gpsimd.tensor_scalar(diags[i % len(diags)], ident, tap(j, k), None, ALU.mult)\
                            .then_inc(sem["diag_ready"], 1)
                if ph.kind == "ffn" and ph.variant == "B":
                    for i, steps in ffn_schedule(ph, pool):
                        if steps[0] > 0:
                            pool.wait_ge(sem["act_lo"], along(i, steps, lambda c: n["act_lo"] + 2 * c))
                        for j in range(2):
                            pool.wait_ge(sem["r_ready"], along(i, steps, lambda c: n["r_ready"] + 2 * c + j + 1))
                            r = ffn_r[:, W * j:W * j + W]
                            nc.gpsimd.tensor_tensor(ffn_r2[:, W * j:W * j + W], r, r, ALU.mult)\
                                .then_inc(sem["r2_ready"], 1)
                n.advance(ph)

        @block.scalar
        def _(act):
            n = Tally()
            steps_done = [0]
            split_at = [0]

            def link(ins):
                steps_done[0] += 1
                ins.then_inc(sem["act_step"], 1)
                act.wait_ge(sem["act_step"], steps_done[0])

            def split_hi(ps_, i=None):
                p0 = ps_[0]
                act.wait_ge(raw_landed[p0.slot], along(i, ps_, lambda p: p.landed))
                if p0.before >= 0:
                    act.wait_ge(sem["piece_used"], along(i, ps_, lambda p: p.before + 1))
                nc.scalar.activation(w_hi[:, p0.slot, 0:p0.floats], raw[:, p0.slot, 0:p0.floats], ACT.Copy)\
                    .then_inc(sem["hi_ready"], 1)

            def split_next(k=2):
                for _ in range(k):
                    if split_at[0] < len(plan.pieces):
                        split_hi([plan.pieces[split_at[0]]])
                        split_at[0] += 1

            def norm(ph):
                for k in range(KT):
                    if k % 2 == 0:
                        act.wait_ge(sem["hT_tr"], n["hT_tr"] + k // 2 + 1)
                    g = gain_col[:, ph.gain + k:ph.gain + k + 1]
                    nc.scalar.activation(hT_hi[:, k, :], norm_bank(ph, k // 2)[:, S * (k % 2):S * (k % 2) + S], ACT.Copy,
                                         scale=g).then_inc(sem["hT_hi"], 1)
                if n["x_written"]:
                    act.wait_ge(sem["x_written"], n["x_written"])
                for t in range(TT):
                    nc.scalar.activation(h[:, t, :], x[:, t, :], ACT.Square, accum_out=ss[:, t:t + 1])\
                        .then_inc(sem["ss_ready"], 1)
                if ph.post is not None:
                    act.dma_start(post_gain[:, :], repeated(ph.post[0], ph.post[1] * D, [1, D])).then_inc(sem["post_landed"], 16)

            def y_square(bank, t, b):
                nc.scalar.activation(proj[:, t, W * b:W * b + W], bank, ACT.Square,
                                     accum_out=ss[:, 2 + 2 * t + b:3 + 2 * t + b]).then_inc(sem["y_sq"], 1)

            def gemm(ph):
                for i, (n0, w, pieces) in enumerate(ph.chunks):
                    split_next()
                    if ph.out == "x":
                        continue
                    if ph.out == "y":
                        act.wait_ge(sem["tile_done"], n["tile_done"] + i + 1)
                        y_square(sum_bank(ph, i, 0), 0, i)
                        act.wait_ge(sem["piece_used"], pieces[-1][0] + 1)
                        y_square(sum_bank(ph, i, 1), 1, i)
                        continue
                    if ph.out == "gated" and i >= 2:
                        continue
                    act.wait_ge(sem["piece_used"], pieces[-1][0] + 1)
                    act.wait_ge(sem["rstd_ready"], n["rstd_ready"])
                    if ph.out == "gated":
                        for t in range(TT):
                            ins = nc.scalar.activation(proj[:, t, n0:n0 + w], sum_bank(ph, i, t), ACT.Sigmoid,
                                                       scale=norm_rstd[:, t:t + 1])
                        ins.then_inc(sem["evac_a"], 1)
                        continue
                    nc.scalar.activation(proj[:, 0, n0:n0 + w], sum_bank(ph, i, 0)[:, 0:w], ACT.Copy,
                                         scale=norm_rstd[:, 0:1]).then_inc(sem["evac_a"], 1)
                    if ph.mix is not None and (ph.mix.kind, i) in between:
                        act.wait_ge(sem["evac_a"], n["evac_a"] + i + 1)
                        act.wait_ge(sem["evac_d"], n["evac_d"] + i + 1)
                        between[ph.mix.kind, i](ph.mix)

            def vectors_out(slabs, turned):
                act.wait_ge(sem["vec_tr"], turned)
                for s in slabs:
                    nc.scalar.activation(vecT[:, s, 0:VEC_ROWS[s]], tr[:, 0, P * s:P * s + VEC_ROWS[s]], ACT.Copy)\
                        .then_inc(sem["vec_evac"], 1)
                act.wait_ge(sem["vec_evac"], slabs[-1] + 1)

            def evac_job(j, dst, scale, base):
                act.wait_ge(sem["pt_ready"], base + j + 1)
                src = tr[0:dst.shape[0], j % 2, 0:dst.shape[1] * S].rearrange("p (a s) -> p a s", s=S)
                nc.scalar.activation(dst, src, ACT.Copy, scale=scale).then_inc(sem["pt_evac"], 1)

            def heads_square(kind, s):
                views, heads, cols, _ = head_set(kind, s)
                act.wait_ge(sem["heads_root"], n["heads_root"] + s)
                for t in range(TT):
                    nc.scalar.activation(shaped_like(head_sq[t], views[t]), views[t], ACT.Square)\
                        .then_inc(sem["heads_sq"], 1)

            def heads_scale(kind, s):
                views, heads, cols, _ = head_set(kind, s)
                act.wait_ge(sem["heads_root"], n["heads_root"] + s + 1)
                for t in range(TT):
                    for j in range(heads):
                        v = views[t][:, j, :] if heads != 4 else views[t][:, j // 2, j % 2, :]
                        ins = nc.scalar.activation(v, v, ACT.Copy, scale=rstd[:, cols[t] + j:cols[t] + j + 1])
                    ins.then_inc(sem["heads_scaled"], 1)

            def nsa_job(jj, j):
                act.wait_ge(sem["pt_ready"], n["pt_ready"] + jj + 1)
                src = tr[:, jj % 2, :].rearrange("p (a s) -> p a s", s=S)
                nc.scalar.activation(jobs_for("nsa")[j][1], src, ACT.Copy).then_inc(sem["pt_evac"], 1)

            def cmp_hi(ph, b):
                if b == 0:
                    act.wait_ge(sem["piece_used"], ph.cmp[1][1] + 1)
                act.wait_ge(sem["x_tap"], n["x_tap"] + 2 - b)
                nc.scalar.activation(aux_hi[:, 0:960], x_tap, ACT.Copy).then_inc(sem["aux_hi"], 1)

            def cmp_out(ph, b):
                act.wait_ge(sem["cmp_tr"], n["cmp_tr"] + 2 - b)
                nc.scalar.activation((c_keyT, c_valueT)[b], up[:, b, HD2:HD2 + 30], ACT.Copy)\
                    .then_inc(sem["cmp_evac"], 1)

            def cmp_raw(ph, b):
                act.wait_ge(sem["piece_used"], ph.cmp[b][1] + 1)
                nc.scalar.activation(c_raw[b], up[0:30, b, 0:HD2], ACT.Copy).then_inc(sem["cmp_raw"], 1)

            def nsa_1(ph):
                nsa_job(0, 7)
                heads_scale("nsa", 0)
                cmp_hi(ph, 1)

            def nsa_2(ph):
                split_next()
                nsa_job(1, 4)
                heads_square("nsa", 1)

            def nsa_3(ph):
                cmp_raw(ph, 1)
                cmp_hi(ph, 0)
                heads_scale("nsa", 1)

            def nsa_5(ph):
                cmp_raw(ph, 0)
                heads_scale("nsa", 2)
                cmp_out(ph, 1)

            def A_0(ph):
                if ph.l == 0:
                    vectors_out((1, 2, 3), 2)
                for t in range(TT):
                    for a, w, dst in ((2048, 256, 12 + t), (2304, P, 14 + t)):
                        at = 256 * t if w == 256 else 512 + P * t
                        nc.scalar.activation(lat_tmp[:, at:at + w], proj[:, t, a:a + w], ACT.Square,
                                             accum_out=ss[:, dst:dst + 1]).then_inc(sem["lat_sq"], 1)

            def A_1(ph):
                for k in range(3):
                    act.wait_ge(sem["aux_tr"], n["aux_tr"] + (1 if k < 2 else 2))
                    g = 96 + 2 * ph.l + k if k < 2 else 100 + ph.l
                    nc.scalar.activation(aux_hi[:, S * k:S * k + S], tr[:, k // 2, S * (k % 2):S * (k % 2) + S],
                                         ACT.Copy, scale=gain_col[:, g:g + 1]).then_inc(sem["aux_hi"], 1)

            def A_2(ph):
                split_next()
                act.wait_ge(sem["piece_used"], ph.uq + 1)
                nc.scalar.activation(proj[:, 0, 2048:2432], up[:, 0, 0:384], ACT.Copy).then_inc(sem["lat_a"], 1)
                act.wait_ge(sem["piece_used"], ph.ukv + 1)
                nc.scalar.activation(proj[:, 0, A_IN:A_IN + W], tr[:, 0, :], ACT.Copy).then_inc(sem["lat_a"], 1)

            def A_3(ph):
                act.wait_ge(sem["lat_a"], n["lat_a"] + 2)
                act.wait_ge(sem["lat_d"], n["lat_d"] + 2)
                for t in range(TT):
                    kv = proj[:, t, A_IN:A_IN + W].rearrange("p (h c) -> p h c", h=ML_H)
                    nc.scalar.activation(kcat[:, t, :, 0:HD], kv[:, :, 0:HD], ACT.Copy).then_inc(sem["kcat_a"], 1)

            def nsa_4(ph):
                split_next()
                heads_square("nsa", 2)

            def sb_turned(j0):
                for j in range(j0, j0 + 4):
                    _, dst, scale = jobs_for("sb")[j]
                    evac_job(j, dst, scale, n["pt_ready"])

            between = {("sb", 2): lambda ph: sb_turned(0), ("sb", 4): lambda ph: sb_turned(4),
                       ("moba", 1): lambda ph: heads_square("moba", 0), ("moba", 2): lambda ph: heads_scale("moba", 0),
                       ("moba", 3): lambda ph: heads_square("moba", 1), ("moba", 4): lambda ph: heads_scale("moba", 1),
                       ("nsa", 0): lambda ph: heads_square("nsa", 0), ("nsa", 1): nsa_1, ("nsa", 2): nsa_2,
                       ("nsa", 3): nsa_3, ("nsa", 4): nsa_4, ("nsa", 5): nsa_5,
                       ("mixA", 0): A_0, ("mixA", 1): A_1, ("mixA", 2): A_2, ("mixA", 3): A_3}

            def unit_pipeline(us, jobs, extra={}):
                with_T = [i for i, u in enumerate(us) if u["pair"] != 0]
                for i in range(len(us) + 3):
                    if i < len(us):
                        u = us[i]
                        act.wait_ge(sem["s_max"], n["s_max"] + i + 1)
                        slot = i % 4
                        for qt in range(TT):
                            c, cols = 2 * slot + qt, score_columns(u, qt)
                            dst = scores_of(slot)[:, cols]
                            src = dst if u["bias"] is not None else up[:, i % 2, cols]
                            nc.scalar.activation(dst, src, ACT.Exp, bias=nmx[:, c:c + 1],
                                                 scale=u["scale"], accum_out=den[:, c:c + 1]).then_inc(sem["p_exp"], 1)
                    if i >= 2 and (i - 2) in with_T:
                        j = with_T.index(i - 2)
                        act.wait_ge(sem["pt_ready"], n["pt_ready"] + jobs + j + 1)
                        if j >= 2:
                            act.wait_ge(sem["o_done"], n["o_done"] + j - 1)
                        width = S + P if us[i - 2]["causal"] else TT * S
                        nc.scalar.activation(probT[:, j % 2, 0:width], tr[:, (jobs + j) % 2, 0:width], ACT.Copy)\
                            .then_inc(sem["pt_evac"], 1)
                    if i in extra:
                        extra[i]()

            def mix_out_hi(ks, n_o):
                act.wait_ge(sem["o_done"], n["o_done"] + n_o)
                for k in ks:
                    nc.scalar.activation(hT_hi[:, k, :], accT[:, k, :], ACT.Copy).then_inc(sem["hT_hi"], 1)

            def mix_A(ph):
                act.wait_ge(sem["lam_ready"], n["lam_ready"] + 1)
                nc.scalar.activation(lam[:, 0:2], lam[:, 2:4], ACT.Exp).then_inc(sem["lam_exp"], 1)
                for j, (_, dst, scale) in enumerate(jobs_for("A")):
                    if j == 2:
                        act.wait_ge(sem["pt_ready"], n["pt_ready"] + j + 1)
                        for a in range(2):
                            ins = nc.scalar.activation(dst[:, a, :], tr[:, j % 2, S * a:S * a + S], ACT.Copy,
                                                       scale=c1("df_scale")[:, a:a + 1])
                        ins.then_inc(sem["pt_evac"], 1)
                    else:
                        evac_job(j, dst, scale, n["pt_ready"])

                def diff_out():
                    act.wait_ge(sem["hT_tr"], n["hT_tr"] + 1)
                    mix_out_hi((2, 3), 8)

                unit_pipeline(units_A(), 10, {8: lambda: mix_out_hi((0, 1), 4), 20: diff_out,
                                              21: lambda: mix_out_hi((4, 5), 12)})
                mix_out_hi((6, 7), 16)

            def mix_nsa(ph):
                for jj in range(2, 6):
                    nsa_job(jj, jj - 2)
                nc.scalar.activation(gates, proj[:, :, 2560:2584], ACT.Sigmoid).then_inc(sem["gate_ready"], 1)
                cmp_out(ph, 0)
                act.wait_ge(sem["pt_ready"], n["pt_ready"] + 7)
                nc.scalar.activation(c_value[0:N_CMP, :], tr[0:N_CMP, 0, 0:2 * HD2], ACT.Copy)\
                    .then_inc(sem["pt_evac"], 1)
                nsa_job(7, 5)
                nsa_job(8, 6)

                def c_exp():
                    act.wait_ge(sem["c_sub"], n["c_sub"] + 1)
                    nc.scalar.activation(c_score, c_score, ACT.Exp, scale=float(HD2) ** -0.5).then_inc(sem["c_exp"], 1)

                def c_turn_out(j):
                    act.wait_ge(sem["c_turned"], n["c_turned"] + j + 1)
                    src = acc[0:N_CMP, 3, :].rearrange("p (a s) -> p a s", s=S)
                    nc.scalar.activation(c_probT[:, j // 2, 2 * (j % 2):2 * (j % 2) + 2, :], src, ACT.Copy)\
                        .then_inc(sem["c_turn_evac"], 1)

                unit_pipeline(units_nsa(), 9, {
                    0: c_exp, 4: lambda: c_turn_out(0), 5: lambda: c_turn_out(1), 6: lambda: c_turn_out(2),
                    7: lambda: c_turn_out(3), 14: lambda: mix_out_hi((0, 1), 10),
                    16: lambda: mix_out_hi((2, 3), 12), 18: lambda: mix_out_hi((4, 5), 14)})
                mix_out_hi((6, 7), 16)

            def mix_moba(ph):
                for j, (_, dst, scale) in enumerate(jobs_for("moba")):
                    evac_job(j, dst, scale, n["pt_ready"])
                unit_pipeline(units_moba(), 8, {6: lambda: mix_out_hi((0, 1), 2), 8: lambda: mix_out_hi((2, 3), 4),
                                                10: lambda: mix_out_hi((4, 5), 6)})
                mix_out_hi((6, 7), 8)

            def mix_sb(ph):
                def exp(heads):
                    for i in heads:
                        act.wait_ge(sem["sb_n"], n["sb_n"] + i + 1)
                        nc.scalar.activation(sb_log[i], sb_log[i], ACT.Exp).then_inc(sem["sb_exp"], 1)

                def log(heads):
                    for i in heads:
                        act.wait_ge(sem["sb_exp"], n["sb_exp"] + i + 1)
                        nc.scalar.activation(sb_log[i], sb_log[i], ACT.Ln, bias=1.0).then_inc(sem["sb_log"], 1)

                def weight(heads):
                    for i in heads:
                        act.wait_ge(sem["sb_diff"], n["sb_diff"] + i + 1)
                        nc.scalar.activation(sb_logit[i], sb_logit[i], ACT.Exp).then_inc(sem["sb_prob"], 1)

                half = H2 // 2
                exp(range(half))
                log(range(half))
                exp(range(half, H2))
                weight(range(half))
                log(range(half, H2))
                mix_out_hi((0, 1), 2)
                weight(range(half, H2))
                for j in (1, 2, 3):
                    mix_out_hi((2 * j, 2 * j + 1), 2 * j + 2)

            def mix_conv(ph):
                for j in range(4):
                    act.wait_ge(sem["pt_ready"], n["pt_ready"] + j + 1)
                    src = tr[:, j % 2, :].rearrange("p (a s) -> p a s", s=S)
                    nc.scalar.activation(u_pad[:, 2 * j:2 * j + 2, TAPS - 1:TAPS - 1 + S], src, ACT.Copy)\
                        .then_inc(sem["pt_evac"], 1)
                for k in range(CONV_PE):
                    act.wait_ge(sem["diag_used"], n["diag_used"] + TAPS * (k + 1))
                    nc.scalar.activation(conv[:, k, :], acc[:, k, 0:S], ACT.Identity, bias=conv_b[:, k:k + 1])\
                        .then_inc(sem["conv_evac"], 1)
                for k in range(KT):
                    act.wait_ge(sem["centred"], n["centred"] + k + 1)
                    nc.scalar.activation(centre_sq[:, k, :], conv[:, k, :], ACT.Square).then_inc(sem["sq_ready"], 1)
                for k in range(KT + 1):
                    if k < KT:
                        act.wait_ge(sem["normed"], n["normed"] + k + 1)
                        nc.scalar.activation(silu[:, k, :], conv[:, k, :], ACT.Silu, scale=conv_g[:, k:k + 1],
                                             bias=conv_beta[:, k:k + 1]).then_inc(sem["silu_ready"], 1)
                    if k >= 1:
                        act.wait_ge(sem["silu_ready"], n["silu_ready"] + k)
                        nc.scalar.activation(hT_hi[:, k - 1, :], silu[:, k - 1, :], ACT.Copy).then_inc(sem["hT_hi"], 1)

            def ffn(ph):
                def used(c):
                    return ph.first + (ph.ups if c == 0 else ph.ups + ph.per * (c - 1) + ph.ups)

                def downs_used(c):
                    return used(c) + ph.downs

                for i, steps in ffn_schedule(ph, act):
                    def pieces_at(offset):
                        at = [ph.first + ph.ups + ph.per * (c - 1) + offset for c in steps]
                        return [plan.pieces[p] for p in at if p < len(plan.pieces)]

                    if steps[0] > 0:
                        for j in range(ph.downs):
                            split_hi(pieces_at(ph.ups + j), i)
                    def next_piece(j):
                        if pieces_at(ph.per + j):
                            split_hi(pieces_at(ph.per + j), i)

                    early = ph.variant == "B" and steps[0] == 0
                    if early:
                        next_piece(0)
                        next_piece(1)
                    if ph.variant == "B":
                        act.wait_ge(sem["piece_used"], along(i, steps, used))
                        for j in range(2):
                            nc.scalar.activation(pairs(ffn_r[:, W * j:W * j + W]), wide_sums[j], ACT.Relu)\
                                .then_inc(sem["r_ready"], 1)
                        if not early:
                            next_piece(0)
                    else:
                        next_piece(0)
                        act.wait_ge(sem["g_ready"], along(i, steps, lambda c: n["g_ready"] + c + 1))
                        nc.scalar.activation(gate_silu, gate_scaled, ACT.Silu).then_inc(sem["r_ready"], 1)
                    if not early:
                        next_piece(1)
                    jobs = ph.kt // 2
                    if steps[0] > 0:
                        act.wait_ge(sem["piece_used"], along(i, steps, downs_used))
                    for j in range(jobs):
                        act.wait_ge(sem["r2_ready"], along(i, steps, lambda c: n["r2_ready"] + jobs * c + j + 1))
                        src = (ffn_product if ph.variant == "A" else ffn_r2)[:, W * j:W * j + W]
                        nc.scalar.activation(aux_hi[:, W * j:W * j + W], src, ACT.Copy).then_inc(sem["act_hi"], 1)
                end = ph.first + ph.ups + ph.per * (ph.n - 1) + ph.downs
                split_at[0] = ph.first + ph.ups + ph.per * (ph.n - 1) + 2
                split_next(end + 2 - split_at[0])
                if ph.variant == "A":
                    for t in range(TT):
                        if t == 0:
                            act.wait_ge(sem["tile_done"], n["tile_done"] + 1)
                        else:
                            act.wait_ge(sem["piece_used"], end)
                        for b in range(2):
                            y_square(acc[:, 2 * t + b, :], t, b)

            vectors_out((0,), 1)
            split_next(1)
            todo = {"norm": norm, "gemm": gemm, "mixA": mix_A, "nsa": mix_nsa, "sb": mix_sb,
                    "conv": mix_conv, "moba": mix_moba, "ffn": ffn}
            for index, ph in enumerate(phases):
                todo[ph.kind](ph)
                if index == 0:
                    split_next(1)
                if ph.kind == "norm" and ph.layer == FIRST_B:
                    act.dma_start(region[:, 0:n_second], A["second"]).then_inc(sem["second_landed"], 16)
                    for dst, src in second_rows:
                        act.dma_start(dst, src).then_inc(sem["second_landed"], 16)
                n.advance(ph)

        @block.vector
        def _(dve):
            n = Tally()
            done = [0]
            split_at = [0]

            def link(ins):
                done[0] += 1
                ins.then_inc(sem["dve_step"], 1)
                dve.wait_ge(sem["dve_step"], done[0])

            def mark(ins):
                done[0] += 1
                ins.then_inc(sem["dve_step"], 1)

            def split_lo(ps_, i=None):
                p0 = ps_[0]
                dve.wait_ge(sem["hi_ready"], along(i, ps_, lambda p: p.index + 1))
                m = p0.floats
                nc.vector.tensor_tensor(w_lo[:, p0.slot, 0:m], raw[:, p0.slot, 0:m], f32(w_hi[:, p0.slot, 0:m]),
                                        ALU.subtract).then_inc(sem["lo_ready"], 1)

            def split_next(k=2):
                for _ in range(k):
                    if split_at[0] < len(plan.pieces):
                        split_lo([plan.pieces[split_at[0]]])
                        split_at[0] += 1

            def root(dst, sums, width, a=None, t=None):
                a, t = newton[:, 0:dst.shape[1]] if a is None else a, sums if t is None else t
                link(nc.vector.tensor_scalar(a, sums, 1.0 / width, EPS, ALU.mult, ALU.add))
                link(nc.vector.tensor_scalar(dst.bitcast(I32), a.bitcast(I32), -0.5, float(0x5f3759df), ALU.mult,
                                             ALU.add))
                link(nc.vector.scalar_tensor_tensor(out=t, in0=dst, scalar=0.375 ** 0.5, in1=dst, op0=ALU.mult,
                                                    op1=ALU.mult))
                link(nc.vector.tensor_tensor(t, t, a, ALU.mult))
                link(nc.vector.scalar_tensor_tensor(out=t, in0=t, scalar=-1.25 / 0.375 ** 0.5, in1=t, op0=ALU.add,
                                                    op1=ALU.mult))
                link(nc.vector.scalar_tensor_tensor(out=dst, in0=t, scalar=1.875, in1=dst, op0=ALU.add, op1=ALU.mult))
                link(nc.vector.scalar_tensor_tensor(out=t, in0=dst, scalar=-0.5, in1=dst, op0=ALU.mult, op1=ALU.mult))
                link(nc.vector.tensor_tensor(t, t, a, ALU.mult))
                return nc.vector.scalar_tensor_tensor(out=dst, in0=t, scalar=1.5, in1=dst, op0=ALU.add, op1=ALU.mult)

            def norm(ph):
                for k in range(KT):
                    dve.wait_ge(sem["hT_hi"], n["hT_hi"] + 2 * (k // 2) + 2)
                    g = gain_col[:, ph.gain + k:ph.gain + k + 1]
                    nc.vector.scalar_tensor_tensor(
                        out=hT_lo[:, k, :], in0=norm_bank(ph, k // 2)[:, S * (k % 2):S * (k % 2) + S], scalar=g,
                        in1=f32(hT_hi[:, k, :]), op0=ALU.mult, op1=ALU.subtract).then_inc(sem["hT_lo"], 1)
                dve.wait_ge(sem["ss_ready"], n["ss_ready"] + TT)
                root(norm_rstd, ss[:, 0:TT], D).then_inc(sem["rstd_ready"], 1)

            def gemm(ph):
                dve.wait_ge(sem["rstd_ready"], n["rstd_ready"])
                for i, (n0, w, pieces) in enumerate(ph.chunks):
                    split_next()
                    if ph.out == "y":
                        for t in range(TT):
                            dve.wait_ge(sem["y_sq"], n["y_sq"] + 2 * i + t + 1)
                            if (i, t) != (len(ph.chunks) - 1, 1):
                                y_gain(ph, sum_bank(ph, i, t), t, i)
                        if i == len(ph.chunks) - 1:
                            add_y(lambda: y_gain(ph, sum_bank(ph, i, 1), 1, i))
                        continue
                    dve.wait_ge(sem["piece_used"], pieces[-1][0] + 1)
                    if ph.out == "gated" and i < 2:
                        continue
                    if ph.out == "gated":
                        dve.wait_ge(sem["evac_a"], n["evac_a"] + i - 1)
                        for t in range(TT):
                            ins = nc.vector.scalar_tensor_tensor(
                                out=proj[:, t, n0:n0 + w], in0=sum_bank(ph, i, t), scalar=norm_rstd[:, t:t + 1],
                                in1=proj[:, t, D + n0:D + n0 + w], op0=ALU.mult, op1=ALU.mult)
                        ins.then_inc(sem["evac_d"], 1)
                        continue
                    if ph.out == "x":
                        for t in range(TT):
                            xt = x[:, t, n0:n0 + w]
                            nc.vector.tensor_tensor(xt, xt, sum_bank(ph, i, t), ALU.add).then_inc(sem["x_written"], 1)
                    else:
                        nc.vector.tensor_scalar(proj[:, 1, n0:n0 + w], sum_bank(ph, i, 1)[:, 0:w], norm_rstd[:, 1:2], None,
                                                ALU.mult).then_inc(sem["evac_d"], 1)
                    if ph.mix is not None and (ph.mix.kind, i) in between:
                        dve.wait_ge(sem["evac_d"], n["evac_d"] + i + 1)
                        between[ph.mix.kind, i](ph.mix)
            def y_gain(ph, bank, t, b):
                dve.wait_ge(sem["post_landed"], 16 * (ph.row + 1))
                c = slice(W * b, W * b + W)
                link(nc.vector.tensor_tensor(h[:, t, c], bank, post_gain[:, c], ALU.mult))

            def add_y(last_gain):
                sums, r = ss[:, 6:8], rstd[:, 0:TT]
                halves = ss[:, 2:6].rearrange("p (t b) -> p t b", b=2)
                link(nc.vector.tensor_tensor(sums, halves[:, :, 0], halves[:, :, 1], ALU.add))
                link(root(r, sums, D))
                for b in range(2):
                    if b == 1:
                        last_gain()
                    for t in range(TT):
                        c = slice(W * b, W * b + W)
                        nc.vector.scalar_tensor_tensor(out=x[:, t, c], in0=h[:, t, c], scalar=r[:, t:t + 1],
                                                       in1=x[:, t, c], op0=ALU.mult, op1=ALU.add)\
                            .then_inc(sem["x_written"], 1)

            def unit_pipeline(us, extra={}):
                for i in range(len(us) + 3):
                    if i < len(us):
                        u, slot = us[i], i % 4
                        dve.wait_ge(sem["s_ready"], n["s_ready"] + i + 1)
                        sc = up[:, i % 2, :]
                        c = slice(2 * slot, 2 * slot + 2)
                        if u["bias"] is not None:
                            for qt in range(TT):
                                cols = score_columns(u, qt)
                                first = score_columns(u, 0).start
                                mark(nc.vector.tensor_tensor_reduce(
                                    scores_of(slot)[:, cols], sc[:, cols],
                                    u["bias"][:, cols.start - first:cols.stop - first], 1.0, LOWEST, ALU.add, ALU.max,
                                    mx[:, 2 * slot + qt:2 * slot + qt + 1]))
                            dve.wait_ge(sem["dve_step"], done[0])
                        else:
                            link(nc.vector.tensor_reduce(mx[:, c], sc.rearrange("p (t s) -> p t s", t=TT), AX_X, ALU.max))
                        nc.vector.tensor_scalar(nmx[:, c], mx[:, c], -u["scale"], None, ALU.mult)\
                            .then_inc(sem["s_max"], 1)
                    if 1 <= i <= len(us):
                        u, slot = us[i - 1], (i - 1) % 4
                        c = slice(2 * slot, 2 * slot + 2)
                        dve.wait_ge(sem["p_exp"], n["p_exp"] + 2 * i)
                        link(nc.vector.reciprocal(rec[:, c], den[:, c]))
                        if u["gate"] is not None:
                            link(nc.vector.tensor_tensor(rec[:, c], rec[:, c], u["gate"], ALU.mult))
                        if u["pair"] == 1:
                            link(nc.vector.tensor_scalar(rec[:, c], rec[:, c], lam[:, 4:5], None, ALU.mult))
                        for qt in range(TT):
                            r = rec[:, 2 * slot + qt:2 * slot + qt + 1]
                            pq = scores_of(slot)[:, score_columns(u, qt)]
                            if u["pair"] == 0:
                                link(nc.vector.tensor_scalar(pq, pq, r, None, ALU.mult))
                            elif u["pair"] == 1:
                                nc.vector.scalar_tensor_tensor(out=pq, in0=pq, scalar=r, in1=prob[:, (i - 2) % 4, qt, :],
                                                               op0=ALU.mult, op1=ALU.add).then_inc(sem["p_norm"], 1)
                            else:
                                nc.vector.tensor_scalar(pq, pq, r, None, ALU.mult).then_inc(sem["p_norm"], 1)

                    if i in extra:
                        extra[i]()

            def mix_out_lo(ks):
                for k in ks:
                    dve.wait_ge(sem["hT_hi"], n["hT_hi"] + 2 * (k // 2) + 2)
                    nc.vector.tensor_tensor(hT_lo[:, k, :], accT[:, k, :], f32(hT_hi[:, k, :]), ALU.subtract)\
                        .then_inc(sem["hT_lo"], 1)

            def sums_of_squares(src, heads, width, dst, tmp):
                link(nc.vector.tensor_tensor(tmp, src, src, ALU.mult))
                return nc.vector.tensor_reduce(dst, tmp, AX_X, ALU.add)

            def A_0(ph):
                dve.wait_ge(sem["lat_sq"], n["lat_sq"] + 4)
                link(root(rstd[:, 12:14], ss[:, 12:14], 256))
                link(root(rstd[:, 14:16], ss[:, 14:16], P))
                dve.wait_ge(sem["evac_a"], n["evac_a"] + 1)
                for t in range(TT):
                    for a, b, r in ((2048, 2304, 12 + t), (2304, 2432, 14 + t)):
                        ins = nc.vector.tensor_scalar(proj[:, t, a:b], proj[:, t, a:b], rstd[:, r:r + 1], None, ALU.mult)
                        if (t, a) != (TT - 1, 2304):
                            link(ins)
                ins.then_inc(sem["prep"], 1)

            def A_1(ph):
                dve.wait_ge(sem["evac_a"], n["evac_a"] + 2)
                for t in range(TT):
                    link(sums_of_squares(gq[t], 6, HD, ss[:, 6 * t:6 * t + 6], gq_t1[t]))
                dve.wait_ge(sem["row_landed"], ROWS_LANDED)
                root(rstd[:, 0:12], ss[:, 0:12], HD).then_inc(sem["gq_root"], 1)
                for k in range(3):
                    dve.wait_ge(sem["aux_hi"], n["aux_hi"] + (2 if k < 2 else 3))
                    g = 96 + 2 * ph.l + k if k < 2 else 100 + ph.l
                    nc.vector.scalar_tensor_tensor(
                        out=aux_lo[:, S * k:S * k + S], in0=tr[:, k // 2, S * (k % 2):S * (k % 2) + S],
                        scalar=gain_col[:, g:g + 1], in1=f32(aux_hi[:, S * k:S * k + S]), op0=ALU.mult,
                        op1=ALU.subtract).then_inc(sem["aux_lo"], 1)

            def A_2(ph):
                split_next()
                dve.wait_ge(sem["piece_used"], ph.uq + 1)
                nc.vector.tensor_copy(proj[:, 1, 2048:2432], up[:, 1, 0:384]).then_inc(sem["lat_d"], 1)
                dve.wait_ge(sem["piece_used"], ph.ukv + 1)
                nc.vector.tensor_copy(proj[:, 1, A_IN:A_IN + W], tr[:, 1, :]).then_inc(sem["lat_d"], 1)

            def A_3(ph):
                lr = lam_rows[:, ph.l, :].rearrange("p (m a c) -> p m a c", m=2, a=2)
                pr = lat_tmp[:, 768:832].rearrange("p (m c) -> p m c", m=2)
                link(nc.vector.tensor_tensor(pr, lr[:, :, 0, :], lr[:, :, 1, :], ALU.mult))
                nc.vector.tensor_reduce(lam[:, 2:4], pr, AX_X, ALU.add).then_inc(sem["lam_ready"], 1)
                dve.wait_ge(sem["na_flip"], n["na_flip"] + 1)
                mask = bc(c1("na_mask").unsqueeze(1), [P, TT, S])
                for hh in range(NA_H):
                    nc.vector.scalar_tensor_tensor(
                        out=na_bias[:, hh, :].rearrange("p (t k) -> p t k", t=TT),
                        in0=flip_bank(hh).rearrange("p (t k) -> p t k", t=TT), scalar=float(HD) ** 0.5, in1=mask,
                        op0=ALU.mult, op1=ALU.add).then_inc(sem["na_ready"], 1)

            def mix_A(ph):
                l = ph.l
                dve.wait_ge(sem["lam_exp"], n["lam_exp"] + 1)
                link(nc.vector.tensor_tensor(lam[:, 5:6], lam[:, 1:2], lam[:, 0:1], ALU.subtract))
                link(nc.vector.tensor_scalar(lam[:, 4:5], lam[:, 5:6], -(0.8 - 0.6 * math.exp(-0.3 * l)), None, ALU.add))
                dve.wait_ge(sem["na_ready"], n["na_ready"] + NA_H)
                od = h[:, 0, 0:512].rearrange("p (a c) -> p a c", c=HD)

                def diff_norm():
                    dve.wait_ge(sem["o_done"], n["o_done"] + 8)
                    tmp = h[:, 0, 512:1024].rearrange("p (a c) -> p a c", c=HD)
                    link(nc.vector.tensor_copy(h[:, 0, 0:512], acc[:, 1, :]))
                    link(sums_of_squares(od, 8, HD, ss[:, 16:24], tmp))
                    link(root(rstd[:, 16:24], ss[:, 16:24], HD))

                def diff_gain():
                    link(nc.vector.tensor_tensor(od, od, bc(rstd[:, 16:24].unsqueeze(2), [P, 8, HD]), ALU.mult))
                    keep = 1.0 - (0.8 - 0.6 * math.exp(-0.3 * l))
                    nc.vector.scalar_tensor_tensor(out=od, in0=od, scalar=keep,
                                                   in1=bc(subln[:, l, :].unsqueeze(1), [P, 8, HD]), op0=ALU.mult,
                                                   op1=ALU.mult).then_inc(sem["od_ready"], 1)

                unit_pipeline(units_A(), {9: lambda: mix_out_lo((0, 1)), 15: diff_norm, 17: diff_gain,
                                          21: lambda: mix_out_lo((2, 3))})
                mix_out_lo((4, 5, 6, 7))

            def heads_root(kind, s):
                views, heads, cols, _ = head_set(kind, s)
                for t in range(TT):
                    dve.wait_ge(sem["heads_sq"], n["heads_sq"] + TT * s + t + 1)
                    sq = head_sq[t][:, 0:heads * HD2].rearrange("p (h c) -> p h c", c=HD2)
                    link(nc.vector.tensor_reduce(ss[:, cols[t]:cols[t] + heads], sq, AX_X, ALU.add))
                a, b = cols[0], cols[1] + heads
                root(rstd[:, a:b], ss[:, a:b], HD2).then_inc(sem["heads_root"], 1)

            def heads_rope(kind, s, t):
                views, heads, cols, gain = head_set(kind, s)
                if s == 0 and t == 0:
                    dve.wait_ge(sem["tab_ready"], n["tab_ready"] + 1)
                dve.wait_ge(sem["heads_scaled"], n["heads_scaled"] + TT * s + t + 1)
                if TT * s + t > 0:
                    dve.wait_ge(sem["prep"], n["prep"] + TT * s + t)
                v = views[t]
                tmp = shaped_like(rope_tmp, v)

                def table(a, b):
                    at = 256 * t
                    if heads == 4:
                        tab = probT[:, :, at + a:at + b].unsqueeze(2)
                        return bc(tab, [P, 2, 2, b - a])
                    return bc(head_tab[gain][:, at + a:at + b].unsqueeze(1), [P, heads, b - a])

                def part(ap, a):
                    return ap[:, :, a:a + 64] if heads != 4 else ap[:, :, :, a:a + 64]

                for a in (0, 64):
                    ins = nc.vector.tensor_tensor(part(tmp, a), part(v, 64 - a), table(128 + a, 192 + a), ALU.mult)
                    link(ins)
                link(nc.vector.tensor_tensor(v, v, table(0, 128), ALU.mult))
                nc.vector.tensor_tensor(v, v, tmp, ALU.add).then_inc(sem["prep"], 1)

            def cmp_taps(b):
                t0 = (8, 14)[b]
                dve.wait_ge(sem["pt_evac"], n["pt_evac"] + 2 - b)
                dve.wait_ge(sem["aux_hi"], n["aux_hi"] + 1 - b)
                src = bass.AP(tiles[:, t0, :].tensor, tiles[:, t0, :].offset,
                              [list(tiles[:, t0, :].ap[0]), [1, CMP_L], [S, GROUPS], [CMP_STRIDE, N_CMP]])
                dst = x_tap.rearrange("p (l g m) -> p l g m", l=CMP_L, g=GROUPS)
                pos = bc(cmp_pos[:, b, :].unsqueeze(2).unsqueeze(3), [P, CMP_L, GROUPS, N_CMP])
                nc.vector.tensor_tensor(dst, src, pos, ALU.add).then_inc(sem["x_tap"], 1)

            def cmp_lo(b):
                dve.wait_ge(sem["x_tap"], n["x_tap"] + 2 - b)
                dve.wait_ge(sem["aux_hi"], n["aux_hi"] + 2 - b)
                nc.vector.tensor_tensor(aux_lo[:, 0:960], x_tap, f32(aux_hi[:, 0:960]), ALU.subtract)\
                    .then_inc(sem["aux_lo"], 1)

            def nsa_1(ph):
                cmp_taps(1)
                for t in range(TT):
                    heads_rope("nsa", 0, t)
                cmp_lo(1)

            def nsa_2(ph):
                split_next()
                cmp_taps(0)
                heads_root("nsa", 1)

            def nsa_3(ph):
                cmp_lo(0)
                heads_rope("nsa", 1, 0)

            def nsa_4(ph):
                split_next()
                heads_rope("nsa", 1, 1)
                heads_root("nsa", 2)

            def nsa_5(ph):
                for t in range(TT):
                    heads_rope("nsa", 2, t)

            def moba_3(ph):
                heads_rope("moba", 0, 1)
                heads_root("moba", 1)

            between = {("moba", 1): lambda ph: heads_root("moba", 0), ("moba", 2): lambda ph: heads_rope("moba", 0, 0),
                       ("moba", 3): moba_3, ("moba", 4): lambda ph: heads_rope("moba", 1, 0),
                       ("moba", 5): lambda ph: heads_rope("moba", 1, 1),
                       ("nsa", 0): lambda ph: heads_root("nsa", 0), ("nsa", 1): nsa_1, ("nsa", 2): nsa_2,
                       ("nsa", 3): nsa_3, ("nsa", 4): nsa_4, ("nsa", 5): nsa_5,
                       ("mixA", 0): A_0, ("mixA", 1): A_1, ("mixA", 2): A_2, ("mixA", 3): A_3}

            def mix_nsa(ph):
                dve.wait_ge(sem["prep"], n["prep"] + 6)
                dve.wait_ge(sem["c_ready"], n["c_ready"] + 1)
                src = acc[:, 3, 0:256].rearrange("p (t h m) -> p t h m", t=TT, h=H2)[:, :, :, 0:N_CMP]
                c4 = h[:, 1, 0:240].rearrange("p (t h m) -> p t h m", t=TT, h=H2)
                mask = bc(c2("cmp_mask").rearrange("p (t m) -> p t m", t=TT).unsqueeze(2), [P, TT, H2, N_CMP])
                link(nc.vector.tensor_tensor(c4, src, mask, ALU.add))
                link(nc.vector.tensor_reduce(c_max, c_score, AX_X, ALU.max))
                nc.vector.tensor_tensor(c_score, c_score, bc(c_max.unsqueeze(2), [P, 16, N_CMP]), ALU.subtract)\
                    .then_inc(sem["c_sub"], 1)
                dve.wait_ge(sem["gate_ready"], n["gate_ready"] + 1)

                def c_norm():
                    dve.wait_ge(sem["c_exp"], n["c_exp"] + 1)
                    link(nc.vector.tensor_reduce(c_max, c_score, AX_X, ALU.add))
                    link(nc.vector.reciprocal(c_rec, c_max))
                    r3 = c_rec.rearrange("p (t h) -> p t h", t=TT)
                    link(nc.vector.tensor_tensor(r3, r3, gates[:, :, 0:8], ALU.mult))
                    link(nc.vector.tensor_tensor(r3, r3, bc(c2("cmp_any").unsqueeze(2), [P, TT, H2]), ALU.mult))
                    nc.vector.tensor_tensor(c_score, c_score, bc(c_rec.unsqueeze(2), [P, 16, N_CMP]), ALU.mult)\
                        .then_inc(sem["c_prob"], 1)

                unit_pipeline(units_nsa(), {2: c_norm, 15: lambda: mix_out_lo((0, 1)), 17: lambda: mix_out_lo((2, 3))})
                mix_out_lo((4, 5, 6, 7))

            def mix_moba(ph):
                unit_pipeline(units_moba(), {7: lambda: mix_out_lo((0, 1)), 9: lambda: mix_out_lo((2, 3))})
                mix_out_lo((4, 5, 6, 7))

            def mix_sb(ph):
                dve.wait_ge(sem["second_landed"], SECOND_LANDED)
                for i in range(H2):
                    dve.wait_ge(sem["s_ready"], n["s_ready"] + i + 1)
                    nc.vector.tensor_tensor(sb_logit[i], up[:, i % 2, 0:SEEN], c2("before"), ALU.add)\
                        .then_inc(sem["sb_z"], 1)
                    dve.wait_ge(sem["sb_z"], n["sb_z"] + i + 1)
                    nc.vector.scalar_tensor_tensor(out=sb_log[i], in0=sb_logit[i], scalar=-1.0, in1=sb_logit[i],
                                                   op0=ALU.mult, op1=ALU.min).then_inc(sem["sb_n"], 1)
                half = H2 // 2
                for heads in (range(half), range(half, H2)):
                    for i in heads:
                        dve.wait_ge(sem["sb_log"], n["sb_log"] + i + 1)
                        nc.vector.scalar_tensor_tensor(out=sb_log[i], in0=sb_logit[i], scalar=0.0, in1=sb_log[i],
                                                       op0=ALU.max, op1=ALU.add).then_inc(sem["sb_sp"], 1)
                    for i in heads:
                        dve.wait_ge(sem["sb_sum"], n["sb_sum"] + i + 1)
                        nc.vector.tensor_tensor(sb_logit[i], sb_logit[i], tr[:, i % 2, 0:SEEN], ALU.subtract)\
                            .then_inc(sem["sb_diff"], 1)
                mix_out_lo(range(KT))

            def mix_conv(ph):
                dve.wait_ge(sem["pad_ready"], n["pad_ready"])
                dve.wait_ge(sem["pt_evac"], n["pt_evac"] + 4)
                first, mine = done[0], KT - CONV_PE
                for j in range(TAPS):
                    for k in range(CONV_PE, KT):
                        src = u_pad[:, k, j:j + S]
                        if j == 0:
                            ins = nc.vector.tensor_scalar(conv[:, k, :], src, tap(0, k), conv_b[:, k:k + 1], ALU.mult,
                                                          ALU.add)
                        else:
                            dve.wait_ge(sem["dve_step"], first + mine * (j - 1) + k - CONV_PE + 1)
                            ins = nc.vector.scalar_tensor_tensor(out=conv[:, k, :], in0=src, scalar=tap(j, k),
                                                                 in1=conv[:, k, :], op0=ALU.mult, op1=ALU.add)
                        if (j, k) == (TAPS - 1, KT - 1):
                            ins.then_inc(sem["conv_done"], 1)
                        else:
                            ins.then_inc(sem["dve_step"], 1)
                            done[0] += 1
                dve.wait_ge(sem["mean_ready"], n["mean_ready"] + 1)
                link(nc.vector.tensor_scalar(mean_b, up[:, 0, 0:S], 1.0 / D, None, ALU.mult))
                for k in range(KT):
                    nc.vector.tensor_tensor(conv[:, k, :], conv[:, k, :], mean_b, ALU.subtract)\
                        .then_inc(sem["centred"], 1)
                dve.wait_ge(sem["var_ready"], n["var_ready"] + 1)
                step_b, t_b = (proj[:, 0, 2560 + S * j:2560 + S * j + S] for j in range(2))
                link(root(rstd_b, up[:, 1, 0:S], D, step_b, t_b))
                for k in range(KT):
                    nc.vector.tensor_tensor(conv[:, k, :], conv[:, k, :], rstd_b, ALU.mult).then_inc(sem["normed"], 1)
                for k in range(KT):
                    dve.wait_ge(sem["hT_hi"], n["hT_hi"] + k + 1)
                    nc.vector.tensor_tensor(hT_lo[:, k, :], silu[:, k, :], f32(hT_hi[:, k, :]), ALU.subtract)\
                        .then_inc(sem["hT_lo"], 1)

            def ffn(ph):
                def used(c):
                    return ph.first + (ph.ups if c == 0 else ph.ups + ph.per * (c - 1) + ph.ups)

                dve.wait_ge(sem["rstd_ready"], n["rstd_ready"])
                if ph.variant == "A":
                    for t in range(TT):
                        ins = nc.vector.tensor_scalar(rstd_diag[:, P * t:P * t + P], ident, norm_rstd[:, t:t + 1], None,
                                                      ALU.mult)
                    ins.then_inc(sem["diag_ready"], 1)
                else:
                    link(nc.vector.tensor_tensor(rstd_sq, norm_rstd, norm_rstd, ALU.mult))
                for i, steps in ffn_schedule(ph, dve):
                    def pieces_at(offset):
                        at = [ph.first + ph.ups + ph.per * (c - 1) + offset for c in steps]
                        return [plan.pieces[p] for p in at if p < len(plan.pieces)]

                    if steps[0] > 0:
                        for j in range(ph.downs):
                            split_lo(pieces_at(ph.ups + j), i)
                    def next_piece(j):
                        if pieces_at(ph.per + j):
                            split_lo(pieces_at(ph.per + j), i)

                    if ph.variant == "B":
                        next_piece(0)
                    if ph.variant == "A":
                        if steps[0] == 0:
                            next_piece(0)
                            dve.wait_ge(sem["rows_done"], n["rows_done"] + 1)
                            link(nc.vector.tensor_copy(rstd_rows, acc[:, 3, 0:S]))
                        dve.wait_ge(sem["piece_used"], along(i, steps, used))
                        if steps[0] > 0:
                            dve.wait_ge(sem["r2_ready"], along(i, steps, lambda c: n["r2_ready"] + c))
                            dve.wait_ge(sem["act_lo"], along(i, steps, lambda c: n["act_lo"] + c))
                        factors = bc(rstd_rows.unsqueeze(1), [P, 2, S])
                        nc.vector.tensor_tensor(pairs(gate_scaled), wide_sums[0], factors, ALU.mult)\
                            .then_inc(sem["g_ready"], 1)
                        nc.vector.tensor_tensor(pairs(up_scaled), wide_sums[1], factors, ALU.mult)\
                            .then_inc(sem["u_ready"], 1)
                        if steps[0] > 0:
                            next_piece(0)
                        dve.wait_ge(sem["u_ready"], along(i, steps, lambda c: n["u_ready"] + c + 1))
                        dve.wait_ge(sem["r_ready"], along(i, steps, lambda c: n["r_ready"] + c + 1))
                        nc.vector.tensor_tensor(ffn_product, gate_silu, up_scaled, ALU.mult).then_inc(sem["r2_ready"], 1)
                    next_piece(1)
                    jobs = ph.kt // 2
                    for j in range(jobs):
                        dve.wait_ge(sem["act_hi"], along(i, steps, lambda c: n["act_hi"] + jobs * c + j + 1))
                        src = (ffn_product if ph.variant == "A" else ffn_r2)[:, W * j:W * j + W]
                        nc.vector.tensor_tensor(aux_lo[:, W * j:W * j + W], src, f32(aux_hi[:, W * j:W * j + W]),
                                                ALU.subtract).then_inc(sem["act_lo"], 1)
                split_at[0] = ph.first + ph.ups + ph.per * (ph.n - 1) + 2
                end = ph.first + ph.ups + ph.per * (ph.n - 1) + ph.downs
                split_next(end + 2 - split_at[0])
                if ph.variant == "A":
                    for t in range(TT):
                        for b in range(2):
                            dve.wait_ge(sem["y_sq"], n["y_sq"] + 2 * t + b + 1)
                            if (t, b) != (1, 1):
                                y_gain(ph, acc[:, 2 * t + b, :], t, b)
                    add_y(lambda: y_gain(ph, acc[:, 3, :], 1, 1))
                else:
                    for b in range(2):
                        dve.wait_ge(sem["piece_used"], end - 1 + b)
                        for t in range(TT):
                            xt = x[:, t, W * b:W * b + W]
                            nc.vector.scalar_tensor_tensor(out=xt, in0=acc[:, 2 * t + b, :], scalar=rstd_sq[:, t:t + 1],
                                                           in1=xt, op0=ALU.mult, op1=ALU.add)\
                                .then_inc(sem["x_written"], 1)

            split_next(1)
            todo = {"norm": norm, "gemm": gemm, "mixA": mix_A, "nsa": mix_nsa, "sb": mix_sb,
                    "conv": mix_conv, "moba": mix_moba, "ffn": ffn}
            for index, ph in enumerate(phases):
                todo[ph.kind](ph)
                if index == 0:
                    split_next(1)
                n.advance(ph)

        @block.tensor
        def _(pe):
            n = Tally()

            def three(dst, hi, lo, whi, wlo, first, last):
                nc.tensor.matmul(dst, hi, whi, start=first, stop=False)
                nc.tensor.matmul(dst, hi, wlo, start=False, stop=False)
                return nc.tensor.matmul(dst, lo, whi, start=False, stop=last)

            def norm(ph):
                for j in range(KT // 2):
                    if n["x_written"]:
                        pe.wait_ge(sem["x_written"], n["x_written"] - 4 + (2 if j < 2 else 4))
                    else:
                        pe.wait_ge(sem["x_landed"], 16)
                        pe.wait_ge(sem["vec_evac"], 1)
                    for k in range(2):
                        for t in range(TT):
                            c = P * (2 * j + k)
                            last = nc.tensor.transpose(norm_bank(ph, j)[:, S * k + P * t:S * k + P * t + P], x[:, t, c:c + P],
                                                       ident)
                    last.then_inc(sem["hT_tr"], 1)

            def gemm(ph):
                place = {k: j for j, k in enumerate(ph.order or range(KT))}
                for i, (n0, w, pieces) in enumerate(ph.chunks):
                    if i >= 2:
                        if ph.out == "gated":
                            pe.wait_ge(sem["evac_a"], n["evac_a"] + i - 1)
                        if ph.out == "proj":
                            pe.wait_ge(sem["evac_a"], n["evac_a"] + i - 1)
                            pe.wait_ge(sem["evac_d"], n["evac_d"] + i - 1)
                    for p, k0, kt in pieces:
                        slot = plan.pieces[p].slot
                        pe.wait_ge(sem["lo_ready"], p + 1)
                        whi, wlo = piece_view(w_hi, slot, 0, kt, w), piece_view(w_lo, slot, 0, kt, w)
                        for t in range(TT):
                            for k in range(kt):
                                kk = k0 + k
                                if i == 0 and t == 0:
                                    pe.wait_ge(sem["hT_lo"], n["hT_lo"] - KT + place[kk] + 1)
                                last = three(sum_bank(ph, i, t)[:, 0:w], hT_hi[:, kk, P * t:P * t + P],
                                             hT_lo[:, kk, P * t:P * t + P], whi[:, k, :], wlo[:, k, :],
                                             kk == 0, kk == KT - 1)
                            if ph.out == "y" and t == 0 and p == pieces[-1][0]:
                                last.then_inc(sem["tile_done"], 1)
                        last.then_inc(sem["piece_used"], 1)
                    if ph.mix is not None and (ph.mix.kind, i) in between:
                        between[ph.mix.kind, i](ph.mix)
            def job(j, src, base):
                if j >= 2:
                    pe.wait_ge(sem["pt_evac"], base + j - 1)
                for b, ap in enumerate(src):
                    last = nc.tensor.transpose(tr[0:ap.shape[1], j % 2, P * b:P * b + P], ap, ident)
                last.then_inc(sem["pt_ready"], 1)

            def cmp_product(ph, b):
                pe.wait_ge(sem["aux_lo"], n["aux_lo"] + 2 - b)
                for half in range(2):
                    p = ph.cmp[b][half]
                    slot = plan.pieces[p].slot
                    pe.wait_ge(sem["lo_ready"], p + 1)
                    whi, wlo = piece_view(w_hi, slot, 0, 16, P), piece_view(w_lo, slot, 0, 16, P)
                    for l in range(16):
                        c = 30 * (16 * half + l)
                        last = three(up[0:30, b, 0:HD2], aux_hi[:, c:c + 30], aux_lo[:, c:c + 30], whi[:, l, :],
                                     wlo[:, l, :], (half, l) == (0, 0), (half, l) == (1, 15))
                    last.then_inc(sem["piece_used"], 1)

            def nsa_1(ph):
                pe.wait_ge(sem["evac_a"], n["evac_a"] + 1)
                pe.wait_ge(sem["evac_d"], n["evac_d"] + 1)
                job(0, jobs_for("nsa")[7][0], n["pt_evac"])

            def cmp_turn(b):
                pe.wait_ge(sem["cmp_raw"], n["cmp_raw"] + 2 - b)
                nc.tensor.transpose(up[:, b, HD2:HD2 + 30], c_raw[b], ident[0:30, 0:30]).then_inc(sem["cmp_tr"], 1)

            def nsa_2(ph):
                pe.wait_ge(sem["prep"], n["prep"] + 2)
                job(1, jobs_for("nsa")[4][0], n["pt_evac"])
                cmp_product(ph, 1)

            def turn_vectors(slabs, landed, count):
                pe.wait_ge(sem[landed], count)
                for s in slabs:
                    w = VEC_ROWS[s]
                    last = nc.tensor.transpose(tr[:, 0, P * s:P * s + w], vec_rows[s][0:w, :], ident[0:w, 0:w])
                last.then_inc(sem["vec_tr"], 1)

            def nsa_4(ph):
                cmp_turn(1)
                cmp_product(ph, 0)

            def A_0(ph):
                if ph.l == 0:
                    turn_vectors((1, 2, 3), "vec_later_landed", 16 * 6)

            def A_1(ph):
                if ph.l == 0:
                    pe.wait_ge(sem["vec_evac"], 4)
                pe.wait_ge(sem["prep"], n["prep"] + 1)
                for k in range(3):
                    for t in range(TT):
                        c = 2048 + P * k
                        last = nc.tensor.transpose(tr[:, k // 2, S * (k % 2) + P * t:S * (k % 2) + P * t + P],
                                                   proj[:, t, c:c + P], ident)
                    if k:
                        last.then_inc(sem["aux_tr"], 1)

            def A_2(ph):
                pe.wait_ge(sem["aux_lo"], n["aux_lo"] + 3)
                for p, ks, w, bank in ((ph.uq, (0, 1), 384, up), (ph.ukv, (2,), W, tr)):
                    slot = plan.pieces[p].slot
                    pe.wait_ge(sem["lo_ready"], p + 1)
                    whi, wlo = piece_view(w_hi, slot, 0, len(ks), w), piece_view(w_lo, slot, 0, len(ks), w)
                    for t in range(TT):
                        for i, k in enumerate(ks):
                            c = S * k + P * t
                            last = three(bank[:, t, 0:w], aux_hi[:, c:c + P], aux_lo[:, c:c + P], whi[:, i, :],
                                         wlo[:, i, :], i == 0, i == len(ks) - 1)
                    last.then_inc(sem["piece_used"], 1)

            def A_3(ph):
                pe.wait_ge(sem["lat_a"], n["lat_a"] + 2)
                pe.wait_ge(sem["lat_d"], n["lat_d"] + 2)
                pe.wait_ge(sem["na_landed"], 16 * NA_H * (S // GRID) * (ph.l + 1))
                pe.wait_ge(sem["row_landed"], ROWS_LANDED)
                for hh in range(NA_H):
                    last = nc.tensor.matmul(flip_bank(hh), c1("flip"), na_raw[:, hh, :], start=True, stop=True)
                last.then_inc(sem["na_flip"], 1)

            def sb_turn(j0):
                pe.wait_ge(sem["evac_a"], n["evac_a"] + j0 // 2 + 2)
                pe.wait_ge(sem["evac_d"], n["evac_d"] + j0 // 2 + 2)
                for j in range(j0, j0 + 4):
                    job(j, jobs_for("sb")[j][0], n["pt_evac"])

            between = {("sb", 2): lambda ph: sb_turn(0), ("sb", 4): lambda ph: sb_turn(4),
                       ("nsa", 1): nsa_1, ("nsa", 2): nsa_2, ("nsa", 4): nsa_4,
                       ("mixA", 0): A_0, ("mixA", 1): A_1, ("mixA", 2): A_2, ("mixA", 3): A_3}

            def unit_pipeline(us, jobs, extra={}):
                with_T = [i for i, u in enumerate(us) if u["pair"] != 0]
                for i in range(len(us) + 3):
                    if i < len(us):
                        u = us[i]
                        if i >= 2 and us[i - 2]["bias"] is not None:
                            pe.wait_ge(sem["s_max"], n["s_max"] + i - 1)
                        elif i >= 2:
                            pe.wait_ge(sem["p_exp"], n["p_exp"] + 2 * (i - 1))
                        for qt in range(TT):
                            cols = score_columns(u, qt)
                            last = nc.tensor.matmul(up[:, i % 2, cols], u["q"][:, P * qt:P * qt + P],
                                                    u["k"][:, 0:cols.stop - cols.start], start=True, stop=True)
                        last.then_inc(sem["s_ready"], 1)
                    if i >= 2 and (i - 2) in with_T:
                        j = with_T.index(i - 2)
                        pe.wait_ge(sem["p_norm"], n["p_norm"] + 2 * (j + 1))
                        if jobs + j >= 2:
                            pe.wait_ge(sem["pt_evac"], n["pt_evac"] + jobs + j - 1)
                        for kt in range(TT):
                            for qt in range(TT):
                                at, first = S * kt + P * qt, score_columns(us[i - 2], qt).start
                                if us[i - 2]["causal"] and kt > 0:
                                    if qt < kt:
                                        continue
                                    at = S
                                last = nc.tensor.transpose(
                                    tr[:, (jobs + j) % 2, at:at + P],
                                    scores_of((i - 2) % 4)[:, first + P * kt:first + P * kt + P], ident)
                        last.then_inc(sem["pt_ready"], 1)
                    if i >= 3 and (i - 3) in with_T:
                        j = with_T.index(i - 3)
                        u = us[i - 3]
                        pe.wait_ge(sem["pt_evac"], n["pt_evac"] + jobs + j + 1)
                        pT = probT[:, j % 2, :].rearrange("p (k s) -> p k s", k=TT)

                        def operand(o):
                            if isinstance(o, tuple) and o[0] == "columns":
                                return probT[:, j % 2, o[1]:o[2]]
                            if isinstance(o, tuple):
                                return pT[:, o[1], :] if o[0] == "probT" else pT[:, o[1], P * o[2]:P * o[2] + P]
                            return o
                        for m, (dst, lhs, rhs) in enumerate(u["outs"]):
                            if u["pair"] == "halves":
                                start, stop = m < 2, m != 1
                            elif u["pair"] == 1:
                                start, stop = m % TT == 0, m % TT == TT - 1
                            else:
                                start = m == 0 and u["pair"] not in ("inner", "close")
                                stop = m == len(u["outs"]) - 1 and u["pair"] not in ("open", "inner")
                            last = nc.tensor.matmul(dst, operand(lhs), operand(rhs), start=start, stop=stop)
                        last.then_inc(sem["o_done"], 1)
                    if i in extra:
                        extra[i]()

            def mix_A(ph):
                pe.wait_ge(sem["evac_a"], n["evac_a"])
                pe.wait_ge(sem["evac_d"], n["evac_d"])
                pe.wait_ge(sem["na_ready"], n["na_ready"] + NA_H)
                for j, (src, _, _) in enumerate(jobs_for("A")):
                    if j == 4:
                        pe.wait_ge(sem["gq_prep"], n["gq_prep"] + 1)
                    if j == 6:
                        pe.wait_ge(sem["ml_prep"], n["ml_prep"] + 1)
                        pe.wait_ge(sem["kcat_a"], n["kcat_a"] + 2)
                    job(j, src, n["pt_evac"])
                pe.wait_ge(sem["pt_evac"], n["pt_evac"] + 10)

                def diff_turn():
                    pe.wait_ge(sem["od_ready"], n["od_ready"] + 1)
                    for k in range(2):
                        for t in range(TT):
                            last = nc.tensor.transpose(accT[:, 2 + k, P * t:P * t + P],
                                                       h[:, 0, 256 * t + P * k:256 * t + P * k + P], ident)
                    last.then_inc(sem["hT_tr"], 1)

                unit_pipeline(units_A(), 10, {19: diff_turn})

            def mix_nsa(ph):
                jobs = jobs_for("nsa")
                pe.wait_ge(sem["prep"], n["prep"] + 4)
                for jj in range(2, 6):
                    job(jj, jobs[jj - 2][0], n["pt_evac"])
                cmp_turn(0)
                pe.wait_ge(sem["cmp_evac"], n["cmp_evac"] + 2)
                pe.wait_ge(sem["pt_evac"], n["pt_evac"] + 5)
                for g in range(GROUPS):
                    last = nc.tensor.transpose(tr[0:N_CMP, 0, HD2 * g:HD2 * g + HD2],
                                               c_valueT[:, N_CMP * g:N_CMP * g + N_CMP], ident)
                last.then_inc(sem["pt_ready"], 1)
                pe.wait_ge(sem["evac_a"], n["evac_a"])
                pe.wait_ge(sem["evac_d"], n["evac_d"])
                pe.wait_ge(sem["pt_evac"], n["pt_evac"] + 6)
                for t in range(TT):
                    for hh in range(H2):
                        c = 128 * t + 16 * hh
                        g = hh // 4
                        last = nc.tensor.matmul(acc[:, 3, c:c + N_CMP], tiles[:, hh, P * t:P * t + P],
                                                c_keyT[:, N_CMP * g:N_CMP * g + N_CMP], start=True, stop=True)
                last.then_inc(sem["c_ready"], 1)
                pe.wait_ge(sem["prep"], n["prep"] + 6)
                job(7, jobs[5][0], n["pt_evac"])
                job(8, jobs[6][0], n["pt_evac"])
                pe.wait_ge(sem["pt_evac"], n["pt_evac"] + 9)
                def c_turn(j):
                    pe.wait_ge(sem["c_prob"], n["c_prob"] + 1)
                    if j >= 1:
                        pe.wait_ge(sem["c_turn_evac"], n["c_turn_evac"] + j)
                    for i in range(2):
                        for t in range(TT):
                            c = P * (2 * i + t)
                            last = nc.tensor.transpose(acc[0:N_CMP, 3, c:c + P], c_score[:, 8 * t + 2 * j + i, :], ident)
                    last.then_inc(sem["c_turned"], 1)

                def c_close():
                    pe.wait_ge(sem["c_turn_evac"], n["c_turn_evac"] + 4)
                    for hh in range(0, H2, 2):
                        nc.tensor.matmul(accT[:, hh, :], *c_share(hh), start=False, stop=True)

                unit_pipeline(units_nsa(), 9, {4: lambda: c_turn(0), 5: lambda: c_turn(1), 6: lambda: c_turn(2),
                                               7: lambda: c_turn(3), 10: c_close})

            def mix_moba(ph):
                for j, (src, _, _) in enumerate(jobs_for("moba")):
                    pe.wait_ge(sem["prep"], n["prep"] + (2 if j < 4 else 4))
                    job(j, src, n["pt_evac"])
                pe.wait_ge(sem["pt_evac"], n["pt_evac"] + 8)
                unit_pipeline(units_moba(), 8)

            def mix_sb(ph):
                pe.wait_ge(sem["pt_evac"], n["pt_evac"] + 8)
                for i in range(H2):
                    if i >= 2:
                        pe.wait_ge(sem["sb_z"], n["sb_z"] + i - 1)
                    q, k = tiles[:, i, :], tiles[:, H2 + i, :]
                    nc.tensor.matmul(up[:, i % 2, 0:S], k[:, 0:P], q, start=True, stop=True)
                    nc.tensor.matmul(up[:, i % 2, S:SEEN], k[:, P:S], q[:, P:S], start=True, stop=True)\
                        .then_inc(sem["s_ready"], 1)
                pe.wait_ge(sem["evac_a"], n["evac_a"])
                pe.wait_ge(sem["evac_d"], n["evac_d"])
                pe.wait_ge(sem["second_landed"], SECOND_LANDED)
                half = H2 // 2
                for heads in (range(half), range(half, H2)):
                    for i in heads:
                        pe.wait_ge(sem["sb_sp"], n["sb_sp"] + i + 1)
                        if i >= 2:
                            pe.wait_ge(sem["sb_diff"], n["sb_diff"] + i - 1)
                        sums, a = tr[:, i % 2, :], sb_log[i]
                        nc.tensor.matmul(sums[:, 0:P], c2("later"), a[:, 0:P], start=True, stop=True)
                        nc.tensor.matmul(sums[:, P:S], c2("later"), a[:, P:S], start=True, stop=False)
                        nc.tensor.matmul(sums[:, P:S], cb("ones"), a[:, S:SEEN], start=False, stop=True)
                        nc.tensor.matmul(sums[:, S:SEEN], c2("later"), a[:, S:SEEN], start=True, stop=True)\
                            .then_inc(sem["sb_sum"], 1)
                    for i in heads:
                        pe.wait_ge(sem["sb_prob"], n["sb_prob"] + i + 1)
                        v = [proj[:, st, 2 * D + HD2 * i:2 * D + HD2 * i + HD2] for st in range(TT)]
                        nc.tensor.matmul(accT[:, i, 0:P], v[0], sb_logit[i][:, 0:P], start=True, stop=True)
                        nc.tensor.matmul(accT[:, i, P:S], v[0], sb_logit[i][:, P:S], start=True, stop=False)
                        nc.tensor.matmul(accT[:, i, P:S], v[1], sb_logit[i][:, S:SEEN], start=False, stop=True)\
                            .then_inc(sem["o_done"], 1)

            def mix_conv(ph):
                for j in range(4):
                    pe.wait_ge(sem["evac_d"], n["evac_d"] - 1 + j // 2)
                    job(j, [proj[:, t, P * (2 * j + i):P * (2 * j + i) + P] for i in range(2) for t in range(TT)],
                        n["pt_evac"])
                pe.wait_ge(sem["pad_ready"], n["pad_ready"])
                for k in range(CONV_PE):
                    pe.wait_ge(sem["pt_evac"], n["pt_evac"] + k // 2 + 1)
                    for j in range(TAPS):
                        i = TAPS * k + j
                        pe.wait_ge(sem["diag_ready"], n["diag_ready"] + i + 1)
                        last = nc.tensor.matmul(acc[:, k, 0:S], diags[i % len(diags)], u_pad[:, k, j:j + S],
                                                start=j == 0, stop=j == TAPS - 1)
                        last.then_inc(sem["diag_used"], 1)
                pe.wait_ge(sem["second_landed"], SECOND_LANDED)
                for k in range(KT):
                    if k < CONV_PE:
                        pe.wait_ge(sem["conv_evac"], n["conv_evac"] + k + 1)
                    else:
                        pe.wait_ge(sem["conv_done"], n["conv_done"] + 1)
                    last = nc.tensor.matmul(up[:, 0, 0:S], cb("ones"), conv[:, k, :], start=k == 0, stop=k == KT - 1)
                last.then_inc(sem["mean_ready"], 1)
                for k in range(KT):
                    pe.wait_ge(sem["sq_ready"], n["sq_ready"] + k + 1)
                    last = nc.tensor.matmul(up[:, 1, 0:S], cb("ones"), centre_sq[:, k, :], start=k == 0, stop=k == KT - 1)
                last.then_inc(sem["var_ready"], 1)

            def ffn(ph):
                jobs = ph.kt // 2

                def hidden(i, steps):
                    for j in range(ph.ups):
                        ps_ = [plan.pieces[ph.first + j if c == 0 else ph.first + ph.ups + ph.per * (c - 1) + j]
                               for c in steps]
                        slot = ps_[0].slot
                        pe.wait_ge(sem["lo_ready"], along(i, ps_, lambda p: p.index + 1))
                        if j == 0 and steps[0] > 0:
                            if ph.variant == "B":
                                pe.wait_ge(sem["r_ready"], along(i, steps, lambda c: n["r_ready"] + 2 * c))
                            else:
                                pe.wait_ge(sem["g_ready"], along(i, steps, lambda c: n["g_ready"] + c))
                                pe.wait_ge(sem["u_ready"], along(i, steps, lambda c: n["u_ready"] + c))
                        for a in range(4):
                            if ph.variant == "A" and steps[0] == 0 and (j, a) == (1, 2):
                                pe.wait_ge(sem["diag_ready"], n["diag_ready"] + 1)
                                nc.tensor.matmul(acc[:, 3, 0:S], cb("ones"), rstd_diag, start=True, stop=True)\
                                    .then_inc(sem["rows_done"], 1)
                            for k in range(PK):
                                kk = PK * j + k
                                if steps[0] == 0 and a == 0:
                                    pe.wait_ge(sem["hT_lo"], n["hT_lo"] - KT + kk + 1)
                                if ph.variant == "B":
                                    at = W * k + P * a
                                else:
                                    at = PK * CH_A * (a // 2) + CH_A * k + P * (a % 2)
                                last = three(hidden_sums[a], w_hi[:, slot, at:at + P], w_lo[:, slot, at:at + P],
                                             hT_hi[:, kk, :], hT_lo[:, kk, :], kk == 0, kk == KT - 1)
                        last.then_inc(sem["piece_used"], 1)

                def down(i, steps, first, final):
                    for j in range(ph.downs):
                        ps_ = [plan.pieces[ph.first + ph.ups + ph.per * (c - 1) + (ph.ups if c < ph.n else 0) + j]
                               for c in steps]
                        slot = ps_[0].slot
                        pe.wait_ge(sem["lo_ready"], along(i, ps_, lambda p: p.index + 1))
                        for t in range(TT):
                            for k in range(ph.kt):
                                c = S * k + P * t
                                if (j, t, k % 2) == (0, 0, 0):
                                    pe.wait_ge(sem["act_lo"],
                                               along(i, steps, lambda c: n["act_lo"] + jobs * (c - 1) + k // 2 + 1))
                                for b in ((0, 1) if ph.downs == 1 else (j,)):
                                    a = D * k + W * b if ph.downs == 1 else W * k
                                    last = three(acc[:, 2 * t + b, :], aux_hi[:, c:c + P], aux_lo[:, c:c + P],
                                                 w_hi[:, slot, a:a + W], w_lo[:, slot, a:a + W], first and k == 0,
                                                 final and k == ph.kt - 1)
                            if ph.variant == "A" and final and t == 0:
                                last.then_inc(sem["tile_done"], 1)
                        last.then_inc(sem["piece_used"], 1)

                for i, steps in ffn_schedule(ph, pe):
                    hidden(i, steps)
                    if steps[0] > 0:
                        down(i, steps, steps[0] == 1, False)
                down(None, [ph.n], False, True)

            pe.wait_ge(sem["const_landed"], 16)
            turn_vectors((0,), "vec_landed", 16 * 6)
            todo = {"norm": norm, "gemm": gemm, "mixA": mix_A, "nsa": mix_nsa, "sb": mix_sb, "conv": mix_conv,
                    "moba": mix_moba, "ffn": ffn}
            for ph in phases:
                if ph.kind in todo:
                    todo[ph.kind](ph)
                n.advance(ph)


def kernel(**inputs):
    import concourse.bacc as bacc
    from concourse.bass_utils import run_bass_kernel_spmd

    tables = [packed(t) for t in constant_tables()]
    nc = bacc.Bacc("TRN2", target_bir_lowering=False, num_devices=1, dynamic_dma_scratch_size=1024)
    arrays, A = {}, {}
    given = {name: np.ascontiguousarray(a) for name, a in inputs.items()}
    given.update(zip(("both", "first", "second"), (t[0] for t in tables)))
    for name, a in given.items():
        arrays["in_" + name] = a
        A[name] = nc.dram_tensor("in_" + name, list(a.shape), mybir.dt.from_np(a.dtype), kind="ExternalInput").ap()
    out = nc.dram_tensor("out", [1, S, D], F32, kind="ExternalOutput").ap()
    first_second_block(nc, A, out, *(t[1] for t in tables))
    r = run_bass_kernel_spmd(nc, [arrays], core_ids=[0])
    return r.results[0]["out"]
```
